# Optimizing a Trainium2 kernel written in Bass

```python
import math, functools
import jax, jax.numpy as jnp
from jax import lax
import numpy as np

D_MODEL = 1024
BATCH = 1
SEQ = 128
DEPTH = 2
DEC_BATCH = 1
DEC_SEQ = 512
PAST_LEN = 256

GRID_W = 64
MIX_WIDTH = D_MODEL
ATT_WIDTH = MIX_WIDTH // 2
CONV_WIDTH = MIX_WIDTH - ATT_WIDTH
N_ATT_HEADS = 4
V_HEAD_DIM = ATT_WIDTH // N_ATT_HEADS
QK_HEAD_DIM = V_HEAD_DIM // 2
N_CONV_GROUPS = 8
CONV_K = 3
ROPE_BASE = 10000.0
D_FF = 2816
N_EXPERTS = 8
TOP_K = 2
D_FF_EXPERT = 1408
N_DENSE = (DEPTH + 1) // 2
N_MOE = DEPTH // 2
N_MOD = 6
Q_BLOCK = 128
NORM_EPS = 1e-6
IN_COLS = 3 * ATT_WIDTH + 3 * CONV_WIDTH

kernel_name = 'hybrid_diffattn_shortconv_prefix_dit_step'

def rms_norm(x, g):
    xf = x.astype(jnp.float32)
    y = xf * lax.rsqrt(jnp.mean(xf * xf, axis=-1, keepdims=True) + NORM_EPS)
    return (y * g.astype(jnp.float32)).astype(x.dtype)

def modulation(cond, w_ada, b_ada):
    m = jax.nn.silu(cond) @ w_ada + b_ada
    return jnp.split(m[:, None, :], N_MOD, axis=-1)

def axial_rope(x):
    L = x.shape[1]
    rows = L // GRID_W
    row = jnp.repeat(jnp.arange(rows), GRID_W)
    col = jnp.tile(jnp.arange(GRID_W), rows)
    ax = QK_HEAD_DIM // 2
    half = ax // 2
    freqs = ROPE_BASE ** (-jnp.arange(half, dtype=jnp.float32) / half)

    def rotate(xa, pos):
        ang = pos.astype(jnp.float32)[:, None] * freqs[None, :]
        cos = jnp.cos(ang)[None, :, None, None, :]
        sin = jnp.sin(ang)[None, :, None, None, :]
        x1 = xa[..., :half].astype(jnp.float32)
        x2 = xa[..., half:].astype(jnp.float32)
        return jnp.concatenate([x1 * cos - x2 * sin, x1 * sin + x2 * cos], axis=-1)

    out = jnp.concatenate([rotate(x[..., :ax], row), rotate(x[..., ax:], col)], axis=-1)
    return out.astype(x.dtype)

def diff_attention(q, k, v, lambda_qk, subln_g, lam_init):
    B, Lq = q.shape[0], q.shape[1]
    qb = min(Q_BLOCK, Lq)
    nblk = Lq // qb
    lq = lambda_qk.astype(jnp.float32)
    lam = jnp.exp(jnp.sum(lq[0] * lq[1])) - jnp.exp(jnp.sum(lq[2] * lq[3])) + lam_init
    scale = QK_HEAD_DIM ** -0.5
    q_blocks = jnp.moveaxis(q.reshape(B, nblk, qb, N_ATT_HEADS, 2, QK_HEAD_DIM), 1, 0)

    def one_block(qblk):
        s = jnp.einsum('bqhsd,bkhsd->bshqk', qblk, k).astype(jnp.float32) * scale
        p = jax.nn.softmax(s, axis=-1)
        a = p[:, 0] - lam * p[:, 1]
        return jnp.einsum('bhqk,bkhe->bqhe', a.astype(v.dtype), v)

    o = lax.map(one_block, q_blocks)
    o = jnp.moveaxis(o, 0, 1).reshape(B, Lq, N_ATT_HEADS, V_HEAD_DIM).astype(jnp.float32)
    o = o * lax.rsqrt(jnp.mean(o * o, axis=-1, keepdims=True) + NORM_EPS)
    o = o * subln_g.astype(jnp.float32) * (1.0 - lam_init)
    return o.reshape(B, Lq, ATT_WIDTH).astype(v.dtype)

def short_conv(u, w):
    up = jnp.pad(u, ((0, 0), (1, 1), (0, 0)))
    return up[:, :-2] * w[0] + up[:, 1:-1] * w[1] + up[:, 2:] * w[2]

def mixer(h, w_in, lambda_qk, subln_g, conv_w, w_out, lam_init, k_ctx, v_ctx):
    B, L, _ = h.shape
    proj = h @ w_in
    q, k, v, gb, gc, xin = jnp.split(
        proj,
        [ATT_WIDTH, 2 * ATT_WIDTH, 3 * ATT_WIDTH, 3 * ATT_WIDTH + CONV_WIDTH, 3 * ATT_WIDTH + 2 * CONV_WIDTH],
        axis=-1)
    q = q.reshape(B, L, N_ATT_HEADS, 2, QK_HEAD_DIM)
    k = k.reshape(B, L, N_ATT_HEADS, 2, QK_HEAD_DIM)
    v = v.reshape(B, L, N_ATT_HEADS, V_HEAD_DIM)
    if k_ctx is None:
        keys, vals = k, v
    else:
        q = axial_rope(q)
        keys = jnp.concatenate([k_ctx, axial_rope(k)], axis=1)
        vals = jnp.concatenate([v_ctx, v], axis=1)
    att = diff_attention(q, keys, vals, lambda_qk, subln_g, lam_init)
    conv = gb * short_conv(gc * xin, conv_w)
    out = jnp.concatenate([att, conv], axis=-1) @ w_out
    return out, k, v

def swiglu(h, w_gu, w_down):
    g, u = jnp.split(h @ w_gu, 2, axis=-1)
    return (jax.nn.silu(g) * u) @ w_down

def moe_swiglu(h, w_router, w_gu, w_down):
    B, L, D = h.shape
    t = h.reshape(B * L, D)
    logits = (t @ w_router).astype(jnp.float32)
    top_v, top_i = lax.top_k(logits, TOP_K)
    top_w = jax.nn.softmax(top_v, axis=-1)
    gates = jnp.einsum('nk,nke->ne', top_w, jax.nn.one_hot(top_i, N_EXPERTS, dtype=jnp.float32)).astype(h.dtype)
    gu = jnp.einsum('nd,edf->enf', t, w_gu)
    g, u = jnp.split(gu, 2, axis=-1)
    eo = jnp.einsum('enf,efd->end', jax.nn.silu(g) * u, w_down)
    y = jnp.einsum('ne,end->nd', gates, eo)
    return y.reshape(B, L, D)

def trunk_layer(x, cond, k_ctx, v_ctx, lam_init, w_ada_l, b_ada_l, g_mix, g_ffn,
                w_in_l, lambda_l, subln_l, conv_l, w_out_l, ffn):
    shift1, scale1, gate1, shift2, scale2, gate2 = modulation(cond, w_ada_l, b_ada_l)
    h = rms_norm(x, g_mix) * (1 + scale1) + shift1
    mo, k, v = mixer(h, w_in_l, lambda_l, subln_l, conv_l, w_out_l, lam_init, k_ctx, v_ctx)
    x = x + gate1 * mo
    h = rms_norm(x, g_ffn) * (1 + scale2) + shift2
    x = x + gate2 * ffn(h)
    return x, k, v

def setup_inputs(seed: int = 0) -> dict:
    key = jax.random.key(seed)
    ks = jax.random.split(key, 21)
    f32 = jnp.float32

    def nrm(k, shape, s):
        return jax.random.normal(k, shape, f32) * s

    return {
        'x_prompt': nrm(ks[0], (BATCH, SEQ, D_MODEL), 1.0),
        'x_sample': nrm(ks[1], (DEC_BATCH, DEC_SEQ, D_MODEL), 1.0),
        'cache_k': nrm(ks[2], (DEC_BATCH, DEPTH, PAST_LEN, N_ATT_HEADS, 2, QK_HEAD_DIM), 1.0),
        'cache_v': nrm(ks[3], (DEC_BATCH, DEPTH, PAST_LEN, N_ATT_HEADS, V_HEAD_DIM), 1.0),
        'c': nrm(ks[4], (DEC_BATCH, D_MODEL), 1.0),
        'c_ctx': nrm(ks[5], (D_MODEL,), 1.0),
        'w_ada': nrm(ks[6], (DEPTH, D_MODEL, N_MOD * D_MODEL), 0.5 * D_MODEL ** -0.5),
        'b_ada': nrm(ks[7], (DEPTH, N_MOD * D_MODEL), 0.01),
        'norm_mix_g': 1.0 + nrm(ks[8], (DEPTH, D_MODEL), 0.02),
        'norm_ffn_g': 1.0 + nrm(ks[9], (DEPTH, D_MODEL), 0.02),
        'w_in': nrm(ks[10], (DEPTH, D_MODEL, IN_COLS), D_MODEL ** -0.5),
        'lambda_qk': nrm(ks[11], (DEPTH, 4, QK_HEAD_DIM), 0.1),
        'subln_g': 1.0 + nrm(ks[12], (DEPTH, V_HEAD_DIM), 0.02),
        'conv_w': nrm(ks[13], (DEPTH, CONV_K, CONV_WIDTH), CONV_K ** -0.5),
        'w_out': nrm(ks[14], (DEPTH, MIX_WIDTH, D_MODEL), MIX_WIDTH ** -0.5),
        'w_gu_dense': nrm(ks[15], (N_DENSE, D_MODEL, 2 * D_FF), D_MODEL ** -0.5),
        'w_down_dense': nrm(ks[16], (N_DENSE, D_FF, D_MODEL), D_FF ** -0.5),
        'w_router': nrm(ks[17], (N_MOE, D_MODEL, N_EXPERTS), D_MODEL ** -0.5),
        'w_gu_moe': nrm(ks[18], (N_MOE, N_EXPERTS, D_MODEL, 2 * D_FF_EXPERT), D_MODEL ** -0.5),
        'w_down_moe': nrm(ks[19], (N_MOE, N_EXPERTS, D_FF_EXPERT, D_MODEL), D_FF_EXPERT ** -0.5),
        'final_g': 1.0 + nrm(ks[20], (D_MODEL,), 0.02),
    }

def reference(x_prompt, x_sample, cache_k, cache_v, c, c_ctx, w_ada, b_ada, norm_mix_g, norm_ffn_g,
              w_in, lambda_qk, subln_g, conv_w, w_out, w_gu_dense, w_down_dense, w_router,
              w_gu_moe, w_down_moe, final_g):
    def layer_ffn(layer):
        if layer % 2 == 0:
            i = layer // 2
            return functools.partial(swiglu, w_gu=w_gu_dense[i], w_down=w_down_dense[i])
        i = layer // 2
        return functools.partial(moe_swiglu, w_router=w_router[i], w_gu=w_gu_moe[i], w_down=w_down_moe[i])

    ctx_cond = c_ctx[None, :]
    xp = x_prompt
    ks, vs = [], []
    for layer in range(DEPTH):
        lam_init = 0.8 - 0.6 * math.exp(-0.3 * layer)
        xp, k, v = trunk_layer(xp, ctx_cond, None, None, lam_init, w_ada[layer], b_ada[layer],
                               norm_mix_g[layer], norm_ffn_g[layer], w_in[layer], lambda_qk[layer],
                               subln_g[layer], conv_w[layer], w_out[layer], layer_ffn(layer))
        ks.append(k)
        vs.append(v)

    xs = x_sample
    for layer in range(DEPTH):
        lam_init = 0.8 - 0.6 * math.exp(-0.3 * layer)
        xs, _, _ = trunk_layer(xs, c, cache_k[:, layer], cache_v[:, layer], lam_init, w_ada[layer],
                               b_ada[layer], norm_mix_g[layer], norm_ffn_g[layer], w_in[layer],
                               lambda_qk[layer], subln_g[layer], conv_w[layer], w_out[layer],
                               layer_ffn(layer))

    y_prompt = rms_norm(xp, final_g)
    y_sample = rms_norm(xs, final_g)
    new_k = jnp.stack(ks, axis=1)
    new_v = jnp.stack(vs, axis=1)
    return (y_prompt, y_sample, new_k, new_v)


_drawn_inputs = setup_inputs


def setup_inputs(seed=0):
    import zlib

    import numpy as np

    out = dict(_drawn_inputs(seed))
    spreads = {}
    factors = {'norm_mix_g': 2.804,
     'norm_ffn_g': 3.576,
     'subln_g': 24.885,
     'final_g': 8.812,
     'cache_k': 8.0,
     'cache_v': 8.0}
    for name, (base, spread) in spreads.items():
        noise = np.random.default_rng([zlib.crc32(name.encode()), seed]).standard_normal(out[name].shape)
        drawn = base * np.exp(spread * noise) if base else spread * noise
        out[name] = __import__('jax').numpy.asarray(drawn.astype(out[name].dtype))
    for name, factor in factors.items():
        out[name] = (out[name] * factor).astype(out[name].dtype)
    return out
```

```python
from contextlib import ExitStack

import concourse.bass as bass
from concourse import mybir

P = 128
D = 1024
KB = D // P
CTX, LAT, PAST = 128, 512, 256
T = CTX + LAT
HALF = T // 2
TT = T // P
NKEY = LAT + PAST
KCOLS = T + PAST
KT = KCOLS // P
LAYERS = 2
HEADS, QK, VH = 4, 64, 128
ATT_BLOCKS = 4
CONV_BLOCKS = 4
EXPERTS = 8
FF = 1408
FB = FF // P
EPS = 1e-6
CHUNK = 8 * P
RAW, SPLIT = 6, 3
ADA_CH, IN_CH, OUT_CH, UNIT_CH = 48, 24, 8, 33
LAM_INIT = [0.8 - 0.6 * 2.718281828459045 ** (-0.3 * l) for l in range(LAYERS)]
SWAP = [(i + 16) % 32 for i in range(32)]

F32 = mybir.dt.float32
F32R = mybir.dt.float32r
U32 = mybir.dt.uint32
ALU = mybir.AluOpType
ACT = mybir.ActivationFunctionType
AX = mybir.AxisListType.X
SEGMENTS = [(0, slice(0, CTX), slice(0, CTX), 0), (0, slice(CTX, HALF), slice(CTX, HALF), 1),
            (1, slice(0, HALF), slice(HALF, T), 1)]
TOKENS_OF = [(slice(0, CTX), 0), (slice(CTX, T), 1)]


def unit_groups(out_major):
    groups = []
    for c in range(2 * FB):
        groups.append((c, c, True, True, [(i, i) for i in range(KB)]))
    pieces = [(d, k) for d in range(KB) for k in range(FB)]
    for c in range(FB):
        part = [(i, *pieces[8 * c + i]) for i in range(8)]
        for d in sorted({p[1] for p in part}):
            mine = [(i, k) for i, dd, k in part if dd == d]
            groups.append((2 * FB + c, 2 * FB + d, mine[0][0] == 0, mine[-1][1] == FB - 1, mine))
    return groups


UNIT = unit_groups(True)
UNIT_BLOCKS = 2 * FB + KB
SIMPLE = [(0, 0, True, True, [(i, i) for i in range(KB)])]


def plan():
    at, n, q, g = {}, 0, 0, 0
    for l in range(LAYERS):
        steps = [("ada", ADA_CH, ADA_CH, 1), ("norm1", 0, 1, 1), ("in", IN_CH, IN_CH, IN_CH), ("vtok", 0, 4, 4),
                 ("sub", 0, 4, 4), ("out", OUT_CH, OUT_CH, OUT_CH), ("norm2", 0, 1, 1)]
        if l % 2 == 0:
            steps += [("ffn", 2 * UNIT_CH, 2 * len(UNIT), 2 * UNIT_BLOCKS)]
        else:
            steps += [("route", 0, 1 + EXPERTS, 1 + EXPERTS),
                      ("ffn", EXPERTS * UNIT_CH, EXPERTS * len(UNIT), EXPERTS * UNIT_BLOCKS)]
        for name, dn, dq, dg in steps:
            at[l, name] = (n, q, g)
            n, q, g = n + dn, q + dq, g + dg
    at["final"] = (n, q, g)
    return at


AT = plan()
NORM_AT = [AT[0, "norm1"], AT[0, "norm2"], AT[1, "norm1"], AT[1, "norm2"], AT["final"]]
IN_ORDER = [("k", j) for j in range(4)] + [("q", j) for j in range(4)] + [("v", j) for j in range(4)] \
    + [("gc", j) for j in range(4)] + [("xin", j) for j in range(4)] + [("gb", j) for j in range(4)]
STEPS = [(h, t, 0, CTX) if t == 0 else (h, t, CTX, NKEY) for h in range(HEADS) for t in range(TT)]
NS = len(STEPS)


def hybrid_step(nc, xT, condT, ada_w, in_w, out_w, gu_w, down_w, router_w, b_ada, g_mix, g_ffn, g_fin, lam_qk,
                subln, conv_w, kcT, vc, cos, sin, ident, iota8, y, newk, newv):
    with ExitStack() as ctx:
        def sb(name, shape, dt=F32, c=ctx):
            return c.enter_context(nc.sbuf_tensor(name, shape, dt))

        def sem(name):
            return ctx.enter_context(nc.semaphore(name))

        x = sb("x", [P, KB, T])
        a_hi = sb("a_hi", [P, KB, T], F32R)
        a_lo = sb("a_lo", [P, KB, T], F32R)
        raw = sb("raw", [P, RAW, CHUNK])
        w_hi = sb("w_hi", [P, SPLIT, CHUNK], F32R)
        w_lo = sb("w_lo", [P, SPLIT, CHUNK], F32R)
        st = sb("st", [P, 2, T])
        tt = sb("tt", [P, 2, T])
        sq = sb("sq", [P, 2, T])
        ss = sb("ss", [P, T])
        rstd = sb("rstd", [P, T])
        eps = sb("eps", [P, 1])
        cos_s = sb("cos_s", [P, LAT])
        sin_s = sb("sin_s", [P, LAT])
        ones = sb("ones", [P, P])
        idn = sb("idn", [P, P])
        cond = sb("cond", [P, KB, 2])
        cs = sb("cs", [P, KB, 2])
        cs4 = sb("cs4", [P, KB, 4], F32R)
        bada = sb("bada", [P, LAYERS, 6 * KB])
        mod = sb("mod", [P, 6 * KB, 2])
        gain = sb("gain", [P, 2, KB, 2])
        gmix = sb("gmix", [P, LAYERS, KB])
        gffn = sb("gffn", [P, LAYERS, KB])
        gfin = sb("gfin", [P, KB])
        lq = sb("lq", [P, LAYERS, 4 * QK])
        lp = sb("lp", [P, 2 * QK])
        lsum = sb("lsum", [P, 2])
        lexp = sb("lexp", [P, 2])
        nlam = sb("nlam", [P, 1])
        subg = sb("subg", [P, LAYERS])
        subgs = sb("subgs", [P, LAYERS])
        convw = sb("convw", [P, LAYERS, 3, CONV_BLOCKS])
        nmax = sb("nmax", [P, 2, 2])
        nbias = sb("nbias", [P, 2, 2])
        rsum = sb("rsum", [P, 2, 2])
        rinv = sb("rinv", [P, 2, 2])
        rneg = sb("rneg", [P, 2, 1])
        wr = sb("wr", [P, KB, EXPERTS])
        wr2 = sb("wr2", [P, KB, 2 * EXPERTS], F32R)
        iot = sb("iot", [P, EXPERTS])
        logits = sb("logits", [P, TT, EXPERTS])
        tv = sb("tv", [P, TT, 8])
        ti = sb("ti", [P, TT, 8], U32)
        tf = sb("tf", [P, TT, 8])
        dv = sb("dv", [P, TT])
        ev = sb("ev", [P, TT])
        g1 = sb("g1", [P, TT])
        g2 = sb("g2", [P, TT])
        gates = sb("gates", [P, TT, EXPERTS])
        oh = sb("oh", [P, 2, EXPERTS])

        with ExitStack() as mix:
            kT = sb("kT", [P, HEADS, KCOLS], c=mix)
            qT = sb("qT", [P, HEADS, T], c=mix)
            vtok = sb("vtok", [P, KT, HEADS * VH], c=mix)
            att = sb("att", [P, HEADS, T], c=mix)
            gcx = sb("gcx", [P, CONV_BLOCKS, T], c=mix)
            cv = sb("cv", [P, T], c=mix)
            swp = sb("swp", [P, LAT], c=mix)
            pT = sb("pT", [P, 2, NKEY], c=mix)
            with ExitStack() as vs:
                vT = sb("vT", [P, HEADS, T], c=vs)
            pr = sb("pr", [P, 2, 2, NKEY], c=mix)
        with ExitStack() as ffn:
            act_hi = sb("act_hi", [P, FB, T], F32R, c=ffn)
            act_lo = sb("act_lo", [P, FB, T], F32R, c=ffn)
            gbc = sb("gbc", [P, EXPERTS, T], c=ffn)
            gex = sb("gex", [P, TT, P], c=ffn)

        ps = ctx.enter_context(nc.psum_tensor("ps", [P, 4, 2, 512], F32))
        S = ps[:, 0:2].rearrange("p a b c -> p a (b c)")
        PT = ps[:, 2].rearrange("p b c -> p (b c)")
        OT = ps[:, 3, 0, 0:P]

        raw_full = [sem(f"raw_full{i}") for i in range(RAW)]
        hi_done = sem("hi_done")
        lo_done = sem("lo_done")
        mm_done = sem("mm_done")
        blk_free = sem("blk_free")
        consts_in = sem("consts_in")
        x_in = sem("x_in")
        cache_in = [sem(f"cache_in{l}") for l in range(LAYERS)]
        ones_set = sem("ones_set")
        dve_step = sem("dve_step")
        silu_c = sem("silu_c")
        cs_hi = sem("cs_hi")
        cs_ready = sem("cs_ready")
        mod_ready = sem("mod_ready")
        x_new = sem("x_new")
        sq_done = sem("sq_done")
        ss_add = sem("ss_add")
        root_done = sem("root_done")
        rstd_done = sem("rstd_done")
        xn_done = sem("xn_done")
        h_done = sem("h_done")
        ahi_done = sem("ahi_done")
        alo_done = sem("alo_done")
        kq_raw = sem("kq_raw")
        kq_ready = sem("kq_ready")
        vt_ready = sem("vt_ready")
        gcx_ready = sem("gcx_ready")
        conv_ready = sem("conv_ready")
        vtok_ready = sem("vtok_ready")
        lam_sum = sem("lam_sum")
        lam_exp = sem("lam_exp")
        lam_ready = sem("lam_ready")
        scores_done = sem("scores_done")
        max_done = sem("max_done")
        exp_done = sem("exp_done")
        comb_done = sem("comb_done")
        tr_done = sem("tr_done")
        pt_ready = sem("pt_ready")
        pv_done = sem("pv_done")
        att_ready = sem("att_ready")
        att_sq = sem("att_sq")
        att_root = sem("att_root")
        att_norm = sem("att_norm")
        silu_done = sem("silu_done")
        t_raw = sem("t_raw")
        t_done = sem("t_done")
        wr_hi = sem("wr_hi")
        wr_ready = sem("wr_ready")
        dv_ready = sem("dv_ready")
        ev_ready = sem("ev_ready")
        gex_ready = sem("gex_ready")
        yblk = sem("yblk")
        out_done = sem("out_done")
        k_out = sem("k_out")
        v_out = sem("v_out")
        FC0 = 2 * FB

        block = ctx.enter_context(nc.Block())

        H0 = {(0, 1): 0, (0, 2): 2 * KB + 0, (1, 1): 0, (1, 2): 0}
        count = 0
        operand = {}
        for l in range(LAYERS):
            for what, k in (("h1", KB), ("cat", KB), ("h2", KB), ("act", (2 if l % 2 == 0 else EXPERTS) * FB)):
                operand[l, what] = count
                count += k

        @block.sync
        def _(sp):
            def load(n, src, it=0, per=0):
                if n >= RAW:
                    sp.wait_ge(lo_done, n - RAW + 1 + per * it)
                sp.dma_start(raw[:, n % RAW, :], src).then_inc(raw_full[n % RAW], 16)

            sp.dma_start(cond[:], condT).then_inc(consts_in, 16)
            small = [(bada, b_ada), (gmix, g_mix), (gffn, g_ffn), (gfin, g_fin), (subg, subln), (convw, conv_w),
                     (cos_s, cos), (sin_s, sin), (idn, ident), (wr, router_w), (iot, iota8),
                     (lq, lam_qk.partition_broadcast(P))]
            n = 0
            for c in range(4):
                load(n, ada_w[0, c])
                n += 1
            for dst, src in small:
                sp.dma_start(dst[:], src).then_inc(consts_in, 16)
            sp.dma_start(x[:], xT).then_inc(x_in, 16)
            for l in range(LAYERS):
                for c in range(4 if l == 0 else 0, ADA_CH):
                    load(n, ada_w[l, c])
                    n += 1
                if l:
                    sp.wait_ge(pv_done, l * NS)
                    sp.wait_ge(mm_done, AT[l, "ada"][1])
                sp.dma_start(kT[:, :, T:KCOLS], kcT[l]).then_inc(cache_in[l], 16)
                sp.dma_start(vtok[:, TT:KT, :], vc[l]).then_inc(cache_in[l], 16)
                for c in range(IN_CH):
                    load(n, in_w[l, c])
                    n += 1
                for c in range(OUT_CH):
                    load(n, out_w[l, c])
                    n += 1
                sp.wait_ge(kq_raw, 8 * l + 4)
                sp.dma_start(newk[l], kT[:, :, 0:CTX]).then_inc(k_out, 16)
                sp.wait_ge(vt_ready, 4 * (l + 1))
                sp.dma_start(newv[l], vT[:, :, 0:CTX]).then_inc(v_out, 16)
                if l % 2 == 0:
                    for u in range(2):
                        for c in range(2 * FB):
                            load(n, gu_w[u, c])
                            n += 1
                        for c in range(FB):
                            load(n, down_w[u, c])
                            n += 1
                else:
                    with sp.Fori(0, EXPERTS // 2) as it:
                        for u in range(2):
                            for c in range(UNIT_CH):
                                src = gu_w[2 + 2 * it + u, c] if c < 2 * FB else down_w[2 + 2 * it + u, c - 2 * FB]
                                load(n + u * UNIT_CH + c, src, it, 2 * UNIT_CH)
                    n += EXPERTS * UNIT_CH
            for c in range(2):
                load(n, gu_w[0, c])
                n += 1
            for kb in range(KB):
                sp.wait_ge(yblk, kb + 1)
                sp.dma_start(y[:, kb], st[:, kb % 2, :] if kb < 0 else x[:, kb, :]).then_inc(out_done, 16)
            sp.wait_ge(out_done, 16 * KB)
            sp.wait_ge(k_out, 16 * LAYERS)
            sp.wait_ge(v_out, 16 * LAYERS)

        @block.tensor
        def _(pe):
            def open_block(g, it=0, per=0):
                if g >= 4:
                    pe.wait_ge(blk_free, g - 3 + per * it)

            def product(out, wsl, opnd_hi, opnd_lo, first, last):
                s, i = wsl
                whi = w_hi[:, s, i * P:(i + 1) * P]
                wlo = w_lo[:, s, i * P:(i + 1) * P]
                for w, o, f, e in ((whi, opnd_hi, first, False), (whi, opnd_lo, False, False),
                                   (wlo, opnd_hi, False, last)):
                    for hf in range(2):
                        ins = nc.tensor.matmul(out[:, hf, 0:HALF], w, o[:, hf * HALF:(hf + 1) * HALF],
                                               start=f, stop=e)
                return ins

            def project(l, name, chunks, opnd):
                n0, q0, g0 = AT[l, name]
                order = list(range(KB)) if name == "in" else [4, 5, 6, 7, 0, 1, 2, 3]
                for c in range(chunks):
                    pe.wait_ge(lo_done, n0 + c + 1)
                    open_block(g0 + c)
                    for j, k in enumerate(order):
                        if c == 0:
                            pe.wait_ge(alo_done, opnd + j + 1)
                        ins = product(ps[:, (g0 + c) % 4], ((n0 + c) % SPLIT, k), a_hi[:, k, :], a_lo[:, k, :],
                                      j == 0, j == KB - 1)
                    ins.then_inc(mm_done, 1)

            def norm_sums(i):
                n0, q0, g0 = NORM_AT[i]
                open_block(g0)
                pe.wait_ge(ss_add, KB * (i + 1))
                for hf in range(2):
                    ins = nc.tensor.matmul(ps[:, g0 % 4, hf, 0:HALF], ones[:], ss[:, hf * HALF:(hf + 1) * HALF],
                                           start=True, stop=True)
                ins.then_inc(mm_done, 1)

            def unit(n0, q0, g0, opnd, l, it=0, first_unit=False):
                per = 2 * UNIT_CH
                perg = 2 * UNIT_BLOCKS
                for c, b, new_chunk, end, pieces in UNIT:
                    if new_chunk:
                        pe.wait_ge(lo_done, n0 + c + 1 + per * it)
                    if pieces[0][1] == 0:
                        open_block(g0 + b, it, perg)
                    down = c >= 2 * FB
                    for i, k in pieces:
                        if down and b == 2 * FB:
                            pe.wait_ge(alo_done, opnd + k + 1 + 2 * FB * it)
                        if not down and c == 0 and first_unit:
                            pe.wait_ge(alo_done, operand[l, "h2"] + k + 1)
                        hi, lo = (act_hi, act_lo) if down else (a_hi, a_lo)
                        ins = product(ps[:, (g0 + b) % 4], ((n0 + c) % SPLIT, i), hi[:, k, :], lo[:, k, :],
                                      k == 0, k == (FB if down else KB) - 1)
                    ins.then_inc(mm_done, 1)

            pe.wait_ge(ones_set, 1)
            for l in range(LAYERS):
                n0, q0, g0 = AT[l, "ada"]
                open_block(g0)
                if l == 0:
                    pe.wait_ge(cs_ready, 1)
                for c in range(ADA_CH):
                    pe.wait_ge(lo_done, n0 + c + 1)
                    for k in range(KB):
                        for w in (w_hi, w_lo):
                            ins = nc.tensor.matmul(ps[:, g0 % 4, 0, 4 * c:4 * c + 4],
                                                   w[:, (n0 + c) % SPLIT, k * P:(k + 1) * P], cs4[:, k, :],
                                                   start=(k == 0 and w is w_hi), stop=(k == KB - 1 and w is w_lo))
                    ins.then_inc(mm_done, 1)
                norm_sums(2 * l)
                project(l, "in", IN_CH, operand[l, "h1"])

                n0, q0, g0 = AT[l, "vtok"]
                pe.wait_ge(vt_ready, 4 * (l + 1))
                pe.wait_ge(consts_in, 16 * 13)
                for h in range(HEADS):
                    open_block(g0 + h)
                    for t in range(TT):
                        ins = nc.tensor.transpose(ps[:, (g0 + h) % 4, t // 4, (t % 4) * P:(t % 4 + 1) * P],
                                                  vT[:, h, t * P:(t + 1) * P], idn[:])
                    ins.then_inc(mm_done, 1)

                pe.wait_ge(blk_free, g0 + HEADS)
                pe.wait_ge(kq_ready, 8 * (l + 1))
                pe.wait_ge(cache_in[l], 32)
                pe.wait_ge(vtok_ready, 4 * (l + 1))

                def scores(i):
                    h, t, k0, nk = STEPS[i]
                    if i > 0:
                        pe.wait_ge(exp_done, 2 * (l * NS + i))
                    for s in range(2):
                        for c0 in range(0, nk, 512):
                            c1 = min(nk, c0 + 512)
                            ins = nc.tensor.matmul(S[:, s, c0:c1], qT[QK * s:QK * (s + 1), h, t * P:(t + 1) * P],
                                                   kT[QK * s:QK * (s + 1), h, k0 + c0:k0 + c1],
                                                   start=True, stop=True)
                    ins.then_inc(scores_done, 1)

                scores(0)
                for i, (h, t, k0, nk) in enumerate(STEPS):
                    if i + 1 < NS:
                        scores(i + 1)
                    pe.wait_ge(comb_done, l * NS + i + 1)
                    if i > 0:
                        pe.wait_ge(pt_ready, l * NS + i)
                    for j in range(nk // P):
                        ins = nc.tensor.transpose(PT[:, j * P:(j + 1) * P], pr[:, i % 2, 0, j * P:(j + 1) * P], idn[:])
                    ins.then_inc(tr_done, 1)
                    pe.wait_ge(pt_ready, l * NS + i + 1)
                    if i > 0:
                        pe.wait_ge(att_ready, l * NS + i)
                    for j in range(nk // P):
                        ins = nc.tensor.matmul(OT, vtok[:, k0 // P + j, h * VH:(h + 1) * VH],
                                               pT[:, i % 2, j * P:(j + 1) * P], start=(j == 0), stop=(j == nk // P - 1))
                    ins.then_inc(pv_done, 1)

                n0, q0, g0 = AT[l, "sub"]
                pe.wait_ge(att_ready, (l + 1) * NS)
                pe.wait_ge(pt_ready, (l + 1) * NS)
                pe.wait_ge(exp_done, 2 * (l + 1) * NS)
                for h in range(HEADS):
                    pe.wait_ge(att_sq, HEADS * l + h + 1)
                    for hf in range(2):
                        ins = nc.tensor.matmul(ps[:, (g0 + h) % 4, hf, 0:HALF], ones[:],
                                               sq[:, h % 2, hf * HALF:(hf + 1) * HALF], start=True, stop=True)
                    ins.then_inc(mm_done, 1)

                project(l, "out", OUT_CH, operand[l, "cat"])
                norm_sums(2 * l + 1)
                n0, q0, g0 = AT[l, "ffn"]
                if l % 2 == 0:
                    for u in range(2):
                        unit(n0 + u * UNIT_CH, q0 + u * len(UNIT), g0 + u * UNIT_BLOCKS,
                             operand[l, "act"] + u * FB, l, first_unit=(u == 0))
                else:
                    rn, rq, rg = AT[l, "route"]
                    open_block(rg)
                    pe.wait_ge(wr_ready, 1)
                    for t in range(TT):
                        for k in range(KB):
                            pe.wait_ge(alo_done, operand[l, "h2"] + k + 1)
                            for a in (a_hi, a_lo):
                                ins = nc.tensor.matmul(ps[:, rg % 4, 0, 16 * t:16 * t + 16],
                                                       a[:, k, t * P:(t + 1) * P], wr2[:, k, :],
                                                       start=(k == 0 and a is a_hi), stop=(k == KB - 1 and a is a_lo))
                    ins.then_inc(mm_done, 1)
                    for e in range(EXPERTS):
                        pe.wait_ge(gex_ready, e + 1)
                        open_block(rg + 1 + e)
                        for t in range(TT):
                            ins = nc.tensor.matmul(ps[:, (rg + 1 + e) % 4, t // 4, (t % 4) * P:(t % 4 + 1) * P],
                                                   gex[:, t, :], idn[:], start=True, stop=True)
                        ins.then_inc(mm_done, 1)
                    with pe.Fori(0, EXPERTS // 2) as it:
                        for u in range(2):
                            unit(n0 + u * UNIT_CH, q0 + u * len(UNIT), g0 + u * UNIT_BLOCKS,
                                 operand[l, "act"] + u * FB, l, it)
            norm_sums(4)

        @block.scalar
        def _(act):
            def split_hi(n, q, it=0, pern=0, perq=0):
                s = n % SPLIT
                act.wait_ge(raw_full[n % RAW], 16 * (n // RAW + 1) + 16 * (pern // RAW) * it)
                if q > 0:
                    act.wait_ge(mm_done, q + perq * it)
                nc.scalar.activation(w_hi[:, s, :], raw[:, n % RAW, :], ACT.Copy).then_inc(hi_done, 1)

            def square(i, kb, dst_sem=sq_done):
                m = KB * i + kb
                if i == 0:
                    act.wait_ge(x_in, 16)
                else:
                    act.wait_ge(x_new, KB * (i - 1) + kb + 1)
                if m >= 2:
                    act.wait_ge(ss_add, m - 1)
                nc.scalar.activation(sq[:, m % 2, :], x[:, kb, :], ACT.Square).then_inc(dst_sem, 1)

            def root(i, width):
                n0, q0, g0 = NORM_AT[i]
                act.wait_ge(mm_done, q0 + 1)
                nc.scalar.activation(rstd[:].rearrange("p (a b) -> p a b", a=2), ps[:, g0 % 4, :, 0:HALF], ACT.Sqrt,
                                     bias=eps[:, 0:1], scale=1.0 / width).then_inc(root_done, 1)

            def modulate(i, opnd):
                l, which = i // 2, i % 2
                if which == 0:
                    act.wait_ge(mod_ready, l + 1)
                for kb in range(KB):
                    act.wait_ge(xn_done, KB * i + kb + 1)
                    if kb >= 2:
                        act.wait_ge(alo_done, opnd + kb - 1)
                    for toks, c in TOKENS_OF:
                        ins = nc.scalar.activation(tt[:, kb % 2, toks], st[:, kb % 2, toks], ACT.Identity,
                                                   bias=mod[:, (3 * which) * KB + kb, c:c + 1],
                                                   scale=gain[:, which, kb, c:c + 1])
                    ins.then_inc(h_done, 1)
                    act.wait_ge(h_done, KB * i + kb + 1)
                    nc.scalar.activation(a_hi[:, kb, :], tt[:, kb % 2, :], ACT.Copy).then_inc(ahi_done, 1)

            def unit(n0, q0, g0, opnd, f0, it=0):
                pern, perq = 2 * UNIT_CH, 2 * len(UNIT)
                for j, (c, b, new_chunk, end, pieces) in enumerate(UNIT):
                    if new_chunk:
                        split_hi(n0 + c + 2, q0 + j, it, pern, perq)
                    if not end or b >= 2 * FB:
                        continue
                    f = b // 2
                    if b % 2 == 0:
                        act.wait_ge(mm_done, q0 + j + 1 + perq * it)
                        if f0 + f >= 2:
                            act.wait_ge(t_done, f0 + f - 1 + 2 * FB * it)
                        nc.scalar.activation(st[:, f % 2, :].rearrange("p (a b) -> p a b", a=2),
                                             ps[:, (g0 + b) % 4, :, 0:HALF], ACT.Silu).then_inc(silu_done, 1)
                    else:
                        act.wait_ge(t_done, f0 + f + 1 + 2 * FB * it)
                        nc.scalar.activation(act_hi[:, f, :], tt[:, f % 2, :], ACT.Copy).then_inc(ahi_done, 1)

            split_hi(0, 0)
            split_hi(1, 0)
            act.wait_ge(consts_in, 16 * 13)
            nc.scalar.activation(cs[:], cond[:], ACT.Silu).then_inc(silu_c, 1)
            act.wait_ge(silu_c, 1)
            nc.scalar.activation(cs4[:, :, 0:2], cs[:], ACT.Copy).then_inc(cs_hi, 1)
            nc.scalar.activation(wr2[:, :, 0:EXPERTS], wr[:], ACT.Copy).then_inc(wr_hi, 1)
            for l in range(LAYERS):
                n0, q0, g0 = AT[l, "ada"]
                for c in range(ADA_CH):
                    split_hi(n0 + c + 2, q0 + c)
                    if l == 0 and 8 <= c < 8 + KB:
                        square(0, c - 8)
                if l == 0:
                    act.wait_ge(ones_set, 2)
                root(2 * l, D)
                modulate(2 * l, operand[l, "h1"])

                n0, q0, g0 = AT[l, "in"]
                for c, (kind, j) in enumerate(IN_ORDER):
                    split_hi(n0 + c + 2, q0 + c)
                    src = ps[:, (g0 + c) % 4, :, 0:HALF]
                    if kind in ("k", "q", "v", "gc"):
                        act.wait_ge(mm_done, q0 + c + 1)
                        buf = {"k": kT, "q": qT, "v": vT, "gc": gcx}[kind]
                        if kind == "v" and j == 0 and l:
                            act.wait_ge(tr_done, l * NS)
                        if kind == "k" and j == 0 and l:
                            act.wait_ge(k_out, 16 * l)
                        nc.scalar.activation(buf[:, j, 0:T].rearrange("p (a b) -> p a b", a=2), src, ACT.Copy)\
                            .then_inc({"k": kq_raw, "q": kq_raw, "v": vt_ready, "gc": gcx_ready}[kind], 1)

                act.wait_ge(lam_sum, l + 1)
                nc.scalar.activation(lexp[:], lsum[:], ACT.Exp).then_inc(lam_exp, 1)
                act.wait_ge(mm_done, AT[l, "vtok"][1])
                for j in range(CONV_BLOCKS):
                    act.wait_ge(conv_ready, 4 * l + j + 1)
                    nc.scalar.activation(a_hi[:, 4 + j, :], gcx[:, j, :], ACT.Copy).then_inc(ahi_done, 1)
                act.wait_ge(v_out, 16 * (l + 1))
                for i, (h, t, k0, nk) in enumerate(STEPS):
                    I = l * NS + i
                    act.wait_ge(max_done, I + 1)
                    if i >= 2:
                        act.wait_ge(tr_done, I - 1)
                    elif i == 0:
                        act.wait_ge(mm_done, AT[l, "vtok"][1] + HEADS)
                    for s in range(2):
                        nc.scalar.activation(pr[:, i % 2, s, 0:nk], S[:, s, 0:nk], ACT.Exp,
                                             bias=nbias[:, i % 2, s:s + 1], scale=QK ** -0.5,
                                             accum_out=rsum[:, i % 2, s:s + 1]).then_inc(exp_done, 1)
                    act.wait_ge(tr_done, I + 1)
                    if i >= 2:
                        act.wait_ge(pv_done, I - 1)
                    nc.scalar.activation(pT[:, i % 2, 0:nk], PT[:, 0:nk], ACT.Copy).then_inc(pt_ready, 1)
                    act.wait_ge(pv_done, I + 1)
                    nc.scalar.activation(att[:, h, t * P:(t + 1) * P], OT, ACT.Copy).then_inc(att_ready, 1)
                n0, q0, g0 = AT[l, "sub"]
                act.wait_ge(att_ready, (l + 1) * NS)
                for h in range(HEADS):
                    if h >= 2:
                        act.wait_ge(mm_done, q0 + h - 1)
                    nc.scalar.activation(sq[:, h % 2, :], att[:, h, :], ACT.Square).then_inc(att_sq, 1)
                for h in range(HEADS):
                    act.wait_ge(mm_done, q0 + h + 1)
                    nc.scalar.activation(st[:, h % 2, :].rearrange("p (a b) -> p a b", a=2) if h < 2 else
                                         tt[:, h % 2, :].rearrange("p (a b) -> p a b", a=2),
                                         ps[:, (g0 + h) % 4, :, 0:HALF], ACT.Sqrt, bias=eps[:, 0:1],
                                         scale=1.0 / VH).then_inc(att_root, 1)
                for h in range(HEADS):
                    act.wait_ge(att_norm, HEADS * l + h + 1)
                    nc.scalar.activation(a_hi[:, h, :], att[:, h, :], ACT.Copy).then_inc(ahi_done, 1)

                n0, q0, g0 = AT[l, "out"]
                for c in range(OUT_CH):
                    split_hi(n0 + c + 2, q0 + c)
                    square(2 * l + 1, c)
                root(2 * l + 1, D)
                modulate(2 * l + 1, operand[l, "h2"])

                n0, q0, g0 = AT[l, "ffn"]
                if l % 2 == 0:
                    for u in range(2):
                        unit(n0 + u * UNIT_CH, q0 + u * len(UNIT), g0 + u * UNIT_BLOCKS,
                             operand[l, "act"] + u * FB, u * FB)
                else:
                    act.wait_ge(dv_ready, 1)
                    nc.scalar.activation(ev[:], dv[:], ACT.Exp).then_inc(ev_ready, 1)
                    with act.Fori(0, EXPERTS // 2) as it:
                        for u in range(2):
                            unit(n0 + u * UNIT_CH, q0 + u * len(UNIT), g0 + u * UNIT_BLOCKS,
                                 operand[l, "act"] + u * FB, FC0 + u * FB, it)
                for kb in range(KB):
                    square(2 * l + 2, kb)
            root(4, D)

        @block.gpsimd
        def _(pool):
            nc.gpsimd.memset(ones[:], 1.0).then_inc(ones_set, 1)
            nc.gpsimd.memset(eps[:], EPS).then_inc(ones_set, 1)
            for i in range(5):
                for kb in range(KB):
                    m = KB * i + kb
                    pool.wait_ge(sq_done, m + 1)
                    if kb == 0:
                        if i:
                            pool.wait_ge(mm_done, NORM_AT[i - 1][1] + 1)
                        nc.gpsimd.tensor_copy(ss[:], sq[:, m % 2, :]).then_inc(ss_add, 1)
                    else:
                        pool.wait_ge(ss_add, m)
                        nc.gpsimd.tensor_tensor(ss[:], ss[:], sq[:, m % 2, :], ALU.add).then_inc(ss_add, 1)

        @block.vector
        def _(dve):
            chain = [0]

            def link(ins):
                chain[0] += 1
                ins.then_inc(dve_step, 1)
                dve.wait_ge(dve_step, chain[0])

            def split_lo(n, it=0, pern=0):
                s = n % SPLIT
                dve.wait_ge(hi_done, n + 1 + pern * it)
                nc.vector.tensor_tensor(w_lo[:, s, :], raw[:, n % RAW, :], w_hi[:, s, :].bitcast(F32), ALU.subtract)\
                    .then_inc(lo_done, 1)

            def lo_part(dst, full, hi, done):
                dve.wait_ge(ahi_done, done)
                nc.vector.tensor_tensor(dst, full, hi.bitcast(F32), ALU.subtract).then_inc(alo_done, 1)

            def normalise(i, width_gain=None):
                dve.wait_ge(root_done, i + 1)
                link(nc.vector.reciprocal(rstd[:], rstd[:]))
                nc.vector.engine_nop().then_inc(blk_free, 1) if False else None

            def norm(i, opnd):
                n0, q0, g0 = NORM_AT[i]
                dve.wait_ge(root_done, i + 1)
                ins = nc.vector.reciprocal(rstd[:], rstd[:])
                ins.then_inc(blk_free, 1)
                dve.wait_ge(blk_free, g0 + 1)
                for kb in range(KB):
                    if kb >= 2:
                        dve.wait_ge(h_done, KB * i + kb - 1)
                    nc.vector.tensor_tensor(st[:, kb % 2, :], x[:, kb, :], rstd[:], ALU.mult).then_inc(xn_done, 1)
                    if kb:
                        lo_part(a_lo[:, kb - 1, :], tt[:, (kb - 1) % 2, :], a_hi[:, kb - 1, :], opnd + kb)
                lo_part(a_lo[:, KB - 1, :], tt[:, (KB - 1) % 2, :], a_hi[:, KB - 1, :], opnd + KB)

            def residual(g, gate, d, x_sem=None, it=0, perg=0):
                for n, (hf, cols, toks, c) in enumerate(SEGMENTS):
                    ins = nc.vector.scalar_tensor_tensor(x[:, d, toks], ps[:, g % 4, hf, cols],
                                                         mod[:, gate * KB + d, c:c + 1], x[:, d, toks],
                                                         op0=ALU.mult, op1=ALU.add)
                ins.then_inc(blk_free, 1)
                if x_sem is not None:
                    dve.wait_ge(blk_free, g + 1)
                    dve.sem_inc(x_sem, 1)

            def unit(n0, q0, g0, opnd, f0, final, it=0, expert=None):
                pern, perq, perg, perf = 2 * UNIT_CH, 2 * len(UNIT), 2 * UNIT_BLOCKS, 2 * FB
                for j, (c, b, new_chunk, end, pieces) in enumerate(UNIT):
                    if new_chunk:
                        split_lo(n0 + c + 2, it, pern)
                    if not end:
                        continue
                    if b < 2 * FB:
                        f = b // 2
                        if b % 2 == 0:
                            continue
                        if f:
                            lo_part(act_lo[:, f - 1, :], tt[:, (f - 1) % 2, :], act_hi[:, f - 1, :],
                                    opnd + f + perf * it)
                        dve.wait_ge(silu_done, f0 + f + 1 + perf * it)
                        dve.wait_ge(mm_done, q0 + j + 1 + perq * it)
                        up = ps[:, (g0 + b) % 4, :, 0:HALF]
                        s3 = st[:, f % 2, :].rearrange("p (a b) -> p a b", a=2)
                        t3 = tt[:, f % 2, :].rearrange("p (a b) -> p a b", a=2)
                        if expert is None:
                            nc.vector.tensor_tensor(t3, s3, up, ALU.mult).then_inc(t_done, 1)
                            dve.wait_ge(t_done, f0 + f + 1)
                            dve.sem_inc(blk_free, 2)
                        else:
                            nc.vector.tensor_tensor(s3, s3, up, ALU.mult).then_inc(blk_free, 2)
                            dve.wait_ge(blk_free, g0 + b + 1 + perg * it)
                            nc.vector.tensor_tensor(tt[:, f % 2, :], st[:, f % 2, :], gbc[:, expert, :], ALU.mult)\
                                .then_inc(t_done, 1)
                    else:
                        d = b - 2 * FB
                        if d == 0:
                            pass
                        dve.wait_ge(mm_done, q0 + j + 1 + perq * it)
                        residual(g0 + b, 5, d, x_new if final else None)
                    if b == 2 * FB - 1:
                        lo_part(act_lo[:, FB - 1, :], tt[:, (FB - 1) % 2, :], act_hi[:, FB - 1, :],
                                opnd + FB + perf * it)

            dve.wait_ge(consts_in, 16 * 13)
            split_lo(0)
            split_lo(1)
            dve.wait_ge(silu_c, 1)
            dve.wait_ge(cs_hi, 1)
            nc.vector.tensor_tensor(cs4[:, :, 2:4], cs[:], cs4[:, :, 0:2].bitcast(F32), ALU.subtract)\
                .then_inc(cs_ready, 1)
            dve.wait_ge(wr_hi, 1)
            nc.vector.tensor_tensor(wr2[:, :, EXPERTS:], wr[:], wr2[:, :, 0:EXPERTS].bitcast(F32), ALU.subtract)\
                .then_inc(wr_ready, 1)
            for l in range(LAYERS):
                n0, q0, g0 = AT[l, "ada"]
                for c in range(ADA_CH):
                    split_lo(n0 + c + 2)
                    if c == 4:
                        link(nc.vector.tensor_tensor(lp[:, 0:QK], lq[:, l, 0:QK], lq[:, l, QK:2 * QK], ALU.mult))
                        link(nc.vector.tensor_tensor(lp[:, QK:], lq[:, l, 2 * QK:3 * QK], lq[:, l, 3 * QK:], ALU.mult))
                        nc.vector.tensor_reduce(lsum[:], lp[:].rearrange("p (a b) -> p a b", a=2), AX, ALU.add)\
                            .then_inc(lam_sum, 1)
                        link(nc.vector.tensor_scalar(subgs[:, l:l + 1], subg[:, l:l + 1], 1.0 - LAM_INIT[l], None,
                                                     ALU.mult))
                dve.wait_ge(mm_done, q0 + ADA_CH)
                col = ps[:, g0 % 4, 0, 0:4 * ADA_CH].rearrange("p (c j) -> p c j", j=4)
                link(nc.vector.tensor_tensor(mod[:], col[:, :, 0:2], bada[:, l, :].unsqueeze(2).broadcast_to([P, 6 * KB, 2]),
                                             ALU.add))
                nc.vector.tensor_tensor(mod[:], mod[:], col[:, :, 2:4], ALU.add).then_inc(blk_free, 1)
                dve.wait_ge(blk_free, g0 + 1)
                for w, g in ((0, gmix), (1, gffn)):
                    ins = nc.vector.scalar_tensor_tensor(gain[:, w], mod[:, (3 * w + 1) * KB:(3 * w + 2) * KB, :], 1.0,
                                                         g[:, l, :].unsqueeze(2).broadcast_to([P, KB, 2]),
                                                         op0=ALU.add, op1=ALU.mult)
                ins.then_inc(mod_ready, 1)
                norm(2 * l, operand[l, "h1"])

                n0, q0, g0 = AT[l, "in"]
                lat = slice(CTX, T)
                for c, (kind, j) in enumerate(IN_ORDER):
                    split_lo(n0 + c + 2)
                    src = ps[:, (g0 + c) % 4, :, 0:HALF]
                    if kind in ("k", "q"):
                        buf = kT if kind == "k" else qT
                        dve.wait_ge(kq_raw, 8 * l + c + 1)
                        dve.sem_inc(blk_free, 1)
                        link(nc.vector.stream_shuffle(swp[:], buf[:, j, lat], SWAP))
                        link(nc.vector.tensor_tensor(swp[:], swp[:], sin_s[:], ALU.mult))
                        link(nc.vector.tensor_tensor(buf[:, j, lat], buf[:, j, lat], cos_s[:], ALU.mult))
                        nc.vector.tensor_tensor(buf[:, j, lat], buf[:, j, lat], swp[:], ALU.add).then_inc(kq_ready, 1)
                        dve.wait_ge(kq_ready, 8 * l + c + 1)
                    elif kind == "v":
                        dve.wait_ge(vt_ready, 4 * l + j + 1)
                        dve.sem_inc(blk_free, 1)
                    elif kind == "gc":
                        dve.wait_ge(gcx_ready, 4 * l + j + 1)
                        dve.sem_inc(blk_free, 1)
                    elif kind == "xin":
                        dve.wait_ge(mm_done, q0 + c + 1)
                        g3 = gcx[:, j, :].rearrange("p (a b) -> p a b", a=2)
                        nc.vector.tensor_tensor(g3, g3, src, ALU.mult).then_inc(blk_free, 1)
                    else:
                        dve.wait_ge(blk_free, g0 + c)
                        link(nc.vector.tensor_scalar(cv[:], gcx[:, j, :], convw[:, l, 1, j:j + 1], None, ALU.mult))
                        for lo, hi in ((0, CTX), (CTX, T)):
                            link(nc.vector.scalar_tensor_tensor(cv[:, lo + 1:hi], gcx[:, j, lo:hi - 1],
                                                                convw[:, l, 0, j:j + 1], cv[:, lo + 1:hi],
                                                                op0=ALU.mult, op1=ALU.add))
                            link(nc.vector.scalar_tensor_tensor(cv[:, lo:hi - 1], gcx[:, j, lo + 1:hi],
                                                                convw[:, l, 2, j:j + 1], cv[:, lo:hi - 1],
                                                                op0=ALU.mult, op1=ALU.add))
                        dve.wait_ge(mm_done, q0 + c + 1)
                        link(nc.vector.tensor_tensor(gcx[:, j, :].rearrange("p (a b) -> p a b", a=2),
                                                     cv[:].rearrange("p (a b) -> p a b", a=2), src, ALU.mult))
                        dve.sem_inc(blk_free, 1)
                        dve.sem_inc(conv_ready, 1)

                vn, vq, vg = AT[l, "vtok"]
                for h in range(HEADS):
                    dve.wait_ge(mm_done, vq + h + 1)
                    for t0, t1, bank in ((0, 4, 0), (4, TT, 1)):
                        ins = nc.vector.tensor_copy(vtok[:, t0:t1, h * VH:(h + 1) * VH],
                                                    ps[:, (vg + h) % 4, bank, 0:(t1 - t0) * P]
                                                    .rearrange("p (t e) -> p t e", e=VH))
                    link(ins)
                    dve.sem_inc(blk_free, 1)
                    dve.sem_inc(vtok_ready, 1)
                dve.wait_ge(lam_exp, l + 1)
                link(nc.vector.tensor_tensor(nlam[:], lexp[:, 1:2], lexp[:, 0:1], ALU.subtract))
                link(nc.vector.tensor_scalar(nlam[:], nlam[:], LAM_INIT[l], None, ALU.subtract))
                for j in range(CONV_BLOCKS):
                    lo_part(a_lo[:, 4 + j, :], gcx[:, j, :], a_hi[:, 4 + j, :], operand[l, "cat"] + j + 1)

                def row_max(i):
                    h, t, k0, nk = STEPS[i]
                    dve.wait_ge(scores_done, l * NS + i + 1)
                    link(nc.vector.tensor_reduce(nmax[:, i % 2, :], S[:, :, 0:nk], AX, ALU.max))
                    nc.vector.tensor_scalar(nbias[:, i % 2, :], nmax[:, i % 2, :], -QK ** -0.5, None, ALU.mult)\
                        .then_inc(max_done, 1)

                row_max(0)
                for i, (h, t, k0, nk) in enumerate(STEPS):
                    I = l * NS + i
                    b = i % 2
                    dve.wait_ge(exp_done, 2 * (I + 1))
                    link(nc.vector.reciprocal(rinv[:, b, :], rsum[:, b, :]))
                    link(nc.vector.tensor_tensor(rneg[:, b, :], rinv[:, b, 1:2], nlam[:], ALU.mult))
                    link(nc.vector.tensor_scalar(pr[:, b, 1, 0:nk], pr[:, b, 1, 0:nk], rneg[:, b, 0:1], None, ALU.mult))
                    nc.vector.scalar_tensor_tensor(pr[:, b, 0, 0:nk], pr[:, b, 0, 0:nk], rinv[:, b, 0:1],
                                                   pr[:, b, 1, 0:nk], op0=ALU.mult, op1=ALU.add)\
                        .then_inc(comb_done, 1)
                    if i + 1 < NS:
                        row_max(i + 1)
                sn, sq0, sg = AT[l, "sub"]
                for h in range(HEADS):
                    buf = (st if h < 2 else tt)[:, h % 2, :]
                    dve.wait_ge(att_root, HEADS * l + h + 1)
                    link(nc.vector.reciprocal(buf, buf))
                    dve.sem_inc(blk_free, 1)
                    nc.vector.scalar_tensor_tensor(att[:, h, :], att[:, h, :], subgs[:, l:l + 1], buf,
                                                   op0=ALU.mult, op1=ALU.mult).then_inc(att_norm, 1)
                    if h:
                        lo_part(a_lo[:, h - 1, :], att[:, h - 1, :], a_hi[:, h - 1, :], operand[l, "cat"] + 4 + h)
                lo_part(a_lo[:, HEADS - 1, :], att[:, HEADS - 1, :], a_hi[:, HEADS - 1, :],
                        operand[l, "cat"] + 4 + HEADS)

                n0, q0, g0 = AT[l, "out"]
                for c in range(OUT_CH):
                    split_lo(n0 + c + 2)
                    dve.wait_ge(mm_done, q0 + c + 1)
                    residual(g0 + c, 2, c, x_new)
                norm(2 * l + 1, operand[l, "h2"])

                n0, q0, g0 = AT[l, "ffn"]
                if l % 2 == 0:
                    for u in range(2):
                        unit(n0 + u * UNIT_CH, q0 + u * len(UNIT), g0 + u * UNIT_BLOCKS,
                             operand[l, "act"] + u * FB, u * FB, u == 1)
                else:
                    rn, rq, rg = AT[l, "route"]
                    dve.wait_ge(mm_done, rq + 1)
                    lg = ps[:, rg % 4, 0, 0:16 * TT].rearrange("p (t j) -> p t j", j=16)
                    link(nc.vector.tensor_copy(logits[:], lg[:, :, 0:EXPERTS]))
                    link(nc.vector.tensor_tensor(logits[:], logits[:], lg[:, :, EXPERTS:], ALU.add))
                    dve.sem_inc(blk_free, 1)
                    for t in range(TT):
                        link(nc.vector.max(tv[:, t, :], logits[:, t, :]))
                        link(nc.vector.max_index(ti[:, t, :], tv[:, t, :], logits[:, t, :]))
                    link(nc.vector.tensor_copy(tf[:], ti[:]))
                    link(nc.vector.tensor_tensor(dv[:], tv[:, :, 1], tv[:, :, 0], ALU.subtract))
                    dve.sem_inc(dv_ready, 1)
                    dve.wait_ge(ev_ready, 1)
                    link(nc.vector.tensor_scalar(g1[:], ev[:], 1.0, None, ALU.add))
                    link(nc.vector.reciprocal(g1[:], g1[:]))
                    link(nc.vector.tensor_tensor(g2[:], ev[:], g1[:], ALU.mult))
                    for t in range(TT):
                        link(nc.vector.tensor_scalar(oh[:, 0, :], iot[:], tf[:, t, 0:1], g1[:, t:t + 1],
                                                     ALU.is_equal, ALU.mult))
                        link(nc.vector.tensor_scalar(oh[:, 1, :], iot[:], tf[:, t, 1:2], g2[:, t:t + 1],
                                                     ALU.is_equal, ALU.mult))
                        link(nc.vector.tensor_tensor(gates[:, t, :], oh[:, 0, :], oh[:, 1, :], ALU.add))
                    for e in range(EXPERTS):
                        if e:
                            dve.wait_ge(mm_done, rq + 1 + e)
                        link(nc.vector.tensor_copy(gex[:], gates[:, :, e:e + 1].broadcast_to([P, TT, P])))
                        dve.sem_inc(gex_ready, 1)
                        dve.wait_ge(mm_done, rq + 2 + e)
                        for bank, t0, t1 in ((0, 0, 4), (1, 4, TT)):
                            ins = nc.vector.tensor_copy(gbc[:, e, t0 * P:t1 * P],
                                                        ps[:, (rg + 1 + e) % 4, bank, 0:(t1 - t0) * P])
                        link(ins)
                        dve.sem_inc(blk_free, 1)
                    with dve.Fori(0, EXPERTS // 2) as it:
                        for u in range(2):
                            unit(n0 + u * UNIT_CH, q0 + u * len(UNIT), g0 + u * UNIT_BLOCKS,
                                 operand[l, "act"] + u * FB, FC0 + u * FB, False, it, 2 * it + u)
                    dve.wait_ge(blk_free, g0 + EXPERTS * UNIT_BLOCKS)
                    dve.sem_inc(x_new, KB)
            n0, q0, g0 = AT["final"]
            dve.wait_ge(root_done, 5)
            link(nc.vector.reciprocal(rstd[:], rstd[:]))
            for kb in range(KB):
                nc.vector.scalar_tensor_tensor(x[:, kb, :], x[:, kb, :], gfin[:, kb:kb + 1], rstd[:],
                                               op0=ALU.mult, op1=ALU.mult).then_inc(yblk, 1)


def kernel(**inputs):
    import numpy as np
    import concourse.bacc as bacc
    from concourse.bass_utils import run_bass_kernel_spmd

    def arr(a):
        return np.ascontiguousarray(a)

    def cols(w):
        *lead, k, n = w.shape
        w = w.reshape(*lead, k // P, P, n // P, P)
        r = len(lead)
        return arr(w.transpose(*range(r), r + 2, r + 1, r, r + 3)).reshape(*lead, n // P, P, k)

    I = {k: np.asarray(v) for k, v in inputs.items()}
    x = np.concatenate([I["x_prompt"][0], I["x_sample"][0]], 0)
    xT = arr(x.T.reshape(KB, P, T).transpose(1, 0, 2))
    cond = np.stack([I["c_ctx"], I["c"][0]], 1)
    condT = arr(cond.reshape(KB, P, 2).transpose(1, 0, 2))
    ada = cols(I["w_ada"])
    w_in = cols(I["w_in"])
    order = [4 + j for j in range(4)] + [j for j in range(4)] + [8 + j for j in range(4)] \
        + [16 + j for j in range(4)] + [20 + j for j in range(4)] + [12 + j for j in range(4)]
    w_in = arr(w_in[:, order])
    w_out = cols(I["w_out"])
    dg = I["w_gu_dense"][0].reshape(D, 2, 2, FF).transpose(2, 0, 1, 3).reshape(2, D, 2 * FF)
    gu = np.concatenate([dg, I["w_gu_moe"][0]], 0)
    gu = cols(gu)
    gu = arr(gu.reshape(-1, 2, FB, P, D).transpose(0, 2, 1, 3, 4)).reshape(-1, 2 * FB, P, D)
    down = np.concatenate([I["w_down_dense"][0].reshape(2, FF, D), I["w_down_moe"][0]], 0)
    down = down.reshape(-1, FB, P, KB, P).transpose(0, 3, 1, 2, 4).reshape(-1, FB, 8, P, P)
    down = arr(down.transpose(0, 1, 3, 2, 4)).reshape(-1, FB, P, CHUNK)

    def feat(a):
        a = a.reshape(*a.shape[:-1], -1, P)
        return arr(np.moveaxis(a, -1, 0))

    half = QK // 4
    freqs = np.float32(10000.0) ** (-np.arange(half, dtype=np.float32) / np.float32(half))
    pos = np.arange(LAT)
    row, col = (pos // 64).astype(np.float32), (pos % 64).astype(np.float32)
    ang = np.stack([row, col])[:, None, :] * freqs[None, :, None]
    c, s = np.cos(ang).astype(np.float32), np.sin(ang).astype(np.float32)
    one = np.concatenate([np.concatenate([c[a], c[a]]) for a in range(2)])
    sgn = np.concatenate([np.concatenate([-s[a], s[a]]) for a in range(2)])
    cos, sin = arr(np.concatenate([one, one])), arr(np.concatenate([sgn, sgn]))

    kc = I["cache_k"][0].reshape(LAYERS, PAST, HEADS, P).transpose(0, 3, 2, 1)
    vc = I["cache_v"][0].reshape(LAYERS, PAST // P, P, HEADS * VH).transpose(0, 2, 1, 3)
    arrays = {
        "xT": xT, "condT": condT, "ada_w": ada, "in_w": w_in, "out_w": w_out, "gu_w": gu, "down_w": down,
        "router_w": arr(I["w_router"][0].reshape(KB, P, EXPERTS).transpose(1, 0, 2)),
        "b_ada": feat(I["b_ada"]), "g_mix": feat(I["norm_mix_g"]), "g_ffn": feat(I["norm_ffn_g"]),
        "g_fin": feat(I["final_g"]), "lam_qk": arr(I["lambda_qk"]).reshape(LAYERS, 4 * QK),
        "subln": arr(I["subln_g"].T), "conv_w": feat(I["conv_w"]), "kcT": arr(kc), "vc": arr(vc),
        "cos": cos, "sin": sin, "ident": np.eye(P, dtype=np.float32),
        "iota8": arr(np.broadcast_to(np.arange(EXPERTS, dtype=np.float32), (P, EXPERTS))),
    }
    nc = bacc.Bacc("TRN2", target_bir_lowering=False, num_devices=1, dynamic_dma_scratch_size=1024)
    args = [nc.dram_tensor(n, a.shape, mybir.dt.from_np(a.dtype), kind="ExternalInput").ap()
            for n, a in arrays.items()]
    outs = [("y", (P, KB, T)), ("newk", (LAYERS, P, HEADS, CTX)), ("newv", (LAYERS, P, HEADS, CTX))]
    args += [nc.dram_tensor(n, s, F32, kind="ExternalOutput").ap() for n, s in outs]
    hybrid_step(nc, *args)
    r = run_bass_kernel_spmd(nc, [arrays], core_ids=[0]).results[0]
    y = np.asarray(r["y"]).transpose(1, 0, 2).reshape(D, T).T
    newk = np.asarray(r["newk"]).transpose(0, 3, 2, 1).reshape(1, LAYERS, CTX, HEADS, 2, QK)
    newv = np.asarray(r["newv"]).transpose(0, 3, 2, 1).reshape(1, LAYERS, CTX, HEADS, VH)
    return arr(y[:CTX])[None], arr(y[CTX:])[None], arr(newk), arr(newv)
```

```python
from contextlib import ExitStack

import concourse.bass as bass
from concourse import mybir

P = 128
D = 1024
KB = D // P
CTX, LAT, PAST = 128, 512, 256
T = CTX + LAT
HALF = T // 2
TT = T // P
NKEY = LAT + PAST
KCOLS = T + PAST
KT = KCOLS // P
LAYERS = 2
HEADS, QK, VH = 4, 64, 128
ATT_BLOCKS = 4
CONV_BLOCKS = 4
EXPERTS = 8
CAP = 256
ROUNDS = -(-T // CAP)
ST = CAP // P
FF = 1408
FB = FF // P
EPS = 1e-6
CHUNK = 8 * P
RAW, SPLIT = 6, 3
ADA_CH, IN_CH, OUT_CH, UNIT_CH = 48, 24, 8, 33
LAM_INIT = [0.8 - 0.6 * 2.718281828459045 ** (-0.3 * l) for l in range(LAYERS)]
SWAP = [(i + 16) % 32 for i in range(32)]

F32 = mybir.dt.float32
F32R = mybir.dt.float32r
U32 = mybir.dt.uint32
I32 = mybir.dt.int32
ALU = mybir.AluOpType
ACT = mybir.ActivationFunctionType
AX = mybir.AxisListType.X
SEGMENTS = [(0, slice(0, CTX), slice(0, CTX), 0), (0, slice(CTX, HALF), slice(CTX, HALF), 1),
            (1, slice(0, HALF), slice(HALF, T), 1)]
TOKENS_OF = [(slice(0, CTX), 0), (slice(CTX, T), 1)]


def unit_groups(out_major):
    groups = []
    for c in range(2 * FB):
        groups.append((c, c, True, True, [(i, i) for i in range(KB)]))
    pieces = [(d, k) for d in range(KB) for k in range(FB)]
    for c in range(FB):
        part = [(i, *pieces[8 * c + i]) for i in range(8)]
        for d in sorted({p[1] for p in part}):
            mine = [(i, k) for i, dd, k in part if dd == d]
            groups.append((2 * FB + c, 2 * FB + d, mine[0][0] == 0, mine[-1][1] == FB - 1, mine))
    return groups


UNIT = unit_groups(True)
UNIT_BLOCKS = 2 * FB + KB
EXPERT = [("gather", i, i, None) for i in range(2)] + [("turn", i, 2 + i, None) for i in range(ST)] \
    + [("scatter", d, 4 + d, None) for d in range(KB)] + [("gu", c, 12 + c, c) for c in range(2 * FB)] \
    + [("down", k, 34, 2 * FB + k) for k in range(FB)]
EXPERT_BLOCKS = 36
EXPERT_OPERANDS = 2 + FB + ST
SCATTER_AT = [j for j, e in enumerate(EXPERT) if e[0] == "scatter"][0]

ADA_SEQ = [("rows", 0, k) for k in range(KB)]
for _g in range(1, 6):
    ADA_SEQ += [("rows", _g, k) for k in range(KB)] + [("turn", _g - 1, 0)]
ADA_SEQ += [("turn", 5, 0)]
ADA_BLOCK = {}
for _kind, _g, _k in ADA_SEQ:
    ADA_BLOCK.setdefault((_kind, _g), len(ADA_BLOCK))


def plan():
    at, n, q, g = {}, 0, 0, 0
    for l in range(LAYERS):
        steps = [("ada", ADA_CH, len(ADA_SEQ), len(ADA_BLOCK)), ("norm1", 0, 1, 1), ("in", IN_CH, 28, 28),
                 ("sub", 0, 4, 4), ("out", OUT_CH, OUT_CH, OUT_CH), ("norm2", 0, 1, 1)]
        if l % 2 == 0:
            steps += [("ffn", 2 * UNIT_CH, 2 * len(UNIT), 2 * UNIT_BLOCKS)]
        else:
            steps += [("route", 0, 3 + TT, 3 + TT),
                      ("ffn", ROUNDS * EXPERTS * UNIT_CH, ROUNDS * EXPERTS * len(EXPERT),
                       ROUNDS * EXPERTS * EXPERT_BLOCKS),
                      ("last", 0, KB, KB)]
        for name, dn, dq, dg in steps:
            at[l, name] = (n, q, g)
            n, q, g = n + dn, q + dq, g + dg
    at["final"] = (n, q, g)
    return at


AT = plan()
NORM_AT = [AT[0, "norm1"], AT[0, "norm2"], AT[1, "norm1"], AT[1, "norm2"], AT["final"]]
IN_KINDS = [("k", j) for j in range(4)] + [("q", j) for j in range(4)] + [("v", j) for j in range(4)] \
    + [("gc", j) for j in range(4)] + [("xin", j) for j in range(4)] + [("gb", j) for j in range(4)]
IN_SEQ = []
for _c, (_kind, _j) in enumerate(IN_KINDS):
    IN_SEQ.append((_kind, _j, _c))
    if _kind == "gc":
        IN_SEQ.append(("turn", _j, None))
STEPS = [(h, t, 0, CTX) if t == 0 else (h, t, CTX, NKEY) for h in range(HEADS) for t in range(TT)]
NS = len(STEPS)
assert len(IN_SEQ) == 28


def hybrid_step(nc, xT, condT, ada_w, in_w, out_w, gu_w, down_w, router_w, b_ada, g_mix, g_ffn, g_fin, lam_qk,
                subln, conv_w, kcT, vc, cos, sin, ident, iota, below, moe_down_w, y, newk, newv):
    with ExitStack() as ctx:
        def sb(name, shape, dt=F32, c=ctx):
            return c.enter_context(nc.sbuf_tensor(name, shape, dt))

        def sem(name):
            return ctx.enter_context(nc.semaphore(name))

        x = sb("x", [P, KB, T])
        a_hi = sb("a_hi", [P, KB, T], F32R)
        a_lo = sb("a_lo", [P, KB, T], F32R)
        raw = sb("raw", [P, RAW, CHUNK])
        w_hi = sb("w_hi", [P, SPLIT, CHUNK], F32R)
        w_lo = sb("w_lo", [P, SPLIT, CHUNK], F32R)
        st = sb("st", [P, 2, T])
        tt = sb("tt", [P, 2, T])
        sq = sb("sq", [P, 2, T])
        ss = sb("ss", [P, T])
        rstd = sb("rstd", [P, T])
        eps = sb("eps", [P, 1])
        cos_s = sb("cos_s", [P, LAT])
        sin_s = sb("sin_s", [P, LAT])
        ones = sb("ones", [P, P])
        idn = sb("idn", [P, P])
        cond = sb("cond", [P, KB, 2])
        cs = sb("cs", [P, KB, 2])
        cs4 = sb("cs4", [P, KB, P], F32R)
        bada = sb("bada", [P, LAYERS, 6 * KB])
        mod = sb("mod", [P, 6 * KB, 2])
        gain = sb("gain", [P, 2, KB, 2])
        gmix = sb("gmix", [P, LAYERS, KB])
        gffn = sb("gffn", [P, LAYERS, KB])
        gfin = sb("gfin", [P, KB])
        lq = sb("lq", [P, LAYERS, 4 * QK])
        lp = sb("lp", [P, 2 * QK])
        lsum = sb("lsum", [P, 2])
        lexp = sb("lexp", [P, 2])
        nlam = sb("nlam", [P, 1])
        subg = sb("subg", [P, LAYERS])
        subgs = sb("subgs", [P, LAYERS])
        convw = sb("convw", [P, LAYERS, 3, CONV_BLOCKS])
        nbias = sb("nbias", [P, 4])
        rsum = sb("rsum", [P, 2, 2])
        rinv = sb("rinv", [P, 2, 2])
        wr = sb("wr", [P, KB, EXPERTS])
        iot = sb("iot", [P, CAP])
        bel = sb("bel", [P, P])
        logits = sb("logits", [P, TT, EXPERTS])
        tv = sb("tv", [P, TT, 8])
        ti = sb("ti", [P, TT, 8], U32)
        tf = sb("tf", [P, TT, 8])
        dv = sb("dv", [P, TT])
        ev = sb("ev", [P, TT])
        g1 = sb("g1", [P, TT])
        g2 = sb("g2", [P, TT])
        gates = sb("gates", [P, TT, EXPERTS])
        oh = sb("oh", [P, 2, EXPERTS])
        mask = sb("mask", [P, TT, EXPERTS])
        before = sb("before", [P, TT + 1, EXPERTS])
        rank = sb("rank", [P, TT, EXPERTS + 1])
        grouped = sb("grouped", [P, TT, EXPERTS, 2], F32R)
        rcol = sb("rcol", [P, TT])
        gsl = sb("gsl", [P, 2, ST, 2])
        gslot = sb("gslot", [P, 2, ST])
        most = sb("most", [P, 1])
        most_i = sb("most_i", [P, 1], I32)

        with ExitStack() as mix:
            kT = sb("kT", [P, HEADS, KCOLS], c=mix)
            qT = sb("qT", [P, HEADS, T], c=mix)
            vtok = sb("vtok", [P, KT, HEADS * VH], c=mix)
            att = sb("att", [P, HEADS, T], c=mix)
            gcx = sb("gcx", [P, CONV_BLOCKS, T], c=mix)
            pT = sb("pT", [P, 2, NKEY], c=mix)
            with ExitStack() as vs:
                vT = sb("vT", [P, HEADS, T], c=vs)
            with ExitStack() as ms:
                mrow = sb("mrow", [P, 2, D], c=ms)
            pr = sb("pr", [P, 2, 2, NKEY], c=mix)
        with ExitStack() as ffn:
            act_hi = sb("act_hi", [P, FB, T], F32R, c=ffn)
            act_lo = sb("act_lo", [P, FB, T], F32R, c=ffn)
        with ExitStack() as moe:
            with ExitStack() as hs:
                hraw = sb("hraw", [P, KB, T], c=hs)
                lgT = sb("lgT", [EXPERTS, T], c=hs)
            hg_hi = sb("hg_hi", [P, KB, CAP], F32R, c=moe)
            hg_lo = sb("hg_lo", [P, KB, CAP], F32R, c=moe)
            ea_hi = sb("ea_hi", [P, FB, CAP], F32R, c=moe)
            ea_lo = sb("ea_lo", [P, FB, CAP], F32R, c=moe)
            sel = sb("sel", [P, TT, CAP], F32R, c=moe)
            selT = sb("selT", [P, 2, ST, T], F32R, c=moe)
            ey_hi = sb("ey_hi", [P, ST, D], F32R, c=moe)
            ey_lo = sb("ey_lo", [P, ST, D], F32R, c=moe)
        ht_hi = a_hi[:].rearrange("p a b -> p (a b)").rearrange("p (t d) -> p t d", t=TT)
        ht_lo = a_lo[:].rearrange("p a b -> p (a b)").rearrange("p (t d) -> p t d", t=TT)

        ps = ctx.enter_context(nc.psum_tensor("ps", [P, 4, 2, 512], F32))
        S = ps[:, 0:3].rearrange("p a b c -> p a (b c)")
        PT = ps[:, 3].rearrange("p b c -> p (b c)")[:, 0:NKEY]
        OT = ps[:, 3, 1, NKEY - 512:512].rearrange("p (a b) -> p a b", a=2)

        raw_full = [sem(f"raw_full{i}") for i in range(RAW)]
        hi_done = sem("hi_done")
        lo_done = sem("lo_done")
        mm_done = sem("mm_done")
        blk_free = sem("blk_free")
        consts_in = sem("consts_in")
        x_in = sem("x_in")
        cache_in = [sem(f"cache_in{l}") for l in range(LAYERS)]
        ones_set = sem("ones_set")
        dve_step = sem("dve_step")
        silu_c = sem("silu_c")
        cs_hi = sem("cs_hi")
        cs_ready = sem("cs_ready")
        mod_ready = sem("mod_ready")
        x_new = sem("x_new")
        sq_done = sem("sq_done")
        ss_add = sem("ss_add")
        root_done = sem("root_done")
        rstd_done = sem("rstd_done")
        xn_done = sem("xn_done")
        h_done = sem("h_done")
        ahi_done = sem("ahi_done")
        alo_done = sem("alo_done")
        kq_raw = sem("kq_raw")
        kq_ready = sem("kq_ready")
        vt_ready = sem("vt_ready")
        gcx_ready = sem("gcx_ready")
        conv_ready = sem("conv_ready")
        vtok_ready = sem("vtok_ready")
        row_done = sem("row_done")
        lam_sum = sem("lam_sum")
        lam_exp = sem("lam_exp")
        lam_ready = sem("lam_ready")
        scores_done = sem("scores_done")
        max_done = sem("max_done")
        exp_done = sem("exp_done")
        comb_done = sem("comb_done")
        tr_done = sem("tr_done")
        pt_ready = sem("pt_ready")
        pv_done = sem("pv_done")
        att_ready = sem("att_ready")
        att_sq = sem("att_sq")
        att_root = sem("att_root")
        att_norm = sem("att_norm")
        silu_done = sem("silu_done")
        t_raw = sem("t_raw")
        t_done = sem("t_done")
        dv_ready = sem("dv_ready")
        ev_ready = sem("ev_ready")
        lgT_ready = sem("lgT_ready")
        mask_ready = sem("mask_ready")
        most_ready = sem("most_ready")
        gates_set = sem("gates_set")
        gates_hi = sem("gates_hi")
        gates_ready = sem("gates_ready")
        cleared = sem("cleared")
        rcol_set = sem("rcol_set")
        rank_moved = sem("rank_moved")
        round_open = sem("round_open")
        sel_ready = sem("sel_ready")
        selT_ready = sem("selT_ready")
        gslot_ready = sem("gslot_ready")
        yblk = sem("yblk")
        out_done = sem("out_done")
        k_out = sem("k_out")
        v_out = sem("v_out")
        FC0 = 2 * FB

        block = ctx.enter_context(nc.Block())

        H0 = {(0, 1): 0, (0, 2): 2 * KB + 0, (1, 1): 0, (1, 2): 0}
        count = 0
        operand = {}
        for l in range(LAYERS):
            for what, k in (("h1", KB), ("cat", KB), ("h2", KB), ("act", 2 * FB if l % 2 == 0 else 0)):
                if l % 2 and what == "h2":
                    k = TT
                operand[l, what] = count
                count += k

        @block.sync
        def _(sp):
            def load(n, src, it=0, per=0):
                if n >= RAW:
                    sp.wait_ge(lo_done, n - RAW + 1 + per * it)
                sp.dma_start(raw[:, n % RAW, :], src).then_inc(raw_full[n % RAW], 16)

            sp.dma_start(cond[:], condT).then_inc(consts_in, 16)
            small = [(bada, b_ada), (gmix, g_mix), (gffn, g_ffn), (gfin, g_fin), (subg, subln), (convw, conv_w),
                     (cos_s, cos), (sin_s, sin), (idn, ident), (wr, router_w), (iot, iota), (bel, below),
                     (lq, lam_qk.partition_broadcast(P))]
            n = 0
            for c in range(4):
                load(n, ada_w[0, c])
                n += 1
            for dst, src in small:
                sp.dma_start(dst[:], src).then_inc(consts_in, 16)
            sp.dma_start(x[:], xT).then_inc(x_in, 16)
            for l in range(LAYERS):
                for c in range(4 if l == 0 else 0, ADA_CH):
                    load(n, ada_w[l, c])
                    n += 1
                if l:
                    sp.wait_ge(pv_done, l * NS)
                    sp.wait_ge(mm_done, AT[l, "ada"][1])
                sp.dma_start(kT[:, :, T:KCOLS], kcT[l]).then_inc(cache_in[l], 16)
                sp.dma_start(vtok[:, TT:KT, :], vc[l]).then_inc(cache_in[l], 16)
                for c in range(IN_CH):
                    load(n, in_w[l, c])
                    n += 1
                for c in range(OUT_CH):
                    load(n, out_w[l, c])
                    n += 1
                sp.wait_ge(kq_raw, 8 * l + 4)
                sp.dma_start(newk[l], kT[:, :, 0:CTX]).then_inc(k_out, 16)
                sp.wait_ge(vt_ready, 4 * (l + 1))
                sp.dma_start(newv[l], vT[:, :, 0:CTX]).then_inc(v_out, 16)
                if l % 2 == 0:
                    for u in range(2):
                        for c in range(2 * FB):
                            load(n, gu_w[2 * FB * u + c])
                            n += 1
                        for c in range(FB):
                            load(n, down_w[u, c])
                            n += 1
                else:
                    def experts(first):
                        with sp.Fori(0, EXPERTS // 2) as it:
                            for c in range(2, 2 * UNIT_CH + 2):
                                u, cc = c // UNIT_CH, c % UNIT_CH
                                e = 2 * it + u
                                src = gu_w[2 * FB * (2 + e) + cc] if cc < 2 * FB else moe_down_w[e, cc - 2 * FB]
                                load(n + c, src, first + it, 2 * UNIT_CH)

                    for c in range(2):
                        load(n + c, gu_w[2 * FB * 2 + c])
                    experts(0)
                    sp.wait_ge(most_ready, 1)
                    with sp.If(sp.value_load(most_i[0:1, 0:1], min_val=0, max_val=T) > CAP):
                        with sp.Fori(1, ROUNDS) as r:
                            experts(EXPERTS // 2 * r)
            for kb in range(KB):
                sp.wait_ge(yblk, kb + 1)
                sp.dma_start(y[:, kb], st[:, kb % 2, :] if kb < 0 else x[:, kb, :]).then_inc(out_done, 16)
            sp.wait_ge(out_done, 16 * KB)
            sp.wait_ge(k_out, 16 * LAYERS)
            sp.wait_ge(v_out, 16 * LAYERS)

        @block.tensor
        def _(pe):
            def open_block(g, it=0, per=0):
                if g >= 4:
                    pe.wait_ge(blk_free, g - 3 + per * it)

            def product(out, wsl, opnd_hi, opnd_lo, first, last):
                s, i = wsl
                whi = w_hi[:, s, i * P:(i + 1) * P]
                wlo = w_lo[:, s, i * P:(i + 1) * P]
                for w, o, f, e in ((whi, opnd_hi, first, False), (whi, opnd_lo, False, False),
                                   (wlo, opnd_hi, False, last)):
                    for hf in range(2):
                        ins = nc.tensor.matmul(out[:, hf, 0:HALF], w, o[:, hf * HALF:(hf + 1) * HALF],
                                               start=f, stop=e)
                return ins

            def project(l, name, chunks, opnd):
                n0, q0, g0 = AT[l, name]
                order = [4, 5, 6, 7, 0, 1, 2, 3]
                for c in range(chunks):
                    pe.wait_ge(lo_done, n0 + c + 1)
                    open_block(g0 + c)
                    for j, k in enumerate(order):
                        if c == 0:
                            pe.wait_ge(alo_done, opnd + j + 1)
                        ins = product(ps[:, (g0 + c) % 4], ((n0 + c) % SPLIT, k), a_hi[:, k, :], a_lo[:, k, :],
                                      j == 0, j == KB - 1)
                    ins.then_inc(mm_done, 1)

            def norm_sums(i):
                n0, q0, g0 = NORM_AT[i]
                open_block(g0)
                pe.wait_ge(ss_add, KB * (i + 1))
                for hf in range(2):
                    ins = nc.tensor.matmul(ps[:, g0 % 4, hf, 0:HALF], ones[:], ss[:, hf * HALF:(hf + 1) * HALF],
                                           start=True, stop=True)
                ins.then_inc(mm_done, 1)

            def unit(n0, q0, g0, opnd, l, it=0, first_unit=False):
                per = 2 * UNIT_CH
                perg = 2 * UNIT_BLOCKS
                for c, b, new_chunk, end, pieces in UNIT:
                    if new_chunk:
                        pe.wait_ge(lo_done, n0 + c + 1 + per * it)
                    if pieces[0][1] == 0:
                        open_block(g0 + b, it, perg)
                    down = c >= 2 * FB
                    for i, k in pieces:
                        if down and b == 2 * FB:
                            pe.wait_ge(alo_done, opnd + k + 1 + 2 * FB * it)
                        if not down and c == 0 and first_unit:
                            pe.wait_ge(alo_done, operand[l, "h2"] + k + 1)
                        hi, lo = (act_hi, act_lo) if down else (a_hi, a_lo)
                        ins = product(ps[:, (g0 + b) % 4], ((n0 + c) % SPLIT, i), hi[:, k, :], lo[:, k, :],
                                      k == 0, k == (FB if down else KB) - 1)
                    ins.then_inc(mm_done, 1)

            pe.wait_ge(ones_set, 1)
            for l in range(LAYERS):
                n0, q0, g0 = AT[l, "ada"]
                if l == 0:
                    pe.wait_ge(cs_ready, 1)
                    pe.wait_ge(consts_in, 16 * 14)
                c = 0
                for kind, grp, k in ADA_SEQ:
                    g = g0 + ADA_BLOCK[kind, grp]
                    if kind == "rows":
                        pe.wait_ge(lo_done, n0 + c + 1)
                        if k == 0:
                            open_block(g)
                        for w in (w_hi, w_lo):
                            for hf in range(2):
                                ins = nc.tensor.matmul(ps[:, g % 4, hf, :], cs4[:, k, :],
                                                       w[:, (n0 + c) % SPLIT, hf * 512:(hf + 1) * 512],
                                                       start=(k == 0 and w is w_hi), stop=(k == KB - 1 and w is w_lo))
                        c += 1
                    else:
                        pe.wait_ge(row_done, 6 * l + grp + 1)
                        open_block(g)
                        for j in range(KB):
                            ins = nc.tensor.transpose(ps[:, g % 4, 0, 4 * j:4 * j + 4],
                                                      mrow[0:4, grp % 2, j * P:(j + 1) * P], idn[0:4, 0:4])
                    ins.then_inc(mm_done, 1)
                norm_sums(2 * l)

                n0, q0, g0 = AT[l, "in"]
                for b, (kind, j, c) in enumerate(IN_SEQ):
                    if kind != "turn":
                        pe.wait_ge(lo_done, n0 + c + 1)
                    open_block(g0 + b)
                    if kind == "turn":
                        pe.wait_ge(vt_ready, 4 * l + j + 1)
                        for t in range(TT):
                            ins = nc.tensor.transpose(ps[:, (g0 + b) % 4, t // 4, (t % 4) * P:(t % 4 + 1) * P],
                                                      vT[:, j, t * P:(t + 1) * P], idn[:])
                    else:
                        for k in range(KB):
                            if c == 0:
                                pe.wait_ge(alo_done, operand[l, "h1"] + k + 1)
                            ins = product(ps[:, (g0 + b) % 4], ((n0 + c) % SPLIT, k), a_hi[:, k, :], a_lo[:, k, :],
                                          k == 0, k == KB - 1)
                    ins.then_inc(mm_done, 1)

                pe.wait_ge(blk_free, g0 + len(IN_SEQ))
                pe.wait_ge(kq_ready, 8 * (l + 1))
                pe.wait_ge(cache_in[l], 32)
                pe.wait_ge(vtok_ready, 4 * (l + 1))

                def scores(m):
                    if m >= 2 * NS:
                        return
                    h, t, k0, nk = STEPS[m // 2]
                    s = m % 2
                    if m >= 3:
                        pe.wait_ge(exp_done, 2 * l * NS + m - 2)
                    for c0 in range(0, nk, 512):
                        c1 = min(nk, c0 + 512)
                        ins = nc.tensor.matmul(S[:, m % 3, c0:c1], qT[QK * s:QK * (s + 1), h, t * P:(t + 1) * P],
                                               kT[QK * s:QK * (s + 1), h, k0 + c0:k0 + c1],
                                               start=True, stop=True)
                    ins.then_inc(scores_done, 1)

                def weigh_values(i):
                    h, t, k0, nk = STEPS[i]
                    pe.wait_ge(pt_ready, l * NS + i + 1)
                    for j in range(nk // P):
                        ins = nc.tensor.matmul(OT[:, i % 2, :], vtok[:, k0 // P + j, h * VH:(h + 1) * VH],
                                               pT[:, i % 2, j * P:(j + 1) * P], start=(j == 0), stop=(j == nk // P - 1))
                    ins.then_inc(pv_done, 1)

                for m in range(3):
                    scores(m)
                for i, (h, t, k0, nk) in enumerate(STEPS):
                    scores(2 * i + 3)
                    if i > 0:
                        weigh_values(i - 1)
                    scores(2 * i + 4)
                    pe.wait_ge(comb_done, l * NS + i + 1)
                    if i > 0:
                        pe.wait_ge(att_ready, l * NS + i)
                    for j in range(nk // P):
                        ins = nc.tensor.transpose(PT[:, j * P:(j + 1) * P], pr[:, i % 2, 0, j * P:(j + 1) * P], idn[:])
                    ins.then_inc(tr_done, 1)
                weigh_values(NS - 1)

                n0, q0, g0 = AT[l, "sub"]
                pe.wait_ge(att_ready, (l + 1) * NS)
                pe.wait_ge(pt_ready, (l + 1) * NS)
                pe.wait_ge(exp_done, 2 * (l + 1) * NS)
                for h in range(HEADS):
                    pe.wait_ge(att_sq, HEADS * l + h + 1)
                    for hf in range(2):
                        ins = nc.tensor.matmul(ps[:, (g0 + h) % 4, hf, 0:HALF], ones[:],
                                               sq[:, h % 2, hf * HALF:(hf + 1) * HALF], start=True, stop=True)
                    ins.then_inc(mm_done, 1)

                project(l, "out", OUT_CH, operand[l, "cat"])
                norm_sums(2 * l + 1)
                n0, q0, g0 = AT[l, "ffn"]
                if l % 2 == 0:
                    for u in range(2):
                        unit(n0 + u * UNIT_CH, q0 + u * len(UNIT), g0 + u * UNIT_BLOCKS,
                             operand[l, "act"] + u * FB, l, first_unit=(u == 0))
                else:
                    rn, rq, rg = AT[l, "route"]
                    open_block(rg)
                    for k in range(KB):
                        pe.wait_ge(h_done, KB * 3 + k + 1)
                        for hf in range(2):
                            ins = nc.tensor.matmul(ps[0:EXPERTS, rg % 4, hf, 0:HALF], wr[:, k, :],
                                                   hraw[:, k, hf * HALF:(hf + 1) * HALF],
                                                   start=(k == 0), stop=(k == KB - 1))
                    ins.then_inc(mm_done, 1)
                    for b in range(1, 3 + TT):
                        open_block(rg + b)
                        if b == 2:
                            pe.wait_ge(lgT_ready, 1)
                            for t in range(TT):
                                ins = nc.tensor.transpose(ps[:, (rg + b) % 4, 0, t * EXPERTS:(t + 1) * EXPERTS],
                                                          lgT[:, t * P:(t + 1) * P], idn[0:EXPERTS, 0:EXPERTS])
                        elif b == 2 + TT:
                            pe.wait_ge(mask_ready, 1)
                            flat = mask[:].rearrange("p t e -> p (t e)")
                            nc.tensor.matmul(ps[:, (rg + b) % 4, 0, 0:TT * EXPERTS], bel[:], flat, start=True, stop=True)
                            ins = nc.tensor.matmul(ps[:, (rg + b) % 4, 1, 0:TT * EXPERTS], ones[:], flat,
                                                   start=True, stop=True)
                        else:
                            t = 0 if b == 1 else b - 2
                            for k in range(KB):
                                ins = nc.tensor.transpose(ps[:, (rg + b) % 4, k // 4, (k % 4) * P:(k % 4 + 1) * P],
                                                          hraw[:, k, t * P:(t + 1) * P], idn[:])
                        ins.then_inc(mm_done, 1)

                    def scatter(g, d, u, j=0, per=None):
                        for st_ in range(ST):
                            for part in (ey_hi, ey_lo):
                                for hf in range(2):
                                    ins = nc.tensor.matmul(ps[:, g % 4, hf, 0:HALF], part[:, st_, d * P:(d + 1) * P],
                                                           selT[:, u, st_, hf * HALF:(hf + 1) * HALF],
                                                           start=(st_ == 0 and part is ey_hi),
                                                           stop=(st_ == ST - 1 and part is ey_lo))
                        ins.then_inc(mm_done, 1)

                    def expert(u, it, now):
                        nn, qq, gg = n0 + u * UNIT_CH, q0 + u * len(EXPERT), g0 + u * EXPERT_BLOCKS
                        oo = operand[l, "act"] + u * EXPERT_OPERANDS
                        pern, perg, pero = 2 * UNIT_CH, 2 * EXPERT_BLOCKS, 2 * EXPERT_OPERANDS
                        pe.wait_ge(sel_ready, u + 1 + 2 * now)
                        for kind, i, b, c in EXPERT:
                            if c is not None:
                                pe.wait_ge(lo_done, nn + c + 1 + pern * now)
                            if kind == "down" and i == 0:
                                open_block(gg + 34, now, perg)
                                open_block(gg + 35, now, perg)
                            elif kind != "down":
                                open_block(gg + b, now, perg)
                            slot = (gg + b) % 4
                            if kind == "gather":
                                for k in range(4):
                                    d = 4 * i + k
                                    out = ps[:, slot, k // 2, (k % 2) * CAP:(k % 2 + 1) * CAP]
                                    for t in range(TT):
                                        for part in (ht_hi, ht_lo):
                                            ins = nc.tensor.matmul(out, part[:, t, d * P:(d + 1) * P], sel[:, t, :],
                                                                   start=(t == 0 and part is ht_hi),
                                                                   stop=(t == TT - 1 and part is ht_lo))
                            elif kind == "turn":
                                for t in range(TT):
                                    ins = nc.tensor.transpose(
                                        ps[:, slot, t // 4, (t % 4) * P:(t % 4 + 1) * P],
                                        sel[:, t, i * P:(i + 1) * P].bitcast(F32), idn[:])
                                for t in range(TT):
                                    ins = nc.tensor.matmul(ps[:, slot, 1, 256:258], sel[:, t, i * P:(i + 1) * P],
                                                           grouped[:, t, 2 * it + u, :],
                                                           start=(t == 0), stop=(t == TT - 1))
                            elif kind == "scatter":
                                if i == 0:
                                    pe.wait_ge(alo_done, oo + pero * now)
                                scatter(gg + b, i, 1 - u)
                                continue
                            elif kind == "gu":
                                if i == 0:
                                    pe.wait_ge(alo_done, oo + 2 + pero * now)
                                for k in range(KB):
                                    whi = w_hi[:, (nn + c) % SPLIT, k * P:(k + 1) * P]
                                    wlo = w_lo[:, (nn + c) % SPLIT, k * P:(k + 1) * P]
                                    for w, o in ((whi, hg_hi), (whi, hg_lo), (wlo, hg_hi)):
                                        ins = nc.tensor.matmul(ps[:, slot, 0, 0:CAP], w, o[:, k, :],
                                                               start=(k == 0 and o is hg_hi and w is whi),
                                                               stop=(k == KB - 1 and w is wlo))
                            else:
                                pe.wait_ge(alo_done, oo + 2 + i + 1 + pero * now)
                                for st_ in range(ST):
                                    for a, w in ((ea_hi, w_hi), (ea_lo, w_hi), (ea_hi, w_lo)):
                                        for hf in range(2):
                                            ins = nc.tensor.matmul(
                                                ps[:, (gg + 34 + st_) % 4, hf, :], a[:, i, st_ * P:(st_ + 1) * P],
                                                w[:, (nn + c) % SPLIT, hf * 512:(hf + 1) * 512],
                                                start=(i == 0 and a is ea_hi and w is w_hi),
                                                stop=(i == FB - 1 and w is w_lo))
                            ins.then_inc(mm_done, 1)

                    def experts(first):
                        with pe.Fori(0, EXPERTS // 2) as it:
                            for u in range(2):
                                expert(u, it, first + it)

                    pe.wait_ge(cleared, 4)
                    pe.wait_ge(gates_ready, 1)
                    experts(0)
                    pe.wait_ge(most_ready, 1)
                    with pe.If(pe.value_load(most_i[0:1, 0:1], min_val=0, max_val=T) > CAP):
                        with pe.Fori(1, ROUNDS) as r:
                            experts(EXPERTS // 2 * r)
                    with pe.Else():
                        pe.wait_ge(mm_done, q0 + EXPERTS * len(EXPERT))
                        pe.sem_inc(mm_done, (ROUNDS - 1) * EXPERTS * len(EXPERT))
                    ln, lq_, lg_ = AT[l, "last"]
                    pe.wait_ge(alo_done, operand[l, "act"] + ROUNDS * EXPERTS * EXPERT_OPERANDS)
                    for d in range(KB):
                        open_block(lg_ + d)
                        scatter(lg_ + d, d, 1)
            norm_sums(4)

        @block.scalar
        def _(act):
            def split_hi(n, q, it=0, pern=0, perq=0):
                s = n % SPLIT
                act.wait_ge(raw_full[n % RAW], 16 * (n // RAW + 1) + 16 * (pern // RAW) * it)
                if q > 0:
                    act.wait_ge(mm_done, q + perq * it)
                nc.scalar.activation(w_hi[:, s, :], raw[:, n % RAW, :], ACT.Copy).then_inc(hi_done, 1)

            def square(i, kb, dst_sem=sq_done):
                m = KB * i + kb
                if i == 0:
                    act.wait_ge(x_in, 16)
                else:
                    act.wait_ge(x_new, KB * (i - 1) + kb + 1)
                if m >= 2:
                    act.wait_ge(ss_add, m - 1)
                nc.scalar.activation(sq[:, m % 2, :], x[:, kb, :], ACT.Square).then_inc(dst_sem, 1)

            def root(i, width):
                n0, q0, g0 = NORM_AT[i]
                act.wait_ge(mm_done, q0 + 1)
                nc.scalar.activation(rstd[:].rearrange("p (a b) -> p a b", a=2), ps[:, g0 % 4, :, 0:HALF], ACT.Sqrt,
                                     bias=eps[:, 0:1], scale=1.0 / width).then_inc(root_done, 1)

            def modulate(i, opnd):
                l, which = i // 2, i % 2
                if which == 0:
                    act.wait_ge(mod_ready, l + 1)
                for kb in range(KB):
                    act.wait_ge(xn_done, KB * i + kb + 1)
                    if kb >= 2 and i != 3:
                        act.wait_ge(alo_done, opnd + kb - 1)
                    dst = hraw[:, kb, :] if i == 3 else tt[:, kb % 2, :]
                    for toks, c in TOKENS_OF:
                        ins = nc.scalar.activation(dst[:, toks], st[:, kb % 2, toks], ACT.Identity,
                                                   bias=mod[:, (3 * which) * KB + kb, c:c + 1],
                                                   scale=gain[:, which, kb, c:c + 1])
                    ins.then_inc(h_done, 1)
                    if i == 3:
                        continue
                    act.wait_ge(h_done, KB * i + kb + 1)
                    nc.scalar.activation(a_hi[:, kb, :], tt[:, kb % 2, :], ACT.Copy).then_inc(ahi_done, 1)

            def unit(n0, q0, g0, opnd, f0, it=0):
                pern, perq = 2 * UNIT_CH, 2 * len(UNIT)
                for j, (c, b, new_chunk, end, pieces) in enumerate(UNIT):
                    if new_chunk:
                        split_hi(n0 + c + 2, q0 + j, it, pern, perq)
                    if not end or b >= 2 * FB:
                        continue
                    f = b // 2
                    if b % 2 == 0:
                        act.wait_ge(mm_done, q0 + j + 1 + perq * it)
                        if f0 + f >= 2:
                            act.wait_ge(t_done, f0 + f - 1 + 2 * FB * it)
                        nc.scalar.activation(st[:, f % 2, :].rearrange("p (a b) -> p a b", a=2),
                                             ps[:, (g0 + b) % 4, :, 0:HALF], ACT.Silu).then_inc(silu_done, 1)
                    else:
                        act.wait_ge(t_done, f0 + f + 1 + 2 * FB * it)
                        nc.scalar.activation(act_hi[:, f, :], tt[:, f % 2, :], ACT.Copy).then_inc(ahi_done, 1)

            split_hi(0, 0)
            split_hi(1, 0)
            act.wait_ge(consts_in, 16 * 14)
            nc.scalar.activation(cs[:], cond[:], ACT.Silu).then_inc(silu_c, 1)
            act.wait_ge(silu_c, 1)
            nc.scalar.activation(cs4[:, :, 0:2], cs[:], ACT.Copy).then_inc(cs_hi, 1)
            for l in range(LAYERS):
                n0, q0, g0 = AT[l, "ada"]
                c = 0
                for b, (kind, grp, k) in enumerate(ADA_SEQ):
                    if kind == "turn":
                        continue
                    split_hi(n0 + c + 2, q0 + b)
                    if l == 0 and 8 <= c < 8 + KB:
                        square(0, c - 8)
                    c += 1
                    if k == KB - 1:
                        act.wait_ge(mm_done, q0 + b + 1)
                        if grp >= 2:
                            act.wait_ge(blk_free, g0 + ADA_BLOCK["turn", grp - 2] + 1)
                        nc.scalar.activation(mrow[0:4, grp % 2, :].rearrange("p (a b) -> p a b", a=2),
                                             ps[0:4, (g0 + ADA_BLOCK["rows", grp]) % 4, :, :], ACT.Copy)\
                            .then_inc(row_done, 1)
                if l == 0:
                    act.wait_ge(ones_set, 2)
                root(2 * l, D)
                modulate(2 * l, operand[l, "h1"])

                n0, q0, g0 = AT[l, "in"]
                for b, (kind, j, c) in enumerate(IN_SEQ):
                    if kind == "turn":
                        continue
                    split_hi(n0 + c + 2, q0 + b)
                    src = ps[:, (g0 + b) % 4, :, 0:HALF]
                    if kind in ("k", "q", "v", "gc"):
                        act.wait_ge(mm_done, q0 + b + 1)
                        buf = {"k": kT, "q": qT, "v": vT, "gc": gcx}[kind]
                        if kind == "v" and j == 0 and l:
                            act.wait_ge(tr_done, l * NS)
                        if kind == "k" and j == 0 and l:
                            act.wait_ge(k_out, 16 * l)
                        nc.scalar.activation(buf[:, j, 0:T].rearrange("p (a b) -> p a b", a=2), src, ACT.Copy,
                                             scale=QK ** -0.5 if kind == "q" else 1.0)\
                            .then_inc({"k": kq_raw, "q": kq_raw, "v": vt_ready, "gc": gcx_ready}[kind], 1)

                act.wait_ge(lam_sum, l + 1)
                nc.scalar.activation(lexp[:], lsum[:], ACT.Exp).then_inc(lam_exp, 1)
                act.wait_ge(v_out, 16 * (l + 1))
                act.wait_ge(mm_done, AT[l, "sub"][1])

                def exponentials(m):
                    i, s = m // 2, m % 2
                    nk = STEPS[i][3]
                    act.wait_ge(max_done, 2 * l * NS + m + 1)
                    if i >= 2:
                        act.wait_ge(tr_done, l * NS + i - 1)
                    nc.scalar.activation(pr[:, i % 2, s, 0:nk], S[:, m % 3, 0:nk], ACT.Exp,
                                         bias=nbias[:, m % 4:m % 4 + 1], accum_out=rsum[:, i % 2, s:s + 1])\
                        .then_inc(exp_done, 1)

                def take_output(i):
                    h, t, _, _ = STEPS[i]
                    act.wait_ge(pv_done, l * NS + i + 1)
                    nc.scalar.activation(att[:, h, t * P:(t + 1) * P], OT[:, i % 2, :], ACT.Copy).then_inc(att_ready, 1)

                def take_transposed(i):
                    nk = STEPS[i][3]
                    act.wait_ge(tr_done, l * NS + i + 1)
                    if i >= 2:
                        act.wait_ge(pv_done, l * NS + i - 1)
                    nc.scalar.activation(pT[:, i % 2, 0:nk], PT[:, 0:nk], ACT.Copy).then_inc(pt_ready, 1)

                for i in range(NS):
                    exponentials(2 * i)
                    if i >= 1:
                        take_transposed(i - 1)
                    exponentials(2 * i + 1)
                    if i >= 1:
                        take_output(i - 1)
                    if i % 5 == 0:
                        j = i // 5
                        act.wait_ge(conv_ready, 4 * l + j + 1)
                        nc.scalar.activation(a_hi[:, 4 + j, :], gcx[:, j, :], ACT.Copy).then_inc(ahi_done, 1)
                take_transposed(NS - 1)
                take_output(NS - 1)
                n0, q0, g0 = AT[l, "sub"]
                act.wait_ge(att_ready, (l + 1) * NS)
                for h in range(HEADS):
                    if h >= 2:
                        act.wait_ge(mm_done, q0 + h - 1)
                    nc.scalar.activation(sq[:, h % 2, :], att[:, h, :], ACT.Square).then_inc(att_sq, 1)
                for h in range(HEADS):
                    act.wait_ge(mm_done, q0 + h + 1)
                    nc.scalar.activation(st[:, h % 2, :].rearrange("p (a b) -> p a b", a=2) if h < 2 else
                                         tt[:, h % 2, :].rearrange("p (a b) -> p a b", a=2),
                                         ps[:, (g0 + h) % 4, :, 0:HALF], ACT.Sqrt, bias=eps[:, 0:1],
                                         scale=1.0 / VH).then_inc(att_root, 1)
                for h in range(HEADS):
                    act.wait_ge(att_norm, HEADS * l + h + 1)
                    nc.scalar.activation(a_hi[:, h, :], att[:, h, :], ACT.Copy).then_inc(ahi_done, 1)

                n0, q0, g0 = AT[l, "out"]
                for c in range(OUT_CH):
                    split_hi(n0 + c + 2, q0 + c)
                    square(2 * l + 1, c)
                root(2 * l + 1, D)
                modulate(2 * l + 1, operand[l, "h2"])

                n0, q0, g0 = AT[l, "ffn"]
                if l % 2 == 0:
                    for u in range(2):
                        unit(n0 + u * UNIT_CH, q0 + u * len(UNIT), g0 + u * UNIT_BLOCKS,
                             operand[l, "act"] + u * FB, u * FB)
                else:
                    rn, rq, rg = AT[l, "route"]
                    act.wait_ge(mm_done, rq + 1)
                    nc.scalar.activation(lgT[:].rearrange("p (a b) -> p a b", a=2), ps[0:EXPERTS, rg % 4, :, 0:HALF],
                                         ACT.Copy).then_inc(lgT_ready, 1)
                    for b in (1, 3):
                        act.wait_ge(mm_done, rq + b + 1)
                        nc.scalar.activation(ht_hi[:, 0 if b == 1 else 1, :].rearrange("p (a b) -> p a b", a=2),
                                             ps[:, (rg + b) % 4], ACT.Copy).then_inc(ahi_done, 1)
                    act.wait_ge(dv_ready, 1)
                    nc.scalar.activation(ev[:], dv[:], ACT.Exp).then_inc(ev_ready, 1)
                    for b in range(4, 2 + TT):
                        act.wait_ge(mm_done, rq + b + 1)
                        nc.scalar.activation(ht_hi[:, b - 2, :].rearrange("p (a b) -> p a b", a=2),
                                             ps[:, (rg + b) % 4], ACT.Copy).then_inc(ahi_done, 1)
                    act.wait_ge(gates_set, 1)
                    nc.scalar.activation(grouped[:, :, :, 0], gates[:], ACT.Copy).then_inc(gates_hi, 1)

                    def expert(u, it, now):
                        nn, qq, gg = n0 + u * UNIT_CH, q0 + u * len(EXPERT), g0 + u * EXPERT_BLOCKS
                        pern, perq = 2 * UNIT_CH, 2 * len(EXPERT)
                        ff = FC0 + u * FB
                        for j, (kind, i, b, c) in enumerate(EXPERT):
                            if c is not None:
                                split_hi(nn + c + 2, qq + j, now, pern, perq)
                            slot = (gg + b) % 4
                            if kind == "gather":
                                act.wait_ge(mm_done, qq + j + 1 + perq * now)
                                nc.scalar.activation(hg_hi[:, 4 * i:4 * i + 4, :].rearrange("p (a k) c -> p a (k c)", a=2),
                                                     ps[:, slot], ACT.Copy).then_inc(ahi_done, 1)
                            elif kind == "turn":
                                act.wait_ge(mm_done, qq + j + 1 + perq * now)
                                nc.scalar.activation(selT[:, u, i, 0:512], ps[:, slot, 0, :], ACT.Copy)
                                nc.scalar.activation(selT[:, u, i, 512:T], ps[:, slot, 1, 0:T - 512], ACT.Copy)
                                nc.scalar.activation(gsl[:, u, i, :], ps[:, slot, 1, 256:258], ACT.Copy)\
                                    .then_inc(selT_ready, 1)
                            elif kind == "gu" and i % 2 == 0:
                                f = i // 2
                                act.wait_ge(mm_done, qq + j + 1 + perq * now)
                                act.wait_ge(t_done, ff + f - 1 + 2 * FB * now)
                                nc.scalar.activation(st[:, f % 2, 0:CAP], ps[:, slot, 0, 0:CAP], ACT.Silu)\
                                    .then_inc(silu_done, 1)
                            elif kind == "gu":
                                f = i // 2
                                act.wait_ge(t_done, ff + f + 1 + 2 * FB * now)
                                nc.scalar.activation(ea_hi[:, f, :], tt[:, f % 2, 0:CAP], ACT.Copy).then_inc(ahi_done, 1)
                            elif kind == "down" and i == FB - 1:
                                act.wait_ge(mm_done, qq + j + 1 + perq * now)
                                act.wait_ge(gslot_ready, u + 1 + 2 * now)
                                for st_ in range(ST):
                                    nc.scalar.activation(ey_hi[:, st_, :].rearrange("p (a b) -> p a b", a=2),
                                                         ps[:, (gg + 34 + st_) % 4], ACT.Copy,
                                                         scale=gslot[:, u, st_:st_ + 1]).then_inc(ahi_done, 1)

                    def experts(first):
                        with act.Fori(0, EXPERTS // 2) as it:
                            for u in range(2):
                                expert(u, it, first + it)

                    act.wait_ge(cleared, 4)
                    experts(0)
                    act.wait_ge(most_ready, 1)
                    with act.If(act.value_load(most_i[0:1, 0:1], min_val=0, max_val=T) > CAP):
                        with act.Fori(1, ROUNDS) as r:
                            experts(EXPERTS // 2 * r)
                for kb in range(KB):
                    square(2 * l + 2, kb)
            root(4, D)

        @block.gpsimd
        def _(pool):
            nc.gpsimd.memset(ones[:], 1.0).then_inc(ones_set, 1)
            nc.gpsimd.memset(eps[:], EPS).then_inc(ones_set, 1)
            for i in range(5):
                if i == 4:
                    pool.wait_ge(ahi_done, operand[1, "h2"] + TT)
                    pool.wait_ge(mask_ready, 1)
                    for buf in (ey_hi, ey_lo, selT[:, 1], gsl):
                        nc.gpsimd.memset(buf[:].bitcast(F32) if buf is not gsl else gsl[:], 0.0).then_inc(cleared, 1)
                for kb in range(KB):
                    m = KB * i + kb
                    pool.wait_ge(sq_done, m + 1)
                    if kb == 0:
                        if i:
                            pool.wait_ge(mm_done, NORM_AT[i - 1][1] + 1)
                        nc.gpsimd.tensor_copy(ss[:], sq[:, m % 2, :]).then_inc(ss_add, 1)
                    else:
                        pool.wait_ge(ss_add, m)
                        nc.gpsimd.tensor_tensor(ss[:], ss[:], sq[:, m % 2, :], ALU.add).then_inc(ss_add, 1)

        @block.vector
        def _(dve):
            chain = [0]

            def link(ins):
                chain[0] += 1
                ins.then_inc(dve_step, 1)
                dve.wait_ge(dve_step, chain[0])

            def split_lo(n, it=0, pern=0):
                s = n % SPLIT
                dve.wait_ge(hi_done, n + 1 + pern * it)
                nc.vector.tensor_tensor(w_lo[:, s, :], raw[:, n % RAW, :], w_hi[:, s, :].bitcast(F32), ALU.subtract)\
                    .then_inc(lo_done, 1)

            def lo_part(dst, full, hi, done):
                dve.wait_ge(ahi_done, done)
                nc.vector.tensor_tensor(dst, full, hi.bitcast(F32), ALU.subtract).then_inc(alo_done, 1)

            def normalise(i, width_gain=None):
                dve.wait_ge(root_done, i + 1)
                link(nc.vector.reciprocal(rstd[:], rstd[:]))
                nc.vector.engine_nop().then_inc(blk_free, 1) if False else None

            def norm(i, opnd):
                n0, q0, g0 = NORM_AT[i]
                dve.wait_ge(root_done, i + 1)
                ins = nc.vector.reciprocal(rstd[:], rstd[:])
                ins.then_inc(blk_free, 1)
                dve.wait_ge(blk_free, g0 + 1)
                for kb in range(KB):
                    if kb >= 2:
                        dve.wait_ge(h_done, KB * i + kb - 1)
                    nc.vector.tensor_tensor(st[:, kb % 2, :], x[:, kb, :], rstd[:], ALU.mult).then_inc(xn_done, 1)
                    if kb and i != 3:
                        lo_part(a_lo[:, kb - 1, :], tt[:, (kb - 1) % 2, :], a_hi[:, kb - 1, :], opnd + kb)
                if i != 3:
                    lo_part(a_lo[:, KB - 1, :], tt[:, (KB - 1) % 2, :], a_hi[:, KB - 1, :], opnd + KB)

            def residual(g, gate, d, x_sem=None, it=0, perg=0):
                for n, (hf, cols, toks, c) in enumerate(SEGMENTS):
                    ins = nc.vector.scalar_tensor_tensor(x[:, d, toks], ps[:, g % 4, hf, cols],
                                                         mod[:, gate * KB + d, c:c + 1], x[:, d, toks],
                                                         op0=ALU.mult, op1=ALU.add)
                ins.then_inc(blk_free, 1)
                if x_sem is not None:
                    dve.wait_ge(blk_free, g + 1)
                    dve.sem_inc(x_sem, 1)

            def unit(n0, q0, g0, opnd, f0, final, it=0):
                pern, perq, perg, perf = 2 * UNIT_CH, 2 * len(UNIT), 2 * UNIT_BLOCKS, 2 * FB
                for j, (c, b, new_chunk, end, pieces) in enumerate(UNIT):
                    if new_chunk:
                        split_lo(n0 + c + 2, it, pern)
                    if not end:
                        continue
                    if b < 2 * FB:
                        f = b // 2
                        if b % 2 == 0:
                            continue
                        if f:
                            lo_part(act_lo[:, f - 1, :], tt[:, (f - 1) % 2, :], act_hi[:, f - 1, :],
                                    opnd + f + perf * it)
                        dve.wait_ge(silu_done, f0 + f + 1 + perf * it)
                        dve.wait_ge(mm_done, q0 + j + 1 + perq * it)
                        up = ps[:, (g0 + b) % 4, :, 0:HALF]
                        s3 = st[:, f % 2, :].rearrange("p (a b) -> p a b", a=2)
                        t3 = tt[:, f % 2, :].rearrange("p (a b) -> p a b", a=2)
                        nc.vector.tensor_tensor(t3, s3, up, ALU.mult).then_inc(t_done, 1)
                        dve.wait_ge(t_done, f0 + f + 1)
                        dve.sem_inc(blk_free, 2)
                    else:
                        d = b - 2 * FB
                        dve.wait_ge(mm_done, q0 + j + 1 + perq * it)
                        residual(g0 + b, 5, d, x_new if final else None)
                    if b == 2 * FB - 1:
                        lo_part(act_lo[:, FB - 1, :], tt[:, (FB - 1) % 2, :], act_hi[:, FB - 1, :],
                                opnd + FB + perf * it)

            dve.wait_ge(consts_in, 16 * 14)
            split_lo(0)
            split_lo(1)
            dve.wait_ge(silu_c, 1)
            dve.wait_ge(cs_hi, 1)
            nc.vector.memset(cs4[:, :, 4:P].bitcast(F32), 0.0)
            nc.vector.tensor_tensor(cs4[:, :, 2:4], cs[:], cs4[:, :, 0:2].bitcast(F32), ALU.subtract)\
                .then_inc(cs_ready, 1)
            for l in range(LAYERS):
                n0, q0, g0 = AT[l, "ada"]
                c = 0
                for b, (kind, grp, k) in enumerate(ADA_SEQ):
                    if kind == "rows":
                        split_lo(n0 + c + 2)
                        c += 1
                        if k == KB - 1:
                            dve.wait_ge(row_done, 6 * l + grp + 1)
                            dve.sem_inc(blk_free, 1)
                    else:
                        dve.wait_ge(mm_done, q0 + b + 1)
                        g = g0 + ADA_BLOCK[kind, grp]
                        mine = mod[:, grp * KB:(grp + 1) * KB, :]
                        col = ps[:, g % 4, 0, 0:4 * KB].rearrange("p (c j) -> p c j", j=4)
                        link(nc.vector.tensor_tensor(
                            mine, col[:, :, 0:2],
                            bada[:, l, grp * KB:(grp + 1) * KB].unsqueeze(2).broadcast_to([P, KB, 2]), ALU.add))
                        nc.vector.tensor_tensor(mine, mine, col[:, :, 2:4], ALU.add).then_inc(blk_free, 1)
                    if b == 4:
                        link(nc.vector.tensor_tensor(lp[:, 0:QK], lq[:, l, 0:QK], lq[:, l, QK:2 * QK], ALU.mult))
                        link(nc.vector.tensor_tensor(lp[:, QK:], lq[:, l, 2 * QK:3 * QK], lq[:, l, 3 * QK:], ALU.mult))
                        nc.vector.tensor_reduce(lsum[:], lp[:].rearrange("p (a b) -> p a b", a=2), AX, ALU.add)\
                            .then_inc(lam_sum, 1)
                        link(nc.vector.tensor_scalar(subgs[:, l:l + 1], subg[:, l:l + 1], 1.0 - LAM_INIT[l], None,
                                                     ALU.mult))
                dve.wait_ge(blk_free, g0 + len(ADA_BLOCK))
                for w, g in ((0, gmix), (1, gffn)):
                    ins = nc.vector.scalar_tensor_tensor(gain[:, w], mod[:, (3 * w + 1) * KB:(3 * w + 2) * KB, :], 1.0,
                                                         g[:, l, :].unsqueeze(2).broadcast_to([P, KB, 2]),
                                                         op0=ALU.add, op1=ALU.mult)
                ins.then_inc(mod_ready, 1)
                norm(2 * l, operand[l, "h1"])

                n0, q0, g0 = AT[l, "in"]
                lat = slice(CTX, T)
                swp, cv = tt[:, 1, 0:LAT], tt[:, 0, :]
                for b, (kind, j, c) in enumerate(IN_SEQ):
                    if kind == "turn":
                        dve.wait_ge(mm_done, q0 + b + 1)
                        for t0, t1, bank in ((0, 4, 0), (4, TT, 1)):
                            ins = nc.vector.tensor_copy(vtok[:, t0:t1, j * VH:(j + 1) * VH],
                                                        ps[:, (g0 + b) % 4, bank, 0:(t1 - t0) * P]
                                                        .rearrange("p (t e) -> p t e", e=VH))
                        link(ins)
                        dve.sem_inc(blk_free, 1)
                        dve.sem_inc(vtok_ready, 1)
                        continue
                    split_lo(n0 + c + 2)
                    src = ps[:, (g0 + b) % 4, :, 0:HALF]
                    if kind in ("k", "q"):
                        buf = kT if kind == "k" else qT
                        dve.wait_ge(kq_raw, 8 * l + c + 1)
                        dve.sem_inc(blk_free, 1)
                        link(nc.vector.stream_shuffle(swp, buf[:, j, lat], SWAP))
                        link(nc.vector.tensor_tensor(swp, swp, sin_s[:], ALU.mult))
                        link(nc.vector.tensor_tensor(buf[:, j, lat], buf[:, j, lat], cos_s[:], ALU.mult))
                        nc.vector.tensor_tensor(buf[:, j, lat], buf[:, j, lat], swp, ALU.add).then_inc(kq_ready, 1)
                        dve.wait_ge(kq_ready, 8 * l + c + 1)
                    elif kind == "v":
                        dve.wait_ge(vt_ready, 4 * l + j + 1)
                        dve.sem_inc(blk_free, 1)
                    elif kind == "gc":
                        dve.wait_ge(gcx_ready, 4 * l + j + 1)
                        dve.sem_inc(blk_free, 1)
                    elif kind == "xin":
                        dve.wait_ge(mm_done, q0 + b + 1)
                        g3 = gcx[:, j, :].rearrange("p (a b) -> p a b", a=2)
                        nc.vector.tensor_tensor(g3, g3, src, ALU.mult).then_inc(blk_free, 1)
                    else:
                        dve.wait_ge(blk_free, g0 + b)
                        link(nc.vector.tensor_scalar(cv, gcx[:, j, :], convw[:, l, 1, j:j + 1], None, ALU.mult))
                        for lo, hi in ((0, CTX), (CTX, T)):
                            link(nc.vector.scalar_tensor_tensor(cv[:, lo + 1:hi], gcx[:, j, lo:hi - 1],
                                                                convw[:, l, 0, j:j + 1], cv[:, lo + 1:hi],
                                                                op0=ALU.mult, op1=ALU.add))
                            link(nc.vector.scalar_tensor_tensor(cv[:, lo:hi - 1], gcx[:, j, lo + 1:hi],
                                                                convw[:, l, 2, j:j + 1], cv[:, lo:hi - 1],
                                                                op0=ALU.mult, op1=ALU.add))
                        dve.wait_ge(mm_done, q0 + b + 1)
                        link(nc.vector.tensor_tensor(gcx[:, j, :].rearrange("p (a b) -> p a b", a=2),
                                                     cv.rearrange("p (a b) -> p a b", a=2), src, ALU.mult))
                        dve.sem_inc(blk_free, 1)
                        dve.sem_inc(conv_ready, 1)

                dve.wait_ge(lam_exp, l + 1)
                link(nc.vector.tensor_tensor(nlam[:], lexp[:, 1:2], lexp[:, 0:1], ALU.subtract))
                link(nc.vector.tensor_scalar(nlam[:], nlam[:], LAM_INIT[l], None, ALU.subtract))

                def row_max(m):
                    if m >= 2 * NS:
                        return
                    dve.wait_ge(scores_done, 2 * l * NS + m + 1)
                    nc.vector.tensor_reduce(nbias[:, m % 4:m % 4 + 1], S[:, m % 3, 0:STEPS[m // 2][3]], AX, ALU.max,
                                            negate=True).then_inc(max_done, 1)

                for m in range(3):
                    row_max(m)
                for i, (h, t, k0, nk) in enumerate(STEPS):
                    b = i % 2
                    dve.wait_ge(exp_done, 2 * (l * NS + i + 1))
                    link(nc.vector.reciprocal(rinv[:, b, :], rsum[:, b, :]))
                    link(nc.vector.tensor_scalar(pr[:, b, 1, 0:nk], pr[:, b, 1, 0:nk], rinv[:, b, 1:2], nlam[:, 0:1],
                                                 ALU.mult, ALU.mult))
                    nc.vector.scalar_tensor_tensor(pr[:, b, 0, 0:nk], pr[:, b, 0, 0:nk], rinv[:, b, 0:1],
                                                   pr[:, b, 1, 0:nk], op0=ALU.mult, op1=ALU.add)\
                        .then_inc(comb_done, 1)
                    row_max(2 * i + 3)
                    row_max(2 * i + 4)
                    if i % 5 == 0:
                        j = i // 5
                        lo_part(a_lo[:, 4 + j, :], gcx[:, j, :], a_hi[:, 4 + j, :], operand[l, "cat"] + j + 1)
                sn, sq0, sg = AT[l, "sub"]
                for h in range(HEADS):
                    buf = (st if h < 2 else tt)[:, h % 2, :]
                    dve.wait_ge(att_root, HEADS * l + h + 1)
                    link(nc.vector.reciprocal(buf, buf))
                    dve.sem_inc(blk_free, 1)
                    nc.vector.scalar_tensor_tensor(att[:, h, :], att[:, h, :], subgs[:, l:l + 1], buf,
                                                   op0=ALU.mult, op1=ALU.mult).then_inc(att_norm, 1)
                    if h:
                        lo_part(a_lo[:, h - 1, :], att[:, h - 1, :], a_hi[:, h - 1, :], operand[l, "cat"] + 4 + h)
                lo_part(a_lo[:, HEADS - 1, :], att[:, HEADS - 1, :], a_hi[:, HEADS - 1, :],
                        operand[l, "cat"] + 4 + HEADS)

                n0, q0, g0 = AT[l, "out"]
                for c in range(OUT_CH):
                    split_lo(n0 + c + 2)
                    dve.wait_ge(mm_done, q0 + c + 1)
                    residual(g0 + c, 2, c, x_new)
                norm(2 * l + 1, operand[l, "h2"])

                n0, q0, g0 = AT[l, "ffn"]
                if l % 2 == 0:
                    for u in range(2):
                        unit(n0 + u * UNIT_CH, q0 + u * len(UNIT), g0 + u * UNIT_BLOCKS,
                             operand[l, "act"] + u * FB, u * FB, u == 1)
                else:
                    rn, rq, rg = AT[l, "route"]

                    def token_lo(b):
                        t = 0 if b == 1 else b - 2
                        dve.wait_ge(ahi_done, operand[l, "h2"] + t + 1)
                        nc.vector.tensor_tensor(ht_lo[:, t, :].rearrange("p (a b) -> p a b", a=2), ps[:, (rg + b) % 4],
                                                ht_hi[:, t, :].bitcast(F32).rearrange("p (a b) -> p a b", a=2),
                                                ALU.subtract).then_inc(alo_done, 1)
                        dve.wait_ge(alo_done, operand[l, "h2"] + t + 1)
                        dve.sem_inc(blk_free, 1)

                    dve.wait_ge(lgT_ready, 1)
                    dve.sem_inc(blk_free, 1)
                    token_lo(1)
                    dve.wait_ge(mm_done, rq + 3)
                    link(nc.vector.tensor_copy(logits[:].rearrange("p t e -> p (t e)"),
                                               ps[:, (rg + 2) % 4, 0, 0:TT * EXPERTS]))
                    dve.sem_inc(blk_free, 1)
                    for t in range(TT):
                        link(nc.vector.max(tv[:, t, :], logits[:, t, :]))
                        link(nc.vector.max_index(ti[:, t, :], tv[:, t, :], logits[:, t, :]))
                    link(nc.vector.tensor_copy(tf[:], ti[:]))
                    link(nc.vector.tensor_tensor(dv[:], tv[:, :, 1], tv[:, :, 0], ALU.subtract))
                    dve.sem_inc(dv_ready, 1)
                    token_lo(3)
                    dve.wait_ge(ev_ready, 1)
                    link(nc.vector.tensor_scalar(g1[:], ev[:], 1.0, None, ALU.add))
                    link(nc.vector.reciprocal(g1[:], g1[:]))
                    link(nc.vector.tensor_tensor(g2[:], ev[:], g1[:], ALU.mult))
                    for t in range(TT):
                        link(nc.vector.tensor_scalar(oh[:, 0, :], iot[:, 0:EXPERTS], tf[:, t, 0:1], g1[:, t:t + 1],
                                                     ALU.is_equal, ALU.mult))
                        link(nc.vector.tensor_scalar(oh[:, 1, :], iot[:, 0:EXPERTS], tf[:, t, 1:2], g2[:, t:t + 1],
                                                     ALU.is_equal, ALU.mult))
                        link(nc.vector.tensor_tensor(gates[:, t, :], oh[:, 0, :], oh[:, 1, :], ALU.add))
                        for o in range(2):
                            link(nc.vector.tensor_scalar(oh[:, o, :], iot[:, 0:EXPERTS], tf[:, t, o:o + 1], None,
                                                         ALU.is_equal))
                        link(nc.vector.tensor_tensor(mask[:, t, :], oh[:, 0, :], oh[:, 1, :], ALU.add))
                    dve.sem_inc(mask_ready, 1)
                    dve.sem_inc(gates_set, 1)
                    for b in range(4, 2 + TT):
                        token_lo(b)
                    dve.wait_ge(gates_hi, 1)
                    nc.vector.tensor_tensor(grouped[:, :, :, 1], gates[:], grouped[:, :, :, 0].bitcast(F32),
                                            ALU.subtract).then_inc(gates_ready, 1)
                    dve.wait_ge(mm_done, rq + 3 + TT)
                    counts = ps[:, (rg + 2 + TT) % 4, :, 0:TT * EXPERTS].rearrange("p a (t e) -> p a t e", e=EXPERTS)
                    link(nc.vector.memset(before[:, 0, :], 0.0))
                    for t in range(TT):
                        link(nc.vector.tensor_tensor(before[:, t + 1, :], before[:, t, :], counts[:, 1, t, :], ALU.add))
                    r = rank[:, :, 0:EXPERTS]
                    link(nc.vector.tensor_tensor(r, counts[:, 0], before[:, 0:TT, :], ALU.add))
                    dve.sem_inc(blk_free, 1)
                    link(nc.vector.scalar_tensor_tensor(r, r, 1.0, mask[:], op0=ALU.add, op1=ALU.mult))
                    link(nc.vector.tensor_scalar(r, r, 1.0, None, ALU.subtract))
                    link(nc.vector.tensor_scalar(rank[:, :, EXPERTS:], rank[:, :, 0:1], float(CAP), None, ALU.subtract))
                    link(nc.vector.tensor_reduce(most[:], before[:, TT, :], AX, ALU.max))
                    nc.vector.tensor_copy(most_i[:], most[:]).then_inc(most_ready, 1)

                    def selection(e, count):
                        nc.vector.tensor_copy(rcol[:], rank[:, :, e]).then_inc(rcol_set, 1)
                        dve.wait_ge(rcol_set, count + 1)
                        for t in range(TT):
                            ins = nc.vector.tensor_scalar(sel[:, t, :], iot[:], rcol[:, t:t + 1], None, ALU.is_equal)
                        ins.then_inc(sel_ready, 1)

                    def expert(u, it, now):
                        nn, qq, gg = n0 + u * UNIT_CH, q0 + u * len(EXPERT), g0 + u * EXPERT_BLOCKS
                        oo = operand[l, "act"] + u * EXPERT_OPERANDS
                        pern, perq, perg, pero = 2 * UNIT_CH, 2 * len(EXPERT), 2 * EXPERT_BLOCKS, 2 * EXPERT_OPERANDS
                        ff = FC0 + u * FB
                        for j, (kind, i, b, c) in enumerate(EXPERT):
                            if c is not None:
                                split_lo(nn + c + 2, now, pern)
                            slot = (gg + b) % 4
                            if kind == "gather":
                                dve.wait_ge(ahi_done, oo + i + 1 + pero * now)
                                four = slice(4 * i, 4 * i + 4)
                                nc.vector.tensor_tensor(
                                    hg_lo[:, four, :].rearrange("p (a k) c -> p a (k c)", a=2), ps[:, slot],
                                    hg_hi[:, four, :].bitcast(F32).rearrange("p (a k) c -> p a (k c)", a=2),
                                    ALU.subtract).then_inc(alo_done, 1)
                                dve.wait_ge(alo_done, oo + i + 1 + pero * now)
                                dve.sem_inc(blk_free, 1)
                            elif kind == "turn":
                                dve.wait_ge(selT_ready, ST * u + i + 1 + 2 * ST * now)
                                dve.sem_inc(blk_free, 1)
                                if i == ST - 1:
                                    nc.vector.tensor_tensor(gslot[:, u, :], gsl[:, u, :, 0], gsl[:, u, :, 1], ALU.add)\
                                        .then_inc(gslot_ready, 1)
                            elif kind == "scatter":
                                dve.wait_ge(mm_done, qq + j + 1 + perq * now)
                                residual(gg + b, 5, i)
                            elif kind == "gu" and i % 2:
                                f = i // 2
                                if f:
                                    lo_part(ea_lo[:, f - 1, :], tt[:, (f - 1) % 2, 0:CAP], ea_hi[:, f - 1, :],
                                            oo + 2 + f + pero * now)
                                dve.wait_ge(silu_done, ff + f + 1 + 2 * FB * now)
                                dve.wait_ge(mm_done, qq + j + 1 + perq * now)
                                nc.vector.tensor_tensor(tt[:, f % 2, 0:CAP], st[:, f % 2, 0:CAP], ps[:, slot, 0, 0:CAP],
                                                        ALU.mult).then_inc(t_done, 1)
                                dve.wait_ge(t_done, ff + f + 1 + 2 * FB * now)
                                dve.sem_inc(blk_free, 2)
                                if f == 4:
                                    selection(2 * it + u + 1, u + 1 + 2 * now)
                                if f == FB - 1:
                                    lo_part(ea_lo[:, f, :], tt[:, f % 2, 0:CAP], ea_hi[:, f, :],
                                            oo + 2 + FB + pero * now)
                            elif kind == "down" and i == FB - 1:
                                for st_ in range(ST):
                                    done = oo + 2 + FB + st_ + 1 + pero * now
                                    dve.wait_ge(ahi_done, done)
                                    for hf in range(2):
                                        cols = slice(512 * hf, 512 * (hf + 1))
                                        ins = nc.vector.scalar_tensor_tensor(
                                            ey_lo[:, st_, cols], ps[:, (gg + 34 + st_) % 4, hf, :],
                                            gslot[:, u, st_:st_ + 1], ey_hi[:, st_, cols].bitcast(F32),
                                            op0=ALU.mult, op1=ALU.subtract)
                                    ins.then_inc(alo_done, 1)
                                    dve.wait_ge(alo_done, done)
                                    dve.sem_inc(blk_free, 1)

                    def experts(first):
                        with dve.Fori(0, EXPERTS // 2) as it:
                            for u in range(2):
                                expert(u, it, first + it)

                    dve.wait_ge(cleared, 4)
                    selection(0, 0)
                    experts(0)
                    with dve.If(dve.value_load(most_i[0:1, 0:1], min_val=0, max_val=T) > CAP):
                        with dve.Fori(1, ROUNDS) as r_:
                            nc.vector.tensor_scalar(rank[:], rank[:], float(CAP), None, ALU.subtract)\
                                .then_inc(rank_moved, 1)
                            dve.wait_ge(rank_moved, r_)
                            dve.sem_inc(round_open, 1)
                            experts(EXPERTS // 2 * r_)
                    with dve.Else():
                        dve.wait_ge(blk_free, g0 + EXPERTS * EXPERT_BLOCKS)
                        dve.sem_inc(blk_free, (ROUNDS - 1) * EXPERTS * EXPERT_BLOCKS)
                        dve.wait_ge(alo_done, operand[l, "act"] + EXPERTS * EXPERT_OPERANDS)
                        dve.sem_inc(alo_done, (ROUNDS - 1) * EXPERTS * EXPERT_OPERANDS)
                    ln, lq_, lg_ = AT[l, "last"]
                    for d in range(KB):
                        dve.wait_ge(mm_done, lq_ + d + 1)
                        residual(lg_ + d, 5, d, x_new)
            n0, q0, g0 = AT["final"]
            dve.wait_ge(root_done, 5)
            link(nc.vector.reciprocal(rstd[:], rstd[:]))
            for kb in range(KB):
                nc.vector.scalar_tensor_tensor(x[:, kb, :], x[:, kb, :], gfin[:, kb:kb + 1], rstd[:],
                                               op0=ALU.mult, op1=ALU.mult).then_inc(yblk, 1)


def kernel(**inputs):
    import numpy as np
    import concourse.bacc as bacc
    from concourse.bass_utils import run_bass_kernel_spmd

    def arr(a):
        return np.ascontiguousarray(a)

    def cols(w):
        *lead, k, n = w.shape
        w = w.reshape(*lead, k // P, P, n // P, P)
        r = len(lead)
        return arr(w.transpose(*range(r), r + 2, r + 1, r, r + 3)).reshape(*lead, n // P, P, k)

    I = {k: np.asarray(v) for k, v in inputs.items()}
    x = np.concatenate([I["x_prompt"][0], I["x_sample"][0]], 0)
    xT = arr(x.T.reshape(KB, P, T).transpose(1, 0, 2))
    cond = np.stack([I["c_ctx"], I["c"][0]], 1)
    condT = arr(cond.reshape(KB, P, 2).transpose(1, 0, 2))
    ada = arr(I["w_ada"].reshape(LAYERS, KB, P, 6, D).transpose(0, 3, 1, 2, 4)).reshape(LAYERS, ADA_CH, P, D)
    w_in = cols(I["w_in"])
    order = [4 + j for j in range(4)] + [j for j in range(4)] + [8 + j for j in range(4)] \
        + [16 + j for j in range(4)] + [20 + j for j in range(4)] + [12 + j for j in range(4)]
    w_in = arr(w_in[:, order])
    w_out = cols(I["w_out"])
    dg = I["w_gu_dense"][0].reshape(D, 2, 2, FF).transpose(2, 0, 1, 3).reshape(2, D, 2 * FF)
    gu = np.concatenate([dg, I["w_gu_moe"][0]], 0)
    gu = cols(gu)
    gu = arr(gu.reshape(-1, 2, FB, P, D).transpose(0, 2, 1, 3, 4)).reshape(-1, P, D)
    gu = np.concatenate([gu, gu[2 * 2 * FB:2 * 2 * FB + 2]], 0)
    moe_down = arr(I["w_down_moe"][0]).reshape(EXPERTS, FB, P, D)
    down = I["w_down_dense"][0].reshape(2, FF, D)
    down = down.reshape(-1, FB, P, KB, P).transpose(0, 3, 1, 2, 4).reshape(-1, FB, 8, P, P)
    down = arr(down.transpose(0, 1, 3, 2, 4)).reshape(-1, FB, P, CHUNK)

    def feat(a):
        a = a.reshape(*a.shape[:-1], -1, P)
        return arr(np.moveaxis(a, -1, 0))

    half = QK // 4
    freqs = np.float32(10000.0) ** (-np.arange(half, dtype=np.float32) / np.float32(half))
    pos = np.arange(LAT)
    row, col = (pos // 64).astype(np.float32), (pos % 64).astype(np.float32)
    ang = np.stack([row, col])[:, None, :] * freqs[None, :, None]
    c, s = np.cos(ang).astype(np.float32), np.sin(ang).astype(np.float32)
    one = np.concatenate([np.concatenate([c[a], c[a]]) for a in range(2)])
    sgn = np.concatenate([np.concatenate([-s[a], s[a]]) for a in range(2)])
    cos, sin = arr(np.concatenate([one, one])), arr(np.concatenate([sgn, sgn]))

    kc = I["cache_k"][0].reshape(LAYERS, PAST, HEADS, P).transpose(0, 3, 2, 1)
    vc = I["cache_v"][0].reshape(LAYERS, PAST // P, P, HEADS * VH).transpose(0, 2, 1, 3)
    arrays = {
        "xT": xT, "condT": condT, "ada_w": ada, "in_w": w_in, "out_w": w_out, "gu_w": gu, "down_w": down,
        "router_w": arr(I["w_router"][0].reshape(KB, P, EXPERTS).transpose(1, 0, 2)),
        "b_ada": feat(I["b_ada"]), "g_mix": feat(I["norm_mix_g"]), "g_ffn": feat(I["norm_ffn_g"]),
        "g_fin": feat(I["final_g"]), "lam_qk": arr(I["lambda_qk"]).reshape(LAYERS, 4 * QK),
        "subln": arr(I["subln_g"].T), "conv_w": feat(I["conv_w"]), "kcT": arr(kc), "vc": arr(vc),
        "cos": cos, "sin": sin, "ident": np.eye(P, dtype=np.float32),
        "iota": arr(np.broadcast_to(np.arange(CAP, dtype=np.float32), (P, CAP))),
        "below": np.triu(np.ones((P, P), np.float32), 1), "moe_down_w": moe_down,
    }
    nc = bacc.Bacc("TRN2", target_bir_lowering=False, num_devices=1, dynamic_dma_scratch_size=1024)
    args = [nc.dram_tensor(n, a.shape, mybir.dt.from_np(a.dtype), kind="ExternalInput").ap()
            for n, a in arrays.items()]
    outs = [("y", (P, KB, T)), ("newk", (LAYERS, P, HEADS, CTX)), ("newv", (LAYERS, P, HEADS, CTX))]
    args += [nc.dram_tensor(n, s, F32, kind="ExternalOutput").ap() for n, s in outs]
    hybrid_step(nc, *args)
    r = run_bass_kernel_spmd(nc, [arrays], core_ids=[0]).results[0]
    y = np.asarray(r["y"]).transpose(1, 0, 2).reshape(D, T).T
    newk = np.asarray(r["newk"]).transpose(0, 3, 2, 1).reshape(1, LAYERS, CTX, HEADS, 2, QK)
    newv = np.asarray(r["newv"]).transpose(0, 3, 2, 1).reshape(1, LAYERS, CTX, HEADS, VH)
    return arr(y[:CTX])[None], arr(y[CTX:])[None], arr(newk), arr(newv)
```

```python
from contextlib import ExitStack

import concourse.bass as bass
from concourse import mybir

P = 128
D = 1024
KB = D // P
CTX, LAT, PAST = 128, 512, 256
T = CTX + LAT
HALF = T // 2
TT = T // P
NKEY = LAT + PAST
KCOLS = T + PAST
KT = KCOLS // P
LAYERS = 2
HEADS, QK, VH = 4, 64, 128
CONV_BLOCKS = 4
EXPERTS = 8
CAP = 256
ROUNDS = -(-T // CAP)
ST = CAP // P
FF = 1408
FB = FF // P
EPS = 1e-6
CHUNK = 8 * P
RAW, SPLIT = 6, 3
ADA_CH, IN_CH, OUT_CH, UNIT_CH = 48, 24, 8, 33
LAM_INIT = [0.8 - 0.6 * 2.718281828459045 ** (-0.3 * l) for l in range(LAYERS)]
SWAP = [(i + 16) % 32 for i in range(32)]

F32 = mybir.dt.float32
F32R = mybir.dt.float32r
U32 = mybir.dt.uint32
I32 = mybir.dt.int32
ALU = mybir.AluOpType
ACT = mybir.ActivationFunctionType
AX = mybir.AxisListType.X
SEGMENTS = [(0, slice(0, CTX), slice(0, CTX), 0), (0, slice(CTX, HALF), slice(CTX, HALF), 1),
            (1, slice(0, HALF), slice(HALF, T), 1)]
TOKENS_OF = [(slice(0, CTX), 0), (slice(CTX, T), 1)]


def unit_groups():
    groups = []
    for c in range(2 * FB):
        groups.append((c, c, True, True, [(i, i) for i in range(KB)]))
    pieces = [(d, k) for d in range(KB) for k in range(FB)]
    for c in range(FB):
        part = [(i, *pieces[8 * c + i]) for i in range(8)]
        for d in sorted({p[1] for p in part}):
            mine = [(i, k) for i, dd, k in part if dd == d]
            groups.append((2 * FB + c, 2 * FB + d, mine[0][0] == 0, mine[-1][1] == FB - 1, mine))
    return groups


UNIT = unit_groups()
EXPERT = [("gather", i, i, None) for i in range(2)] + [("turn", i, 2 + i, None) for i in range(ST)] \
    + [("scatter", d, 4 + d, None) for d in range(KB)] + [("gu", c, 12 + c, c) for c in range(2 * FB)] \
    + [("down", k, 34, 2 * FB + k) for k in range(FB)]
EXPERT_BLOCKS = 36
EXPERT_OPERANDS = 2 + FB + ST

ADA_FIRST = [("rows", 0, k, k) for k in range(KB)] + [("rows", 1, 0, KB), ("turn", 0, 0, None)] \
    + [("rows", 1, k, KB + k) for k in range(1, KB - 1)] + [("norm", 0, 0, None)] \
    + [("rows", 1, KB - 1, 2 * KB - 1), ("spread", 0, 0, None), ("turn", 1, 0, None)]
ADA_BLOCK = {("rows", 0): 0, ("rows", 1): 1, ("turn", 0): 2, ("turn", 1): 3, ("norm", 0): 4, ("spread", 0): 4}


def mingle(items, groups, gaps):
    ada = []
    for g in groups:
        ada += [("rows", g, k) for k in range(KB)] + [("turn", g, 0)]
    out = []
    for i, item in enumerate(items):
        out.append(item)
        taken = 0
        while ada and taken < gaps(i):
            out.append(("ada",) + ada.pop(0))
            taken += out[-1][1] == "rows"
            if out[-1][1] == "rows" and ada and ada[0][0] == "turn":
                break
    assert not ada
    return out


DENSE = mingle([("unit", u, i) for u in range(2) for i in range(len(UNIT))], range(5, 9),
               lambda i: i > 0 and i % len(UNIT) < 2 * FB)


IN_KINDS = [("k", j) for j in range(4)] + [("q", j) for j in range(4)] + [("v", j) for j in range(4)] \
    + [("gc", j) for j in range(4)] + [("xin", j) for j in range(4)] + [("gb", j) for j in range(4)]
IN_SEQ = {l: [] for l in range(LAYERS)}
for _c, (_kind, _j) in enumerate(IN_KINDS):
    for _l in range(LAYERS):
        IN_SEQ[_l].append((_kind, _j))
        if _kind == "gc":
            IN_SEQ[_l].append(("turn", _j))
IN_SEQ[0] = mingle(IN_SEQ[0], range(2, 5), lambda i: i > 0)
IN_SEQ[1] = mingle(IN_SEQ[1], range(9, 12), lambda i: i > 0)


def numbered(seq):
    out, c = [], 0
    for item in seq:
        has = item[1] == "rows" if item[0] == "ada" else item[0] == "unit" and UNIT[item[2]][2] \
            or item[0] not in ("turn", "unit")
        out.append((item, c if has else None))
        c += has
    return out, c


def blocks_of(seq):
    at, count, out = {}, 0, []
    for item in seq:
        key = item if item[0] == "ada" else (item[1], UNIT[item[2]][1])
        if key not in at:
            at[key] = count
            count += 1
        out.append(at[key])
    return out, count


IN_ITEMS = {l: numbered(IN_SEQ[l]) for l in range(LAYERS)}
DENSE_ITEMS = numbered(DENSE)
DENSE_BLOCKS = blocks_of(DENSE)


def plan():
    at, n, q, g = {}, 0, 0, 0
    for l in range(LAYERS):
        items, chunks = IN_ITEMS[l]
        steps = [("ada", 2 * KB, len(ADA_FIRST), 5)] if l == 0 else []
        steps += [("norm1", 0, 2 * l, l), ("in", chunks, len(items), len(items)),
                 ("sub", 0, 2 * HEADS, 1), ("out", OUT_CH, OUT_CH, OUT_CH), ("norm2", 0, 2, 1)]
        if l % 2 == 0:
            steps += [("ffn", DENSE_ITEMS[1], len(DENSE), DENSE_BLOCKS[1])]
        else:
            steps += [("route", 0, 3 + TT, 3 + TT),
                      ("ffn", ROUNDS * EXPERTS * UNIT_CH, ROUNDS * EXPERTS * len(EXPERT),
                       ROUNDS * EXPERTS * EXPERT_BLOCKS),
                      ("last", 0, KB, KB)]
        for name, dn, dq, dg in steps:
            at[l, name] = (n, q, g)
            n, q, g = n + dn, q + dq, g + dg
    at["final"] = (n, q, g)
    return at


AT = plan()
NORM_AT = [(0, ADA_FIRST.index(("norm", 0, 0, None)), ADA_BLOCK["norm", 0]), AT[0, "norm2"], AT[1, "norm1"],
           AT[1, "norm2"], AT["final"]]
SPREAD_AT = [ADA_FIRST.index(("spread", 0, 0, None))] + [_at[1] + 1 for _at in NORM_AT[1:]]
STEPS = [(h, t, 0, CTX) if t == 0 else (h, t, CTX, NKEY) for h in range(HEADS) for t in range(TT)]
NS = len(STEPS)


def hybrid_step(nc, xT, condT, ada_w, in_w, out_w, gu_w, down_w, router_w, b_ada, g_mix, g_ffn, g_fin, lam_qk,
                subln, conv_w, kcT, vc, cos, sin, ident, iota, below, moe_down_w, y, newk, newv):
    with ExitStack() as ctx:
        def sb(name, shape, dt=F32, c=ctx):
            return c.enter_context(nc.sbuf_tensor(name, shape, dt))

        def sem(name):
            return ctx.enter_context(nc.semaphore(name))

        x = sb("x", [P, KB, T])
        a_hi = sb("a_hi", [P, KB, T], F32R)
        a_lo = sb("a_lo", [P, KB, T], F32R)
        raw = sb("raw", [P, RAW, CHUNK])
        w_hi = sb("w_hi", [P, SPLIT, CHUNK], F32R)
        w_lo = sb("w_lo", [P, SPLIT, CHUNK], F32R)
        st = sb("st", [P, 2, T])
        tt = sb("tt", [P, 2, T])
        sq = sb("sq", [P, 2, T])
        ss = sb("ss", [P, T])
        diag = sb("diag", [P, TT, P])
        rms = sb("rms", [P, HEADS, TT])
        eps = sb("eps", [P, 1])
        cos_s = sb("cos_s", [P, LAT])
        sin_s = sb("sin_s", [P, LAT])
        ones = sb("ones", [P, P])
        idn = sb("idn", [P, P])
        cond = sb("cond", [P, KB, 2])
        cs = sb("cs", [P, KB, 2])
        cs4 = sb("cs4", [P, KB, P], F32R)
        bada = sb("bada", [P, LAYERS, 6 * KB])
        mods = sb("mods", [P, LAYERS, 6 * KB, 2])
        gains = sb("gains", [P, LAYERS, 2, KB, 2])
        gmix = sb("gmix", [P, LAYERS, KB])
        gffn = sb("gffn", [P, LAYERS, KB])
        gfin = sb("gfin", [P, KB])
        lq = sb("lq", [P, LAYERS, 4 * QK])
        lp = sb("lp", [P, 2 * QK])
        lsum = sb("lsum", [P, 2])
        lexp = sb("lexp", [P, 2])
        nlam = sb("nlam", [P, 1])
        subg = sb("subg", [P, LAYERS])
        subgs = sb("subgs", [P, LAYERS])
        convw = sb("convw", [P, LAYERS, 3, CONV_BLOCKS])
        nbias = sb("nbias", [P, 4])
        rsum = sb("rsum", [P, 2, 2])
        rinv = sb("rinv", [P, 2, 2])
        wr = sb("wr", [P, KB, EXPERTS])
        iot = sb("iot", [P, CAP])
        bel = sb("bel", [P, P])
        logits = sb("logits", [P, TT, EXPERTS])
        tv = sb("tv", [P, TT, 8])
        ti = sb("ti", [P, TT, 8], U32)
        tf = sb("tf", [P, TT, 8])
        dv = sb("dv", [P, TT])
        ev = sb("ev", [P, TT])
        g1 = sb("g1", [P, TT])
        g2 = sb("g2", [P, TT])
        gates = sb("gates", [P, TT, EXPERTS])
        oh = sb("oh", [P, 2, TT, EXPERTS])
        mask = sb("mask", [P, TT, EXPERTS])
        before = sb("before", [P, TT + 1, EXPERTS])
        rank = sb("rank", [P, TT, EXPERTS + 1])
        grouped = sb("grouped", [P, TT, EXPERTS, 2], F32R)
        rcol = sb("rcol", [P, TT])
        gsl = sb("gsl", [P, 2, ST, 2])
        gslot = sb("gslot", [P, 2, ST])
        most = sb("most", [P, 1])
        most_i = sb("most_i", [P, 1], I32)

        with ExitStack() as mix:
            kT = sb("kT", [P, HEADS, KCOLS], c=mix)
            qT = sb("qT", [P, HEADS, T], c=mix)
            vtok = sb("vtok", [P, KT, HEADS * VH], c=mix)
            att = sb("att", [P, HEADS, T], c=mix)
            gcx = sb("gcx", [P, CONV_BLOCKS, T], c=mix)
            pT = sb("pT", [P, 2, NKEY], c=mix)
            with ExitStack() as vs:
                vT = sb("vT", [P, HEADS, T], c=vs)
            pr = sb("pr", [P, 2, 2, NKEY], c=mix)
        mrow = pT[:].rearrange("p a b -> p (a b)")[:, 0:D]
        with ExitStack() as ffn:
            act_hi = sb("act_hi", [P, FB, T], F32R, c=ffn)
            act_lo = sb("act_lo", [P, FB, T], F32R, c=ffn)
        with ExitStack() as moe:
            with ExitStack() as hs:
                hraw = sb("hraw", [P, KB, T], c=hs)
                lgT = sb("lgT", [EXPERTS, T], c=hs)
            hg_hi = sb("hg_hi", [P, KB, CAP], F32R, c=moe)
            hg_lo = sb("hg_lo", [P, KB, CAP], F32R, c=moe)
            ea_hi = sb("ea_hi", [P, FB, CAP], F32R, c=moe)
            ea_lo = sb("ea_lo", [P, FB, CAP], F32R, c=moe)
            sel = sb("sel", [P, TT, CAP], F32R, c=moe)
            selT = sb("selT", [P, 2, ST, T], F32R, c=moe)
            ey_hi = sb("ey_hi", [P, ST, D], F32R, c=moe)
            ey_lo = sb("ey_lo", [P, ST, D], F32R, c=moe)
        ht_hi = a_hi[:].rearrange("p a b -> p (a b)").rearrange("p (t d) -> p t d", t=TT)
        ht_lo = a_lo[:].rearrange("p a b -> p (a b)").rearrange("p (t d) -> p t d", t=TT)

        ps = ctx.enter_context(nc.psum_tensor("ps", [P, 4, 2, 512], F32))
        S = ps[:, 0:3].rearrange("p a b c -> p a (b c)")
        PT = ps[:, 3].rearrange("p b c -> p (b c)")[:, 0:NKEY]
        OT = ps[:, 3, 1, NKEY - 512:512].rearrange("p (a b) -> p a b", a=2)

        raw_full = [sem(f"raw_full{i}") for i in range(RAW)]
        hi_done = sem("hi_done")
        lo_done = sem("lo_done")
        mm_done = sem("mm_done")
        blk_free = sem("blk_free")
        cond_in = sem("cond_in")
        consts_in = sem("consts_in")
        late_in = sem("late_in")
        x_in = [sem(f"x_in{kb}") for kb in range(KB)]
        cache_in = [sem(f"cache_in{l}") for l in range(LAYERS)]
        ones_set = sem("ones_set")
        dve_step = sem("dve_step")
        silu_c = sem("silu_c")
        cs_hi = sem("cs_hi")
        cs_ready = sem("cs_ready")
        mod_ready = sem("mod_ready")
        x_new = sem("x_new")
        sq_done = sem("sq_done")
        ss_add = sem("ss_add")
        root_done = sem("root_done")
        diag_ready = sem("diag_ready")
        att_diag = sem("att_diag")
        xn_done = sem("xn_done")
        h_done = sem("h_done")
        ahi_done = sem("ahi_done")
        alo_done = sem("alo_done")
        kq_raw = sem("kq_raw")
        kq_ready = sem("kq_ready")
        vt_ready = sem("vt_ready")
        gcx_ready = sem("gcx_ready")
        conv_ready = sem("conv_ready")
        vtok_ready = sem("vtok_ready")
        row_done = sem("row_done")
        lam_sum = sem("lam_sum")
        lam_exp = sem("lam_exp")
        scores_done = sem("scores_done")
        max_done = sem("max_done")
        exp_done = sem("exp_done")
        comb_done = sem("comb_done")
        tr_done = sem("tr_done")
        pt_ready = sem("pt_ready")
        pv_done = sem("pv_done")
        att_ready = sem("att_ready")
        att_sq = sem("att_sq")
        att_root = sem("att_root")
        att_norm = sem("att_norm")
        silu_done = sem("silu_done")
        t_done = sem("t_done")
        dv_ready = sem("dv_ready")
        ev_ready = sem("ev_ready")
        lgT_ready = sem("lgT_ready")
        mask_ready = sem("mask_ready")
        most_ready = sem("most_ready")
        gates_set = sem("gates_set")
        gates_hi = sem("gates_hi")
        gates_ready = sem("gates_ready")
        cleared = sem("cleared")
        rcol_set = sem("rcol_set")
        rank_moved = sem("rank_moved")
        round_open = sem("round_open")
        sel_ready = sem("sel_ready")
        selT_ready = sem("selT_ready")
        gslot_ready = sem("gslot_ready")
        yblk = sem("yblk")
        out_done = sem("out_done")
        k_out = sem("k_out")
        v_out = sem("v_out")
        FC0 = 2 * FB

        block = ctx.enter_context(nc.Block())

        count = 0
        operand = {}
        for l in range(LAYERS):
            for what, k in (("h1", KB), ("cat", KB), ("h2", KB), ("act", 2 * FB if l % 2 == 0 else 0)):
                if l % 2 and what == "h2":
                    k = TT
                operand[l, what] = count
                count += k

        @block.sync
        def _(sp):
            def load(n, src, it=0, per=0):
                if n >= RAW:
                    sp.wait_ge(lo_done, n - RAW + 1 + per * it)
                sp.dma_start(raw[:, n % RAW, :], src).then_inc(raw_full[n % RAW], 16)

            def load_cache(l):
                sp.dma_start(kT[:, :, T:KCOLS], kcT[l]).then_inc(cache_in[l], 16)
                sp.dma_start(vtok[:, TT:KT, :], vc[l]).then_inc(cache_in[l], 16)

            sp.dma_start(cond[:], condT).then_inc(cond_in, 16)
            for n in range(4):
                load(n, ada_w[0, n])
            for dst, src in ((bada, b_ada), (idn, ident), (gmix, g_mix)):
                sp.dma_start(dst[:], src).then_inc(consts_in, 16)
            for n in range(4, 4 + KB):
                sp.dma_start(x[:, n - 4, :], xT[:, n - 4, :]).then_inc(x_in[n - 4], 16)
                load(n, ada_w[0, n])
            for n in range(4 + KB, 2 * KB):
                load(n, ada_w[0, n])
            n = 2 * KB
            late = [(gffn, g_ffn), (gfin, g_fin), (subg, subln), (convw, conv_w), (cos_s, cos), (sin_s, sin),
                    (wr, router_w), (iot, iota), (bel, below), (lq, lam_qk.partition_broadcast(P))]
            for l in range(LAYERS):
                w = 0
                for item, c in IN_ITEMS[l][0]:
                    if c == RAW:
                        if l == 0:
                            for dst, src in late:
                                sp.dma_start(dst[:], src).then_inc(late_in, 16)
                        else:
                            sp.wait_ge(pv_done, l * NS)
                            sp.wait_ge(mm_done, AT[l, "norm1"][1])
                        load_cache(l)
                    if item[0] == "ada" and c is not None:
                        load(n, ada_w[item[2] // 6, KB * (item[2] % 6) + item[3]])
                        n += 1
                    elif c is not None:
                        load(n, in_w[l, w])
                        n, w = n + 1, w + 1
                for c in range(OUT_CH):
                    load(n, out_w[l, c])
                    n += 1
                sp.wait_ge(kq_raw, 8 * l + 4)
                sp.dma_start(newk[l], kT[:, :, 0:CTX]).then_inc(k_out, 16)
                sp.wait_ge(vt_ready, 4 * (l + 1))
                sp.dma_start(newv[l], vT[:, :, 0:CTX]).then_inc(v_out, 16)
                if l % 2 == 0:
                    for item, c in DENSE_ITEMS[0]:
                        if c is None:
                            continue
                        if item[0] == "ada":
                            load(n, ada_w[item[2] // 6, KB * (item[2] % 6) + item[3]])
                        else:
                            u, cc = item[1], UNIT[item[2]][0]
                            load(n, gu_w[2 * FB * u + cc] if cc < 2 * FB else down_w[u, cc - 2 * FB])
                        n += 1
                else:
                    def experts(first):
                        with sp.Fori(0, EXPERTS // 2) as it:
                            for c in range(2, 2 * UNIT_CH + 2):
                                u, cc = c // UNIT_CH, c % UNIT_CH
                                e = 2 * it + u
                                src = gu_w[2 * FB * (2 + e) + cc] if cc < 2 * FB else moe_down_w[e, cc - 2 * FB]
                                load(n + c, src, first + it, 2 * UNIT_CH)

                    for c in range(2):
                        load(n + c, gu_w[2 * FB * 2 + c])
                    experts(0)
                    sp.wait_ge(most_ready, 1)
                    with sp.If(sp.value_load(most_i[0:1, 0:1], min_val=0, max_val=T) > CAP):
                        with sp.Fori(1, ROUNDS) as r:
                            experts(EXPERTS // 2 * r)
            for kb in range(KB):
                sp.wait_ge(yblk, kb + 1)
                sp.dma_start(y[:, kb], x[:, kb, :]).then_inc(out_done, 16)
            sp.wait_ge(out_done, 16 * KB)
            sp.wait_ge(k_out, 16 * LAYERS)
            sp.wait_ge(v_out, 16 * LAYERS)

        @block.tensor
        def _(pe):
            def open_block(g, it=0, per=0):
                if g >= 4:
                    pe.wait_ge(blk_free, g - 3 + per * it)

            def product(out, wsl, opnd_hi, opnd_lo, first, last):
                s, i = wsl
                whi = w_hi[:, s, i * P:(i + 1) * P]
                wlo = w_lo[:, s, i * P:(i + 1) * P]
                for w, o, f, e in ((whi, opnd_hi, first, False), (whi, opnd_lo, False, False),
                                   (wlo, opnd_hi, False, last)):
                    for hf in range(2):
                        ins = nc.tensor.matmul(out[:, hf, 0:HALF], w, o[:, hf * HALF:(hf + 1) * HALF],
                                               start=f, stop=e)
                return ins

            def project_out(l, opnd):
                n0, q0, g0 = AT[l, "out"]
                order = [4, 5, 6, 7, 0, 1, 2, 3]
                two_blocks([(n0, g0), (n0 + 1, g0 + 1)], opnd, order, HEADS, KB)
                for c in range(2, OUT_CH):
                    pe.wait_ge(lo_done, n0 + c + 1)
                    open_block(g0 + c)
                    for j, k in enumerate(order):
                        ins = product(ps[:, (g0 + c) % 4], ((n0 + c) % SPLIT, k), a_hi[:, k, :], a_lo[:, k, :],
                                      j == 0, j == KB - 1)
                    ins.then_inc(mm_done, 1)

            def sums_of(g, col, parts):
                for t in range(TT):
                    for squares in parts:
                        ins = nc.tensor.matmul(ps[:, g % 4, 0, col + t:col + t + 1], squares[:, t * P:(t + 1) * P],
                                               ones[:, 0:1], start=squares is parts[0], stop=squares is parts[-1])
                ins.then_inc(mm_done, 1)

            def spread(g, d):
                for hf in range(2):
                    ins = nc.tensor.matmul(ps[:, g % 4, hf, 0:HALF], ones[:], d[:, hf * HALF:(hf + 1) * HALF],
                                           start=True, stop=True)
                ins.then_inc(mm_done, 1)

            def norm_sums(i):
                n0, q0, g0 = NORM_AT[i]
                open_block(g0)
                pe.wait_ge(ss_add, KB * (i + 1))
                sums_of(g0, 0, [ss[:], sq[:, (KB - 1) % 2, :]])

            def norm_spread(i):
                pe.wait_ge(diag_ready, i + 1)
                spread(NORM_AT[i][2], diag[:].rearrange("p t c -> p (t c)"))

            def weigh_conditions(n, g, first, last):
                pe.wait_ge(lo_done, n + 1)
                k = first[1]
                for w in (w_hi, w_lo):
                    for hf in range(2):
                        ins = nc.tensor.matmul(ps[:, g % 4, hf, :], cs4[:, k, :],
                                               w[:, n % SPLIT, hf * 512:(hf + 1) * 512],
                                               start=(first[0] and w is w_hi), stop=(last and w is w_lo))
                ins.then_inc(mm_done, 1)

            def turn_rows(g, count):
                pe.wait_ge(row_done, count)
                open_block(g)
                for j in range(KB):
                    ins = nc.tensor.transpose(ps[:, g % 4, 0, 4 * j:4 * j + 4], mrow[0:4, j * P:(j + 1) * P],
                                              idn[0:4, 0:4])
                ins.then_inc(mm_done, 1)

            def two_blocks(blocks, opnd, order, j0=0, j1=KB):
                if j0 == 0:
                    for n, g in blocks:
                        pe.wait_ge(lo_done, n + 1)
                        open_block(g)
                for j in range(j0, j1):
                    k = order[j]
                    pe.wait_ge(alo_done, opnd + j + 1)
                    for n, g in blocks:
                        ins = product(ps[:, g % 4], (n % SPLIT, k), a_hi[:, k, :], a_lo[:, k, :], j == 0, j == KB - 1)
                        if j == KB - 1:
                            ins.then_inc(mm_done, 1)

            pe.wait_ge(ones_set, 1)
            for l in range(LAYERS):
                if l == 0:
                    n0, q0, g0 = AT[l, "ada"]
                    pe.wait_ge(cs_ready, 1)
                    pe.wait_ge(consts_in, 16 * 3)
                    for kind, grp, k, c in ADA_FIRST:
                        g = g0 + ADA_BLOCK[kind, grp]
                        if kind == "rows":
                            weigh_conditions(n0 + c, g, (k == 0, k), k == KB - 1)
                        elif kind == "norm":
                            norm_sums(0)
                        elif kind == "spread":
                            norm_spread(0)
                        else:
                            turn_rows(g, grp + 1)
                else:
                    norm_sums(2 * l)
                    norm_spread(2 * l)

                n0, q0, g0 = AT[l, "in"]
                two_blocks([(n0, g0), (n0 + 1, g0 + 1)], operand[l, "h1"], list(range(KB)))
                for b, (item, c) in enumerate(IN_ITEMS[l][0]):
                    if b < 2:
                        continue
                    kind, j = item[0], item[1]
                    if kind == "ada":
                        if c is None:
                            turn_rows(g0 + b, item[2] + 1)
                        else:
                            open_block(g0 + b)
                            weigh_conditions(n0 + c, g0 + b, (True, item[3]), True)
                        continue
                    if kind != "turn":
                        pe.wait_ge(lo_done, n0 + c + 1)
                    open_block(g0 + b)
                    if kind == "turn":
                        pe.wait_ge(vt_ready, 4 * l + j + 1)
                        for t in range(TT):
                            ins = nc.tensor.transpose(ps[:, (g0 + b) % 4, t // 4, (t % 4) * P:(t % 4 + 1) * P],
                                                      vT[:, j, t * P:(t + 1) * P], idn[:])
                    else:
                        for k in range(KB):
                            ins = product(ps[:, (g0 + b) % 4], ((n0 + c) % SPLIT, k), a_hi[:, k, :], a_lo[:, k, :],
                                          k == 0, k == KB - 1)
                    ins.then_inc(mm_done, 1)

                if l == 0:
                    pe.wait_ge(late_in, 16 * 10)
                pe.wait_ge(blk_free, g0 + len(IN_SEQ[l]))
                pe.wait_ge(kq_ready, 8 * (l + 1))
                pe.wait_ge(cache_in[l], 32)
                pe.wait_ge(vtok_ready, 4 * (l + 1))

                def scores(m):
                    if m >= 2 * NS:
                        return
                    h, t, k0, nk = STEPS[m // 2]
                    s = m % 2
                    if m >= 3:
                        pe.wait_ge(exp_done, 2 * l * NS + m - 2)
                    for c0 in range(0, nk, 512):
                        c1 = min(nk, c0 + 512)
                        ins = nc.tensor.matmul(S[:, m % 3, c0:c1], qT[QK * s:QK * (s + 1), h, t * P:(t + 1) * P],
                                               kT[QK * s:QK * (s + 1), h, k0 + c0:k0 + c1],
                                               start=True, stop=True)
                    ins.then_inc(scores_done, 1)

                def weigh_values(i):
                    h, t, k0, nk = STEPS[i]
                    pe.wait_ge(pt_ready, l * NS + i + 1)
                    for j in range(nk // P):
                        ins = nc.tensor.matmul(OT[:, i % 2, :], vtok[:, k0 // P + j, h * VH:(h + 1) * VH],
                                               pT[:, i % 2, j * P:(j + 1) * P], start=(j == 0), stop=(j == nk // P - 1))
                    ins.then_inc(pv_done, 1)

                for m in range(3):
                    scores(m)
                for i, (h, t, k0, nk) in enumerate(STEPS):
                    scores(2 * i + 3)
                    if i > 0:
                        weigh_values(i - 1)
                    scores(2 * i + 4)
                    pe.wait_ge(comb_done, l * NS + i + 1)
                    if i > 0:
                        pe.wait_ge(att_ready, l * NS + i)
                    for j in range(nk // P):
                        ins = nc.tensor.transpose(PT[:, j * P:(j + 1) * P], pr[:, i % 2, 0, j * P:(j + 1) * P], idn[:])
                    ins.then_inc(tr_done, 1)
                weigh_values(NS - 1)

                n0, q0, g0 = AT[l, "sub"]
                pe.wait_ge(att_ready, (l + 1) * NS)
                pe.wait_ge(pt_ready, (l + 1) * NS)
                pe.wait_ge(exp_done, 2 * (l + 1) * NS)
                on0, oq0, og0 = AT[l, "out"]
                first = [(on0, og0), (on0 + 1, og0 + 1)]
                order = [4, 5, 6, 7, 0, 1, 2, 3]
                for h in range(HEADS):
                    pe.wait_ge(att_sq, HEADS * l + h + 1)
                    sums_of(g0, TT * h, [sq[:, h % 2, :]])
                    if h % 2:
                        two_blocks(first, operand[l, "cat"], order, h - 1, h + 1)
                for h in range(HEADS):
                    pe.wait_ge(att_diag, HEADS * l + h + 1)
                    if h >= 2:
                        pe.wait_ge(att_norm, HEADS * l + h - 1)
                    spread(g0 + 3 * (h % 2), sq[:, h % 2, :])

                project_out(l, operand[l, "cat"])
                norm_sums(2 * l + 1)
                norm_spread(2 * l + 1)
                n0, q0, g0 = AT[l, "ffn"]
                if l % 2 == 0:
                    two_blocks([(n0, g0), (n0 + 1, g0 + 1)], operand[l, "h2"], list(range(KB)))
                    for i, (item, c) in enumerate(DENSE_ITEMS[0]):
                        if i < 2:
                            continue
                        g = g0 + DENSE_BLOCKS[0][i]
                        if item[0] == "ada":
                            if c is None:
                                turn_rows(g, item[2] + 1)
                            else:
                                open_block(g)
                                weigh_conditions(n0 + c, g, (True, item[3]), True)
                            continue
                        u = item[1]
                        uc, b, new_chunk, end, pieces = UNIT[item[2]]
                        if new_chunk:
                            slot = (n0 + c) % SPLIT
                            pe.wait_ge(lo_done, n0 + c + 1)
                        if pieces[0][1] == 0:
                            open_block(g)
                        down = uc >= 2 * FB
                        for pos, k in pieces:
                            if down and b == 2 * FB:
                                pe.wait_ge(alo_done, operand[l, "act"] + u * FB + k + 1)
                            hi, lo = (act_hi, act_lo) if down else (a_hi, a_lo)
                            ins = product(ps[:, g % 4], (slot, pos), hi[:, k, :], lo[:, k, :],
                                          k == 0, k == (FB if down else KB) - 1)
                        ins.then_inc(mm_done, 1)
                else:
                    rn, rq, rg = AT[l, "route"]
                    open_block(rg)
                    for k in range(KB):
                        pe.wait_ge(h_done, KB * 3 + k + 1)
                        for hf in range(2):
                            ins = nc.tensor.matmul(ps[0:EXPERTS, rg % 4, hf, 0:HALF], wr[:, k, :],
                                                   hraw[:, k, hf * HALF:(hf + 1) * HALF],
                                                   start=(k == 0), stop=(k == KB - 1))
                    ins.then_inc(mm_done, 1)
                    for b in range(1, 3 + TT):
                        open_block(rg + b)
                        if b == 2:
                            pe.wait_ge(lgT_ready, 1)
                            for t in range(TT):
                                ins = nc.tensor.transpose(ps[:, (rg + b) % 4, 0, t * EXPERTS:(t + 1) * EXPERTS],
                                                          lgT[:, t * P:(t + 1) * P], idn[0:EXPERTS, 0:EXPERTS])
                        elif b == 2 + TT:
                            pe.wait_ge(mask_ready, 1)
                            flat = mask[:].rearrange("p t e -> p (t e)")
                            nc.tensor.matmul(ps[:, (rg + b) % 4, 0, 0:TT * EXPERTS], bel[:], flat, start=True, stop=True)
                            ins = nc.tensor.matmul(ps[:, (rg + b) % 4, 1, 0:TT * EXPERTS], ones[:], flat,
                                                   start=True, stop=True)
                        else:
                            t = 0 if b == 1 else b - 2
                            for k in range(KB):
                                ins = nc.tensor.transpose(ps[:, (rg + b) % 4, k // 4, (k % 4) * P:(k % 4 + 1) * P],
                                                          hraw[:, k, t * P:(t + 1) * P], idn[:])
                        ins.then_inc(mm_done, 1)

                    def scatter(g, d, u, j=0, per=None):
                        for st_ in range(ST):
                            for part in (ey_hi, ey_lo):
                                for hf in range(2):
                                    ins = nc.tensor.matmul(ps[:, g % 4, hf, 0:HALF], part[:, st_, d * P:(d + 1) * P],
                                                           selT[:, u, st_, hf * HALF:(hf + 1) * HALF],
                                                           start=(st_ == 0 and part is ey_hi),
                                                           stop=(st_ == ST - 1 and part is ey_lo))
                        ins.then_inc(mm_done, 1)

                    def expert(u, it, now):
                        nn, qq, gg = n0 + u * UNIT_CH, q0 + u * len(EXPERT), g0 + u * EXPERT_BLOCKS
                        oo = operand[l, "act"] + u * EXPERT_OPERANDS
                        pern, perg, pero = 2 * UNIT_CH, 2 * EXPERT_BLOCKS, 2 * EXPERT_OPERANDS
                        pe.wait_ge(sel_ready, u + 1 + 2 * now)
                        for kind, i, b, c in EXPERT:
                            if c is not None:
                                pe.wait_ge(lo_done, nn + c + 1 + pern * now)
                            if kind == "down" and i == 0:
                                open_block(gg + 34, now, perg)
                                open_block(gg + 35, now, perg)
                            elif kind != "down":
                                open_block(gg + b, now, perg)
                            slot = (gg + b) % 4
                            if kind == "gather":
                                for k in range(4):
                                    d = 4 * i + k
                                    out = ps[:, slot, k // 2, (k % 2) * CAP:(k % 2 + 1) * CAP]
                                    for t in range(TT):
                                        for part in (ht_hi, ht_lo):
                                            ins = nc.tensor.matmul(out, part[:, t, d * P:(d + 1) * P], sel[:, t, :],
                                                                   start=(t == 0 and part is ht_hi),
                                                                   stop=(t == TT - 1 and part is ht_lo))
                            elif kind == "turn":
                                for t in range(TT):
                                    ins = nc.tensor.transpose(
                                        ps[:, slot, t // 4, (t % 4) * P:(t % 4 + 1) * P],
                                        sel[:, t, i * P:(i + 1) * P].bitcast(F32), idn[:])
                                for t in range(TT):
                                    ins = nc.tensor.matmul(ps[:, slot, 1, 256:258], sel[:, t, i * P:(i + 1) * P],
                                                           grouped[:, t, 2 * it + u, :],
                                                           start=(t == 0), stop=(t == TT - 1))
                            elif kind == "scatter":
                                if i == 0:
                                    pe.wait_ge(alo_done, oo + pero * now)
                                scatter(gg + b, i, 1 - u)
                                continue
                            elif kind == "gu":
                                if i == 0:
                                    pe.wait_ge(alo_done, oo + 2 + pero * now)
                                for k in range(KB):
                                    whi = w_hi[:, (nn + c) % SPLIT, k * P:(k + 1) * P]
                                    wlo = w_lo[:, (nn + c) % SPLIT, k * P:(k + 1) * P]
                                    for w, o in ((whi, hg_hi), (whi, hg_lo), (wlo, hg_hi)):
                                        ins = nc.tensor.matmul(ps[:, slot, 0, 0:CAP], w, o[:, k, :],
                                                               start=(k == 0 and o is hg_hi and w is whi),
                                                               stop=(k == KB - 1 and w is wlo))
                            else:
                                pe.wait_ge(alo_done, oo + 2 + i + 1 + pero * now)
                                for st_ in range(ST):
                                    for a, w in ((ea_hi, w_hi), (ea_lo, w_hi), (ea_hi, w_lo)):
                                        for hf in range(2):
                                            ins = nc.tensor.matmul(
                                                ps[:, (gg + 34 + st_) % 4, hf, :], a[:, i, st_ * P:(st_ + 1) * P],
                                                w[:, (nn + c) % SPLIT, hf * 512:(hf + 1) * 512],
                                                start=(i == 0 and a is ea_hi and w is w_hi),
                                                stop=(i == FB - 1 and w is w_lo))
                            ins.then_inc(mm_done, 1)

                    def experts(first):
                        with pe.Fori(0, EXPERTS // 2) as it:
                            for u in range(2):
                                expert(u, it, first + it)

                    pe.wait_ge(cleared, 4)
                    pe.wait_ge(gates_ready, 1)
                    experts(0)
                    pe.wait_ge(most_ready, 1)
                    with pe.If(pe.value_load(most_i[0:1, 0:1], min_val=0, max_val=T) > CAP):
                        with pe.Fori(1, ROUNDS) as r:
                            experts(EXPERTS // 2 * r)
                    with pe.Else():
                        pe.wait_ge(mm_done, q0 + EXPERTS * len(EXPERT))
                        pe.sem_inc(mm_done, (ROUNDS - 1) * EXPERTS * len(EXPERT))
                    ln, lq_, lg_ = AT[l, "last"]
                    pe.wait_ge(alo_done, operand[l, "act"] + ROUNDS * EXPERTS * EXPERT_OPERANDS)
                    for d in range(KB):
                        open_block(lg_ + d)
                        scatter(lg_ + d, d, 1)
            norm_sums(4)
            norm_spread(4)

        @block.scalar
        def _(act):
            def split_hi(n, q, it=0, pern=0, perq=0):
                s = n % SPLIT
                act.wait_ge(raw_full[n % RAW], 16 * (n // RAW + 1) + 16 * (pern // RAW) * it)
                if q > 0:
                    act.wait_ge(mm_done, q + perq * it)
                nc.scalar.activation(w_hi[:, s, :], raw[:, n % RAW, :], ACT.Copy).then_inc(hi_done, 1)

            def square(i, kb, dst_sem=sq_done):
                m = KB * i + kb
                if i == 0:
                    act.wait_ge(x_in[kb], 16)
                else:
                    act.wait_ge(x_new, KB * (i - 1) + kb + 1)
                if m >= 2:
                    act.wait_ge(ss_add, m - 1)
                nc.scalar.activation(sq[:, m % 2, :], x[:, kb, :], ACT.Square).then_inc(dst_sem, 1)

            def root(i, width):
                n0, q0, g0 = NORM_AT[i]
                act.wait_ge(mm_done, q0 + 1)
                nc.scalar.activation(rms[:, 0, :], ps[:, g0 % 4, 0, 0:TT], ACT.Sqrt,
                                     bias=eps[:, 0:1], scale=1.0 / width).then_inc(root_done, 1)

            def modulate(i, opnd):
                l, which = i // 2, i % 2
                act.wait_ge(mod_ready, 2 * l + which + 1)
                for kb in range(KB):
                    act.wait_ge(xn_done, KB * i + kb + 1)
                    if kb >= 2 and i != 3:
                        act.wait_ge(alo_done, opnd + kb - 1)
                    dst = hraw[:, kb, :] if i == 3 else tt[:, kb % 2, :]
                    for toks, c in TOKENS_OF:
                        ins = nc.scalar.activation(dst[:, toks], st[:, kb % 2, toks], ACT.Identity,
                                                   bias=mods[:, l, (3 * which) * KB + kb, c:c + 1],
                                                   scale=gains[:, l, which, kb, c:c + 1])
                    ins.then_inc(h_done, 1)
                    if i == 3:
                        continue
                    act.wait_ge(h_done, KB * i + kb + 1)
                    nc.scalar.activation(a_hi[:, kb, :], tt[:, kb % 2, :], ACT.Copy).then_inc(ahi_done, 1)

            def take_rows(grp, g0):
                nc.scalar.activation(mrow[0:4, :].rearrange("p (a b) -> p a b", a=2),
                                     ps[0:4, (g0 + ADA_BLOCK["rows", grp]) % 4, :, :], ACT.Copy).then_inc(row_done, 1)

            split_hi(0, 0)
            split_hi(1, 0)
            act.wait_ge(cond_in, 16)
            nc.scalar.activation(cs[:], cond[:], ACT.Silu).then_inc(silu_c, 1)
            act.wait_ge(silu_c, 1)
            nc.scalar.activation(cs4[:, :, 0:2], cs[:], ACT.Copy).then_inc(cs_hi, 1)
            for l in range(LAYERS):
                if l == 0:
                    n0, q0, g0 = AT[l, "ada"]
                    for b, (kind, grp, k, c) in enumerate(ADA_FIRST):
                        if kind in ("turn", "spread"):
                            continue
                        if kind == "norm":
                            root(0, D)
                            continue
                        split_hi(n0 + c + 2, q0 + b)
                        if k == KB - 1:
                            act.wait_ge(mm_done, q0 + b + 1)
                            take_rows(grp, g0)
                            act.wait_ge(ones_set, 2)
                        if 5 <= c < 5 + KB:
                            square(0, c - 5)
                else:
                    root(2 * l, D)
                modulate(2 * l, operand[l, "h1"])

                n0, q0, g0 = AT[l, "in"]
                for b, (item, c) in enumerate(IN_ITEMS[l][0]):
                    kind, j = item[0], item[1]
                    if c is not None:
                        split_hi(n0 + c + 2, q0 + b)
                    src = ps[:, (g0 + b) % 4, :, 0:HALF]
                    if kind in ("k", "q", "v", "gc"):
                        act.wait_ge(mm_done, q0 + b + 1)
                        buf = {"k": kT, "q": qT, "v": vT, "gc": gcx}[kind]
                        if kind == "v" and j == 0 and l:
                            act.wait_ge(tr_done, l * NS)
                        if kind == "k" and j == 0 and l:
                            act.wait_ge(k_out, 16 * l)
                        nc.scalar.activation(buf[:, j, 0:T].rearrange("p (a b) -> p a b", a=2), src, ACT.Copy,
                                             scale=QK ** -0.5 if kind == "q" else 1.0)\
                            .then_inc({"k": kq_raw, "q": kq_raw, "v": vt_ready, "gc": gcx_ready}[kind], 1)

                act.wait_ge(lam_sum, l + 1)
                nc.scalar.activation(lexp[:], lsum[:], ACT.Exp).then_inc(lam_exp, 1)
                act.wait_ge(v_out, 16 * (l + 1))
                act.wait_ge(mm_done, AT[l, "sub"][1])

                def exponentials(m):
                    i, s = m // 2, m % 2
                    nk = STEPS[i][3]
                    act.wait_ge(max_done, 2 * l * NS + m + 1)
                    if i >= 2:
                        act.wait_ge(tr_done, l * NS + i - 1)
                    nc.scalar.activation(pr[:, i % 2, s, 0:nk], S[:, m % 3, 0:nk], ACT.Exp,
                                         bias=nbias[:, m % 4:m % 4 + 1], accum_out=rsum[:, i % 2, s:s + 1])\
                        .then_inc(exp_done, 1)

                def take_output(i):
                    h, t, _, _ = STEPS[i]
                    act.wait_ge(pv_done, l * NS + i + 1)
                    nc.scalar.activation(att[:, h, t * P:(t + 1) * P], OT[:, i % 2, :], ACT.Copy).then_inc(att_ready, 1)

                def take_transposed(i):
                    nk = STEPS[i][3]
                    act.wait_ge(tr_done, l * NS + i + 1)
                    if i >= 2:
                        act.wait_ge(pv_done, l * NS + i - 1)
                    nc.scalar.activation(pT[:, i % 2, 0:nk], PT[:, 0:nk], ACT.Copy).then_inc(pt_ready, 1)

                for i in range(NS):
                    exponentials(2 * i)
                    if i >= 1:
                        take_transposed(i - 1)
                    exponentials(2 * i + 1)
                    if i >= 1:
                        take_output(i - 1)
                    if i % 5 == 0:
                        j = i // 5
                        act.wait_ge(conv_ready, 4 * l + j + 1)
                        nc.scalar.activation(a_hi[:, 4 + j, :], gcx[:, j, :], ACT.Copy).then_inc(ahi_done, 1)

                def square_head(h):
                    act.wait_ge(att_ready, l * NS + (h + 1) * TT)
                    if h >= 2:
                        act.wait_ge(mm_done, AT[l, "sub"][1] + h - 1)
                    nc.scalar.activation(sq[:, h % 2, :], att[:, h, :], ACT.Square).then_inc(att_sq, 1)

                for h in range(2):
                    square_head(h)
                take_transposed(NS - 1)
                take_output(NS - 1)
                n0, q0, g0 = AT[l, "sub"]
                for h in range(2, HEADS):
                    square_head(h)
                act.wait_ge(mm_done, q0 + HEADS)
                nc.scalar.activation(rms[:].rearrange("p h t -> p (h t)"), ps[:, g0 % 4, 0, 0:HEADS * TT], ACT.Sqrt,
                                     bias=eps[:, 0:1], scale=1.0 / VH).then_inc(att_root, 1)
                for h in range(HEADS):
                    act.wait_ge(att_norm, HEADS * l + h + 1)
                    nc.scalar.activation(a_hi[:, h, :], att[:, h, :], ACT.Copy).then_inc(ahi_done, 1)

                n0, q0, g0 = AT[l, "out"]
                for c in range(OUT_CH):
                    split_hi(n0 + c + 2, q0 + c)
                    square(2 * l + 1, c)
                root(2 * l + 1, D)
                modulate(2 * l + 1, operand[l, "h2"])

                n0, q0, g0 = AT[l, "ffn"]
                if l % 2 == 0:
                    for i, (item, c) in enumerate(DENSE_ITEMS[0]):
                        if c is not None:
                            split_hi(n0 + c + 2, q0 + i)
                        if item[0] == "ada":
                            continue
                        u = item[1]
                        _, b, _, end, _ = UNIT[item[2]]
                        if not end:
                            continue
                        f, ff = b // 2, u * FB + b // 2
                        if b >= 2 * FB:
                            if u == 1 and b > 2 * FB:
                                square(2, b - 2 * FB - 1)
                        elif b % 2 == 0:
                            act.wait_ge(mm_done, q0 + i + 1)
                            if ff >= 2:
                                act.wait_ge(t_done, ff - 1)
                            nc.scalar.activation(st[:, f % 2, :].rearrange("p (a b) -> p a b", a=2),
                                                 ps[:, (g0 + DENSE_BLOCKS[0][i]) % 4, :, 0:HALF], ACT.Silu)\
                                .then_inc(silu_done, 1)
                        else:
                            act.wait_ge(t_done, ff + 1)
                            nc.scalar.activation(act_hi[:, f, :], tt[:, f % 2, :], ACT.Copy).then_inc(ahi_done, 1)
                else:
                    rn, rq, rg = AT[l, "route"]
                    act.wait_ge(mm_done, rq + 1)
                    nc.scalar.activation(lgT[:].rearrange("p (a b) -> p a b", a=2), ps[0:EXPERTS, rg % 4, :, 0:HALF],
                                         ACT.Copy).then_inc(lgT_ready, 1)
                    for b in (1, 3):
                        act.wait_ge(mm_done, rq + b + 1)
                        nc.scalar.activation(ht_hi[:, 0 if b == 1 else 1, :].rearrange("p (a b) -> p a b", a=2),
                                             ps[:, (rg + b) % 4], ACT.Copy).then_inc(ahi_done, 1)
                    act.wait_ge(dv_ready, 1)
                    nc.scalar.activation(ev[:], dv[:], ACT.Exp).then_inc(ev_ready, 1)
                    for b in range(4, 2 + TT):
                        act.wait_ge(mm_done, rq + b + 1)
                        nc.scalar.activation(ht_hi[:, b - 2, :].rearrange("p (a b) -> p a b", a=2),
                                             ps[:, (rg + b) % 4], ACT.Copy).then_inc(ahi_done, 1)
                    act.wait_ge(gates_set, 1)
                    nc.scalar.activation(grouped[:, :, :, 0], gates[:], ACT.Copy).then_inc(gates_hi, 1)

                    def expert(u, it, now):
                        nn, qq, gg = n0 + u * UNIT_CH, q0 + u * len(EXPERT), g0 + u * EXPERT_BLOCKS
                        pern, perq = 2 * UNIT_CH, 2 * len(EXPERT)
                        ff = FC0 + u * FB
                        for j, (kind, i, b, c) in enumerate(EXPERT):
                            if c is not None:
                                split_hi(nn + c + 2, qq + j, now, pern, perq)
                            slot = (gg + b) % 4
                            if kind == "gather":
                                act.wait_ge(mm_done, qq + j + 1 + perq * now)
                                nc.scalar.activation(hg_hi[:, 4 * i:4 * i + 4, :].rearrange("p (a k) c -> p a (k c)", a=2),
                                                     ps[:, slot], ACT.Copy).then_inc(ahi_done, 1)
                            elif kind == "turn":
                                act.wait_ge(mm_done, qq + j + 1 + perq * now)
                                nc.scalar.activation(selT[:, u, i, 0:512], ps[:, slot, 0, :], ACT.Copy)
                                nc.scalar.activation(selT[:, u, i, 512:T], ps[:, slot, 1, 0:T - 512], ACT.Copy)
                                nc.scalar.activation(gsl[:, u, i, :], ps[:, slot, 1, 256:258], ACT.Copy)\
                                    .then_inc(selT_ready, 1)
                            elif kind == "gu" and i % 2 == 0:
                                f = i // 2
                                act.wait_ge(mm_done, qq + j + 1 + perq * now)
                                act.wait_ge(t_done, ff + f - 1 + 2 * FB * now)
                                nc.scalar.activation(st[:, f % 2, 0:CAP], ps[:, slot, 0, 0:CAP], ACT.Silu)\
                                    .then_inc(silu_done, 1)
                            elif kind == "gu":
                                f = i // 2
                                act.wait_ge(t_done, ff + f + 1 + 2 * FB * now)
                                nc.scalar.activation(ea_hi[:, f, :], tt[:, f % 2, 0:CAP], ACT.Copy).then_inc(ahi_done, 1)
                            elif kind == "down" and i == FB - 1:
                                act.wait_ge(mm_done, qq + j + 1 + perq * now)
                                act.wait_ge(gslot_ready, u + 1 + 2 * now)
                                for st_ in range(ST):
                                    nc.scalar.activation(ey_hi[:, st_, :].rearrange("p (a b) -> p a b", a=2),
                                                         ps[:, (gg + 34 + st_) % 4], ACT.Copy,
                                                         scale=gslot[:, u, st_:st_ + 1]).then_inc(ahi_done, 1)

                    def experts(first):
                        with act.Fori(0, EXPERTS // 2) as it:
                            for u in range(2):
                                expert(u, it, first + it)

                    act.wait_ge(cleared, 4)
                    experts(0)
                    act.wait_ge(most_ready, 1)
                    with act.If(act.value_load(most_i[0:1, 0:1], min_val=0, max_val=T) > CAP):
                        with act.Fori(1, ROUNDS) as r:
                            experts(EXPERTS // 2 * r)
                for kb in range(KB - 1 if l == 0 else 0, KB):
                    square(2 * l + 2, kb)
            root(4, D)

        @block.gpsimd
        def _(pool):
            nc.gpsimd.memset(ones[:], 1.0).then_inc(ones_set, 1)
            nc.gpsimd.memset(eps[:], EPS).then_inc(ones_set, 1)
            for i in range(5):
                if i == 4:
                    pool.wait_ge(ahi_done, operand[1, "h2"] + TT)
                    pool.wait_ge(mask_ready, 1)
                    for buf in (ey_hi, ey_lo, selT[:, 1], gsl):
                        nc.gpsimd.memset(buf[:].bitcast(F32) if buf is not gsl else gsl[:], 0.0).then_inc(cleared, 1)
                for kb in range(KB):
                    m = KB * i + kb
                    pool.wait_ge(sq_done, m + 1)
                    if kb == 0:
                        if i:
                            pool.wait_ge(mm_done, NORM_AT[i - 1][1] + 1)
                        nc.gpsimd.tensor_copy(ss[:], sq[:, m % 2, :]).then_inc(ss_add, 1)
                    elif kb == KB - 1:
                        pool.wait_ge(ss_add, m)
                        pool.sem_inc(ss_add, 1)
                    else:
                        pool.wait_ge(ss_add, m)
                        nc.gpsimd.tensor_tensor(ss[:], ss[:], sq[:, m % 2, :], ALU.add).then_inc(ss_add, 1)

        @block.vector
        def _(dve):
            chain = [0]

            def link(ins):
                chain[0] += 1
                ins.then_inc(dve_step, 1)
                dve.wait_ge(dve_step, chain[0])

            def split_lo(n, it=0, pern=0):
                s = n % SPLIT
                dve.wait_ge(hi_done, n + 1 + pern * it)
                nc.vector.tensor_tensor(w_lo[:, s, :], raw[:, n % RAW, :], w_hi[:, s, :].bitcast(F32), ALU.subtract)\
                    .then_inc(lo_done, 1)

            def lo_part(dst, full, hi, done):
                dve.wait_ge(ahi_done, done)
                nc.vector.tensor_tensor(dst, full, hi.bitcast(F32), ALU.subtract).then_inc(alo_done, 1)

            def reciprocal_root(i):
                dve.wait_ge(root_done, i + 1)
                link(nc.vector.reciprocal(rms[:, 0, :], rms[:, 0, :]))
                diagonal(diag[:], 0).then_inc(diag_ready, 1)

            def diagonal(dst, h):
                return nc.vector.tensor_tensor(dst, idn[:].unsqueeze(1).broadcast_to([P, TT, P]),
                                               rms[:, h, :].unsqueeze(2).broadcast_to([P, TT, P]), ALU.mult)

            def halves(a):
                return a.rearrange("p (a b) -> p a b", a=2)

            def norm(i, opnd):
                if i:
                    reciprocal_root(i)
                g = NORM_AT[i][2]
                dve.wait_ge(mm_done, SPREAD_AT[i] + 1)
                for kb in range(KB):
                    if kb >= 2:
                        dve.wait_ge(h_done, KB * i + kb - 1)
                    nc.vector.tensor_tensor(halves(st[:, kb % 2, :]), halves(x[:, kb, :]), ps[:, g % 4, :, 0:HALF],
                                            ALU.mult).then_inc(xn_done, 1)
                    if kb == KB - 1:
                        dve.wait_ge(xn_done, KB * (i + 1))
                        dve.sem_inc(blk_free, 1)
                    if kb and i != 3:
                        lo_part(a_lo[:, kb - 1, :], tt[:, (kb - 1) % 2, :], a_hi[:, kb - 1, :], opnd + kb)
                if i != 3:
                    lo_part(a_lo[:, KB - 1, :], tt[:, (KB - 1) % 2, :], a_hi[:, KB - 1, :], opnd + KB)

            def residual(l, g, gate, d, x_sem=None):
                for n, (hf, cols, toks, c) in enumerate(SEGMENTS):
                    ins = nc.vector.scalar_tensor_tensor(x[:, d, toks], ps[:, g % 4, hf, cols],
                                                         mods[:, l, gate * KB + d, c:c + 1], x[:, d, toks],
                                                         op0=ALU.mult, op1=ALU.add)
                ins.then_inc(blk_free, 1)
                if x_sem is not None:
                    dve.wait_ge(blk_free, g + 1)
                    dve.sem_inc(x_sem, 1)

            def modulation(l, grp, g, q):
                dve.wait_ge(mm_done, q + 1)
                mine = mods[:, l, grp * KB:(grp + 1) * KB, :]
                col = ps[:, g % 4, 0, 0:4 * KB].rearrange("p (c j) -> p c j", j=4)
                link(nc.vector.tensor_tensor(
                    mine, col[:, :, 0:2],
                    bada[:, l, grp * KB:(grp + 1) * KB].unsqueeze(2).broadcast_to([P, KB, 2]), ALU.add))
                link(nc.vector.tensor_tensor(mine, mine, col[:, :, 2:4], ALU.add))
                dve.sem_inc(blk_free, 1)
                if grp % 3 == 1:
                    w = grp // 3
                    nc.vector.scalar_tensor_tensor(gains[:, l, w], mine, 1.0,
                                                   (gmix, gffn)[w][:, l, :].unsqueeze(2).broadcast_to([P, KB, 2]),
                                                   op0=ALU.add, op1=ALU.mult).then_inc(mod_ready, 1)

            def modulation_item(item, g, q):
                _, kind, grp, k = item
                if kind == "turn":
                    modulation(grp // 6, grp % 6, g, q)
                    return
                dve.wait_ge(mm_done, q + 1)
                rows = mrow[0:4, :].rearrange("p (a b) -> p a b", a=2)
                if k == 0:
                    link(nc.vector.tensor_copy(rows, ps[0:4, g % 4]))
                else:
                    link(nc.vector.tensor_tensor(rows, rows, ps[0:4, g % 4], ALU.add))
                dve.sem_inc(blk_free, 1)
                if k == KB - 1:
                    dve.sem_inc(row_done, 1)

            def lambda_sums(l):
                link(nc.vector.tensor_tensor(lp[:, 0:QK], lq[:, l, 0:QK], lq[:, l, QK:2 * QK], ALU.mult))
                link(nc.vector.tensor_tensor(lp[:, QK:], lq[:, l, 2 * QK:3 * QK], lq[:, l, 3 * QK:], ALU.mult))
                nc.vector.tensor_reduce(lsum[:], lp[:].rearrange("p (a b) -> p a b", a=2), AX, ALU.add)\
                    .then_inc(lam_sum, 1)
                link(nc.vector.tensor_scalar(subgs[:, l:l + 1], subg[:, l:l + 1], 1.0 - LAM_INIT[l], None,
                                             ALU.mult))

            split_lo(0)
            split_lo(1)
            dve.wait_ge(silu_c, 1)
            dve.wait_ge(cs_hi, 1)
            nc.vector.memset(cs4[:, :, 4:P].bitcast(F32), 0.0)
            nc.vector.tensor_tensor(cs4[:, :, 2:4], cs[:], cs4[:, :, 0:2].bitcast(F32), ALU.subtract)\
                .then_inc(cs_ready, 1)
            for l in range(LAYERS):
                if l == 0:
                    n0, q0, g0 = AT[l, "ada"]
                    for b, (kind, grp, k, c) in enumerate(ADA_FIRST):
                        if kind == "turn":
                            dve.wait_ge(consts_in, 16 * 3)
                            modulation(l, grp, g0 + ADA_BLOCK[kind, grp], q0 + b)
                            continue
                        if kind == "norm":
                            dve.wait_ge(consts_in, 16 * 3)
                            reciprocal_root(0)
                        if kind in ("norm", "spread"):
                            continue
                        split_lo(n0 + c + 2)
                        if k == KB - 1:
                            dve.wait_ge(row_done, grp + 1)
                            dve.sem_inc(blk_free, 1)
                if l:
                    lambda_sums(l)
                norm(2 * l, operand[l, "h1"])
                if l == 0:
                    dve.wait_ge(late_in, 16 * 10)
                    lambda_sums(l)

                n0, q0, g0 = AT[l, "in"]
                lat = slice(CTX, T)
                swp, cv = tt[:, 1, 0:LAT], tt[:, 0, :]
                for b, (item, c) in enumerate(IN_ITEMS[l][0]):
                    kind, j = item[0], item[1]
                    if kind == "ada":
                        if c is not None:
                            split_lo(n0 + c + 2)
                        modulation_item(item, g0 + b, q0 + b)
                        continue
                    if kind == "turn":
                        dve.wait_ge(mm_done, q0 + b + 1)
                        for t0, t1, bank in ((0, 4, 0), (4, TT, 1)):
                            ins = nc.vector.tensor_copy(vtok[:, t0:t1, j * VH:(j + 1) * VH],
                                                        ps[:, (g0 + b) % 4, bank, 0:(t1 - t0) * P]
                                                        .rearrange("p (t e) -> p t e", e=VH))
                        link(ins)
                        dve.sem_inc(blk_free, 1)
                        dve.sem_inc(vtok_ready, 1)
                        continue
                    split_lo(n0 + c + 2)
                    src = ps[:, (g0 + b) % 4, :, 0:HALF]
                    if kind in ("k", "q"):
                        buf = kT if kind == "k" else qT
                        kq = 8 * l + (0 if kind == "k" else 4) + j + 1
                        dve.wait_ge(kq_raw, kq)
                        dve.sem_inc(blk_free, 1)
                        link(nc.vector.stream_shuffle(swp, buf[:, j, lat], SWAP))
                        link(nc.vector.tensor_tensor(swp, swp, sin_s[:], ALU.mult))
                        link(nc.vector.tensor_tensor(buf[:, j, lat], buf[:, j, lat], cos_s[:], ALU.mult))
                        nc.vector.tensor_tensor(buf[:, j, lat], buf[:, j, lat], swp, ALU.add).then_inc(kq_ready, 1)
                        dve.wait_ge(kq_ready, kq)
                    elif kind == "v":
                        dve.wait_ge(vt_ready, 4 * l + j + 1)
                        dve.sem_inc(blk_free, 1)
                    elif kind == "gc":
                        dve.wait_ge(gcx_ready, 4 * l + j + 1)
                        dve.sem_inc(blk_free, 1)
                    elif kind == "xin":
                        dve.wait_ge(mm_done, q0 + b + 1)
                        g3 = gcx[:, j, :].rearrange("p (a b) -> p a b", a=2)
                        nc.vector.tensor_tensor(g3, g3, src, ALU.mult).then_inc(blk_free, 1)
                    else:
                        dve.wait_ge(blk_free, g0 + b)
                        link(nc.vector.tensor_scalar(cv, gcx[:, j, :], convw[:, l, 1, j:j + 1], None, ALU.mult))
                        for lo, hi in ((0, CTX), (CTX, T)):
                            link(nc.vector.scalar_tensor_tensor(cv[:, lo + 1:hi], gcx[:, j, lo:hi - 1],
                                                                convw[:, l, 0, j:j + 1], cv[:, lo + 1:hi],
                                                                op0=ALU.mult, op1=ALU.add))
                            link(nc.vector.scalar_tensor_tensor(cv[:, lo:hi - 1], gcx[:, j, lo + 1:hi],
                                                                convw[:, l, 2, j:j + 1], cv[:, lo:hi - 1],
                                                                op0=ALU.mult, op1=ALU.add))
                        dve.wait_ge(mm_done, q0 + b + 1)
                        link(nc.vector.tensor_tensor(gcx[:, j, :].rearrange("p (a b) -> p a b", a=2),
                                                     cv.rearrange("p (a b) -> p a b", a=2), src, ALU.mult))
                        dve.sem_inc(blk_free, 1)
                        dve.sem_inc(conv_ready, 1)

                dve.wait_ge(lam_exp, l + 1)
                link(nc.vector.tensor_tensor(nlam[:], lexp[:, 1:2], lexp[:, 0:1], ALU.subtract))
                link(nc.vector.tensor_scalar(nlam[:], nlam[:], LAM_INIT[l], None, ALU.subtract))

                def row_max(m):
                    if m >= 2 * NS:
                        return
                    dve.wait_ge(scores_done, 2 * l * NS + m + 1)
                    nc.vector.tensor_reduce(nbias[:, m % 4:m % 4 + 1], S[:, m % 3, 0:STEPS[m // 2][3]], AX, ALU.max,
                                            negate=True).then_inc(max_done, 1)

                for m in range(3):
                    row_max(m)
                for i, (h, t, k0, nk) in enumerate(STEPS):
                    b = i % 2
                    dve.wait_ge(exp_done, 2 * (l * NS + i + 1))
                    link(nc.vector.reciprocal(rinv[:, b, :], rsum[:, b, :]))
                    link(nc.vector.tensor_scalar(pr[:, b, 1, 0:nk], pr[:, b, 1, 0:nk], rinv[:, b, 1:2], nlam[:, 0:1],
                                                 ALU.mult, ALU.mult))
                    nc.vector.scalar_tensor_tensor(pr[:, b, 0, 0:nk], pr[:, b, 0, 0:nk], rinv[:, b, 0:1],
                                                   pr[:, b, 1, 0:nk], op0=ALU.mult, op1=ALU.add)\
                        .then_inc(comb_done, 1)
                    row_max(2 * i + 3)
                    row_max(2 * i + 4)
                    if i % 5 == 0:
                        j = i // 5
                        lo_part(a_lo[:, 4 + j, :], gcx[:, j, :], a_hi[:, 4 + j, :], operand[l, "cat"] + j + 1)
                sn, sq0, sg = AT[l, "sub"]
                dve.wait_ge(att_root, l + 1)
                rall = rms[:].rearrange("p h t -> p (h t)")
                link(nc.vector.reciprocal(rall, rall))
                for h in range(-2, HEADS):
                    if h >= 0:
                        dve.wait_ge(mm_done, sq0 + HEADS + h + 1)
                        nc.vector.scalar_tensor_tensor(halves(att[:, h, :]), halves(att[:, h, :]), subgs[:, l:l + 1],
                                                       ps[:, (sg + 3 * (h % 2)) % 4, :, 0:HALF],
                                                       op0=ALU.mult, op1=ALU.mult).then_inc(att_norm, 1)
                    if h + 2 < HEADS:
                        diagonal(sq[:, h % 2, :].rearrange("p (t c) -> p t c", c=P), h + 2).then_inc(att_diag, 1)
                    if h < 0:
                        continue
                    if h:
                        lo_part(a_lo[:, h - 1, :], att[:, h - 1, :], a_hi[:, h - 1, :], operand[l, "cat"] + 4 + h)
                lo_part(a_lo[:, HEADS - 1, :], att[:, HEADS - 1, :], a_hi[:, HEADS - 1, :],
                        operand[l, "cat"] + 4 + HEADS)
                dve.sem_inc(blk_free, 1)

                n0, q0, g0 = AT[l, "out"]
                for c in range(OUT_CH):
                    split_lo(n0 + c + 2)
                    dve.wait_ge(mm_done, q0 + c + 1)
                    residual(l, g0 + c, 2, c, x_new)
                norm(2 * l + 1, operand[l, "h2"])

                n0, q0, g0 = AT[l, "ffn"]
                if l % 2 == 0:
                    for i, (item, c) in enumerate(DENSE_ITEMS[0]):
                        if c is not None:
                            split_lo(n0 + c + 2)
                        g = g0 + DENSE_BLOCKS[0][i]
                        if item[0] == "ada":
                            modulation_item(item, g, q0 + i)
                            continue
                        u = item[1]
                        opnd = operand[l, "act"] + u * FB
                        _, b, _, end, _ = UNIT[item[2]]
                        if not end:
                            continue
                        f, ff = b // 2, u * FB + b // 2
                        if b >= 2 * FB:
                            dve.wait_ge(mm_done, q0 + i + 1)
                            residual(l, g, 5, b - 2 * FB, x_new if u == 1 else None)
                        elif b % 2 == 0:
                            dve.wait_ge(silu_done, ff + 1)
                            dve.sem_inc(blk_free, 1)
                        else:
                            if f:
                                lo_part(act_lo[:, f - 1, :], tt[:, (f - 1) % 2, :], act_hi[:, f - 1, :], opnd + f)
                            dve.wait_ge(mm_done, q0 + i + 1)
                            nc.vector.tensor_tensor(tt[:, f % 2, :].rearrange("p (a b) -> p a b", a=2),
                                                    st[:, f % 2, :].rearrange("p (a b) -> p a b", a=2),
                                                    ps[:, g % 4, :, 0:HALF], ALU.mult).then_inc(t_done, 1)
                            dve.wait_ge(t_done, ff + 1)
                            dve.sem_inc(blk_free, 1)
                            if f == FB - 1:
                                lo_part(act_lo[:, f, :], tt[:, f % 2, :], act_hi[:, f, :], opnd + FB)
                else:
                    rn, rq, rg = AT[l, "route"]

                    def token_lo(b):
                        t = 0 if b == 1 else b - 2
                        dve.wait_ge(ahi_done, operand[l, "h2"] + t + 1)
                        nc.vector.tensor_tensor(ht_lo[:, t, :].rearrange("p (a b) -> p a b", a=2), ps[:, (rg + b) % 4],
                                                ht_hi[:, t, :].bitcast(F32).rearrange("p (a b) -> p a b", a=2),
                                                ALU.subtract).then_inc(alo_done, 1)
                        dve.wait_ge(alo_done, operand[l, "h2"] + t + 1)
                        dve.sem_inc(blk_free, 1)

                    dve.wait_ge(lgT_ready, 1)
                    dve.sem_inc(blk_free, 1)
                    token_lo(1)
                    dve.wait_ge(mm_done, rq + 3)
                    link(nc.vector.tensor_copy(logits[:].rearrange("p t e -> p (t e)"),
                                               ps[:, (rg + 2) % 4, 0, 0:TT * EXPERTS]))
                    dve.sem_inc(blk_free, 1)
                    for t in range(TT):
                        link(nc.vector.max(tv[:, t, :], logits[:, t, :]))
                        link(nc.vector.max_index(ti[:, t, :], tv[:, t, :], logits[:, t, :]))
                    link(nc.vector.tensor_copy(tf[:], ti[:]))
                    link(nc.vector.tensor_tensor(dv[:], tv[:, :, 1], tv[:, :, 0], ALU.subtract))
                    dve.sem_inc(dv_ready, 1)
                    experts_row = iot[:, 0:EXPERTS].unsqueeze(1).broadcast_to([P, TT, EXPERTS])
                    for o in range(2):
                        link(nc.vector.tensor_tensor(oh[:, o], experts_row,
                                                     tf[:, :, o:o + 1].broadcast_to([P, TT, EXPERTS]), ALU.is_equal))
                    link(nc.vector.tensor_tensor(mask[:], oh[:, 0], oh[:, 1], ALU.add))
                    dve.sem_inc(mask_ready, 1)
                    token_lo(3)
                    dve.wait_ge(ev_ready, 1)
                    link(nc.vector.tensor_scalar(g1[:], ev[:], 1.0, None, ALU.add))
                    link(nc.vector.reciprocal(g1[:], g1[:]))
                    link(nc.vector.tensor_tensor(g2[:], ev[:], g1[:], ALU.mult))
                    for o, share in enumerate((g1, g2)):
                        link(nc.vector.tensor_tensor(oh[:, o], oh[:, o],
                                                     share[:].unsqueeze(2).broadcast_to([P, TT, EXPERTS]), ALU.mult))
                    link(nc.vector.tensor_tensor(gates[:], oh[:, 0], oh[:, 1], ALU.add))
                    dve.sem_inc(gates_set, 1)
                    for b in range(4, 2 + TT):
                        token_lo(b)
                    dve.wait_ge(gates_hi, 1)
                    nc.vector.tensor_tensor(grouped[:, :, :, 1], gates[:], grouped[:, :, :, 0].bitcast(F32),
                                            ALU.subtract).then_inc(gates_ready, 1)
                    dve.wait_ge(mm_done, rq + 3 + TT)
                    counts = ps[:, (rg + 2 + TT) % 4, :, 0:TT * EXPERTS].rearrange("p a (t e) -> p a t e", e=EXPERTS)
                    link(nc.vector.memset(before[:, 0, :], 0.0))
                    for t in range(TT):
                        link(nc.vector.tensor_tensor(before[:, t + 1, :], before[:, t, :], counts[:, 1, t, :], ALU.add))
                    r = rank[:, :, 0:EXPERTS]
                    link(nc.vector.tensor_tensor(r, counts[:, 0], before[:, 0:TT, :], ALU.add))
                    dve.sem_inc(blk_free, 1)
                    link(nc.vector.scalar_tensor_tensor(r, r, 1.0, mask[:], op0=ALU.add, op1=ALU.mult))
                    link(nc.vector.tensor_scalar(r, r, 1.0, None, ALU.subtract))
                    link(nc.vector.tensor_scalar(rank[:, :, EXPERTS:], rank[:, :, 0:1], float(CAP), None, ALU.subtract))
                    link(nc.vector.tensor_reduce(most[:], before[:, TT, :], AX, ALU.max))
                    nc.vector.tensor_copy(most_i[:], most[:]).then_inc(most_ready, 1)

                    def selection(e, count):
                        nc.vector.tensor_copy(rcol[:], rank[:, :, e]).then_inc(rcol_set, 1)
                        dve.wait_ge(rcol_set, count + 1)
                        for t in range(TT):
                            ins = nc.vector.tensor_scalar(sel[:, t, :], iot[:], rcol[:, t:t + 1], None, ALU.is_equal)
                        ins.then_inc(sel_ready, 1)

                    def expert(u, it, now):
                        nn, qq, gg = n0 + u * UNIT_CH, q0 + u * len(EXPERT), g0 + u * EXPERT_BLOCKS
                        oo = operand[l, "act"] + u * EXPERT_OPERANDS
                        pern, perq, perg, pero = 2 * UNIT_CH, 2 * len(EXPERT), 2 * EXPERT_BLOCKS, 2 * EXPERT_OPERANDS
                        ff = FC0 + u * FB
                        for j, (kind, i, b, c) in enumerate(EXPERT):
                            if c is not None:
                                split_lo(nn + c + 2, now, pern)
                            slot = (gg + b) % 4
                            if kind == "gather":
                                dve.wait_ge(ahi_done, oo + i + 1 + pero * now)
                                four = slice(4 * i, 4 * i + 4)
                                nc.vector.tensor_tensor(
                                    hg_lo[:, four, :].rearrange("p (a k) c -> p a (k c)", a=2), ps[:, slot],
                                    hg_hi[:, four, :].bitcast(F32).rearrange("p (a k) c -> p a (k c)", a=2),
                                    ALU.subtract).then_inc(alo_done, 1)
                                dve.wait_ge(alo_done, oo + i + 1 + pero * now)
                                dve.sem_inc(blk_free, 1)
                            elif kind == "turn":
                                dve.wait_ge(selT_ready, ST * u + i + 1 + 2 * ST * now)
                                dve.sem_inc(blk_free, 1)
                                if i == ST - 1:
                                    nc.vector.tensor_tensor(gslot[:, u, :], gsl[:, u, :, 0], gsl[:, u, :, 1], ALU.add)\
                                        .then_inc(gslot_ready, 1)
                            elif kind == "scatter":
                                dve.wait_ge(mm_done, qq + j + 1 + perq * now)
                                residual(l, gg + b, 5, i)
                            elif kind == "gu" and i % 2:
                                f = i // 2
                                if f:
                                    lo_part(ea_lo[:, f - 1, :], tt[:, (f - 1) % 2, 0:CAP], ea_hi[:, f - 1, :],
                                            oo + 2 + f + pero * now)
                                dve.wait_ge(silu_done, ff + f + 1 + 2 * FB * now)
                                dve.wait_ge(mm_done, qq + j + 1 + perq * now)
                                nc.vector.tensor_tensor(tt[:, f % 2, 0:CAP], st[:, f % 2, 0:CAP], ps[:, slot, 0, 0:CAP],
                                                        ALU.mult).then_inc(t_done, 1)
                                dve.wait_ge(t_done, ff + f + 1 + 2 * FB * now)
                                dve.sem_inc(blk_free, 2)
                                if f == 4:
                                    selection(2 * it + u + 1, u + 1 + 2 * now)
                                if f == FB - 1:
                                    lo_part(ea_lo[:, f, :], tt[:, f % 2, 0:CAP], ea_hi[:, f, :],
                                            oo + 2 + FB + pero * now)
                            elif kind == "down" and i == FB - 1:
                                for st_ in range(ST):
                                    done = oo + 2 + FB + st_ + 1 + pero * now
                                    dve.wait_ge(ahi_done, done)
                                    for hf in range(2):
                                        cols = slice(512 * hf, 512 * (hf + 1))
                                        ins = nc.vector.scalar_tensor_tensor(
                                            ey_lo[:, st_, cols], ps[:, (gg + 34 + st_) % 4, hf, :],
                                            gslot[:, u, st_:st_ + 1], ey_hi[:, st_, cols].bitcast(F32),
                                            op0=ALU.mult, op1=ALU.subtract)
                                    ins.then_inc(alo_done, 1)
                                    dve.wait_ge(alo_done, done)
                                    dve.sem_inc(blk_free, 1)

                    def experts(first):
                        with dve.Fori(0, EXPERTS // 2) as it:
                            for u in range(2):
                                expert(u, it, first + it)

                    dve.wait_ge(cleared, 4)
                    selection(0, 0)
                    experts(0)
                    with dve.If(dve.value_load(most_i[0:1, 0:1], min_val=0, max_val=T) > CAP):
                        with dve.Fori(1, ROUNDS) as r_:
                            nc.vector.tensor_scalar(rank[:], rank[:], float(CAP), None, ALU.subtract)\
                                .then_inc(rank_moved, 1)
                            dve.wait_ge(rank_moved, r_)
                            dve.sem_inc(round_open, 1)
                            experts(EXPERTS // 2 * r_)
                    with dve.Else():
                        dve.wait_ge(blk_free, g0 + EXPERTS * EXPERT_BLOCKS)
                        dve.sem_inc(blk_free, (ROUNDS - 1) * EXPERTS * EXPERT_BLOCKS)
                        dve.wait_ge(alo_done, operand[l, "act"] + EXPERTS * EXPERT_OPERANDS)
                        dve.sem_inc(alo_done, (ROUNDS - 1) * EXPERTS * EXPERT_OPERANDS)
                    ln, lq_, lg_ = AT[l, "last"]
                    for d in range(KB):
                        dve.wait_ge(mm_done, lq_ + d + 1)
                        residual(l, lg_ + d, 5, d, x_new)
            n0, q0, g0 = AT["final"]
            reciprocal_root(4)
            dve.wait_ge(mm_done, SPREAD_AT[4] + 1)
            for kb in range(KB):
                nc.vector.scalar_tensor_tensor(halves(x[:, kb, :]), halves(x[:, kb, :]), gfin[:, kb:kb + 1],
                                               ps[:, g0 % 4, :, 0:HALF],
                                               op0=ALU.mult, op1=ALU.mult).then_inc(yblk, 1)


def kernel(**inputs):
    import numpy as np
    import concourse.bacc as bacc
    from concourse.bass_utils import run_bass_kernel_spmd

    def arr(a):
        return np.ascontiguousarray(a)

    def cols(w):
        *lead, k, n = w.shape
        w = w.reshape(*lead, k // P, P, n // P, P)
        r = len(lead)
        return arr(w.transpose(*range(r), r + 2, r + 1, r, r + 3)).reshape(*lead, n // P, P, k)

    I = {k: np.asarray(v) for k, v in inputs.items()}
    x = np.concatenate([I["x_prompt"][0], I["x_sample"][0]], 0)
    xT = arr(x.T.reshape(KB, P, T).transpose(1, 0, 2))
    cond = np.stack([I["c_ctx"], I["c"][0]], 1)
    condT = arr(cond.reshape(KB, P, 2).transpose(1, 0, 2))
    ada = arr(I["w_ada"].reshape(LAYERS, KB, P, 6, D).transpose(0, 3, 1, 2, 4)).reshape(LAYERS, ADA_CH, P, D)
    w_in = cols(I["w_in"])
    order = [4 + j for j in range(4)] + [j for j in range(4)] + [8 + j for j in range(4)] \
        + [16 + j for j in range(4)] + [20 + j for j in range(4)] + [12 + j for j in range(4)]
    w_in = arr(w_in[:, order])
    w_out = cols(I["w_out"])
    dg = I["w_gu_dense"][0].reshape(D, 2, 2, FF).transpose(2, 0, 1, 3).reshape(2, D, 2 * FF)
    gu = np.concatenate([dg, I["w_gu_moe"][0]], 0)
    gu = cols(gu)
    gu = arr(gu.reshape(-1, 2, FB, P, D).transpose(0, 2, 1, 3, 4)).reshape(-1, P, D)
    gu = np.concatenate([gu, gu[2 * 2 * FB:2 * 2 * FB + 2]], 0)
    moe_down = arr(I["w_down_moe"][0]).reshape(EXPERTS, FB, P, D)
    down = I["w_down_dense"][0].reshape(2, FF, D)
    down = down.reshape(-1, FB, P, KB, P).transpose(0, 3, 1, 2, 4).reshape(-1, FB, 8, P, P)
    down = arr(down.transpose(0, 1, 3, 2, 4)).reshape(-1, FB, P, CHUNK)

    def feat(a):
        a = a.reshape(*a.shape[:-1], -1, P)
        return arr(np.moveaxis(a, -1, 0))

    half = QK // 4
    freqs = np.float32(10000.0) ** (-np.arange(half, dtype=np.float32) / np.float32(half))
    pos = np.arange(LAT)
    row, col = (pos // 64).astype(np.float32), (pos % 64).astype(np.float32)
    ang = np.stack([row, col])[:, None, :] * freqs[None, :, None]
    c, s = np.cos(ang).astype(np.float32), np.sin(ang).astype(np.float32)
    one = np.concatenate([np.concatenate([c[a], c[a]]) for a in range(2)])
    sgn = np.concatenate([np.concatenate([-s[a], s[a]]) for a in range(2)])
    cos, sin = arr(np.concatenate([one, one])), arr(np.concatenate([sgn, sgn]))

    kc = I["cache_k"][0].reshape(LAYERS, PAST, HEADS, P).transpose(0, 3, 2, 1)
    vc = I["cache_v"][0].reshape(LAYERS, PAST // P, P, HEADS * VH).transpose(0, 2, 1, 3)
    arrays = {
        "xT": xT, "condT": condT, "ada_w": ada, "in_w": w_in, "out_w": w_out, "gu_w": gu, "down_w": down,
        "router_w": arr(I["w_router"][0].reshape(KB, P, EXPERTS).transpose(1, 0, 2)),
        "b_ada": feat(I["b_ada"]), "g_mix": feat(I["norm_mix_g"]), "g_ffn": feat(I["norm_ffn_g"]),
        "g_fin": feat(I["final_g"]), "lam_qk": arr(I["lambda_qk"]).reshape(LAYERS, 4 * QK),
        "subln": arr(I["subln_g"].T), "conv_w": feat(I["conv_w"]), "kcT": arr(kc), "vc": arr(vc),
        "cos": cos, "sin": sin, "ident": np.eye(P, dtype=np.float32),
        "iota": arr(np.broadcast_to(np.arange(CAP, dtype=np.float32), (P, CAP))),
        "below": np.triu(np.ones((P, P), np.float32), 1), "moe_down_w": moe_down,
    }
    nc = bacc.Bacc("TRN2", target_bir_lowering=False, num_devices=1, dynamic_dma_scratch_size=1024)
    args = [nc.dram_tensor(n, a.shape, mybir.dt.from_np(a.dtype), kind="ExternalInput").ap()
            for n, a in arrays.items()]
    outs = [("y", (P, KB, T)), ("newk", (LAYERS, P, HEADS, CTX)), ("newv", (LAYERS, P, HEADS, CTX))]
    args += [nc.dram_tensor(n, s, F32, kind="ExternalOutput").ap() for n, s in outs]
    hybrid_step(nc, *args)
    r = run_bass_kernel_spmd(nc, [arrays], core_ids=[0]).results[0]
    y = np.asarray(r["y"]).transpose(1, 0, 2).reshape(D, T).T
    newk = np.asarray(r["newk"]).transpose(0, 3, 2, 1).reshape(1, LAYERS, CTX, HEADS, 2, QK)
    newv = np.asarray(r["newv"]).transpose(0, 3, 2, 1).reshape(1, LAYERS, CTX, HEADS, VH)
    return arr(y[:CTX])[None], arr(y[CTX:])[None], arr(newk), arr(newv)
```
